# Optimizing a Trainium2 kernel written in Bass

```python
import math
import jax, jax.numpy as jnp
from jax import lax
import numpy as np

D_MODEL = 1024
BATCH = 1
SEQ = 256
DEPTH = 2

N_EVEN = (DEPTH + 1) // 2
N_ODD = DEPTH // 2

A_HEADS = 8
A_HEAD_DIM = D_MODEL // 16
A_WIDTH = A_HEADS * A_HEAD_DIM
DILATED_CONFIGS = ((128, 1), (512, 4), (2048, 16))
ROT_DIM = A_HEAD_DIM // 4
ROPE_THETA = 500000.0

POOL_WINDOWS = (2, 4, 8, 16)
POOL_GROUPS = 4
POOL_GROUP_DIM = D_MODEL // 8
POOL_WIDTH = POOL_GROUPS * POOL_GROUP_DIM

EVEN_IN = 3 * A_WIDTH + POOL_WIDTH
EVEN_MIX = A_WIDTH + POOL_WIDTH

DN_HEADS = 8
DN_HEAD_DIM = D_MODEL // 8
DN_WIDTH = DN_HEADS * DN_HEAD_DIM
CONV_WIDTH = 4
CHUNK = 64
ODD_IN = 4 * DN_WIDTH + 2 * DN_HEADS

FFN_DIM = D_MODEL * 7 // 2
N_EXPERTS = 8
TOP_K = 2
EPS = 1e-6

kernel_name = 'hybrid_dilated_pool_deltanet_moe_block'

def _rmsnorm(x, g):
    xf = x.astype(jnp.float32)
    y = xf * lax.rsqrt(jnp.mean(xf * xf, axis=-1, keepdims=True) + EPS) * g
    return y.astype(x.dtype)

def _partial_rope(t, positions):
    half = ROT_DIM // 2
    inv_freq = ROPE_THETA ** (-jnp.arange(0, ROT_DIM, 2, dtype=jnp.float32) / ROT_DIM)
    ang = positions.astype(jnp.float32)[..., None] * inv_freq
    cos, sin = jnp.cos(ang)[:, :, None, :], jnp.sin(ang)[:, :, None, :]
    x1 = t[..., :half].astype(jnp.float32)
    x2 = t[..., half:ROT_DIM].astype(jnp.float32)
    rot = jnp.concatenate([x1 * cos - x2 * sin, x2 * cos + x1 * sin], axis=-1)
    return jnp.concatenate([rot.astype(t.dtype), t[..., ROT_DIM:]], axis=-1)

def _dilated_branch(q, k, v, window, dilation):
    bsz, nh, seq, hd = q.shape
    blk = window // dilation
    span = blk * dilation
    length = -(-seq // span) * span
    n_sub = length // dilation
    nb = n_sub // blk

    def to_blocks(t):
        t = jnp.pad(t, ((0, 0), (0, 0), (0, length - seq), (0, 0)))
        t = t.reshape(bsz, nh, n_sub, dilation, hd).transpose(0, 1, 3, 2, 4)
        return t.reshape(bsz, nh, dilation, nb, blk, hd)

    def with_prev(t):
        prev = jnp.pad(t, ((0, 0), (0, 0), (0, 0), (1, 0), (0, 0), (0, 0)))[:, :, :, :-1]
        return jnp.concatenate([prev, t], axis=4)

    qb = to_blocks(q)
    kk = with_prev(to_blocks(k))
    vv = with_prev(to_blocks(v))
    s = jnp.einsum('bhrnqd,bhrnkd->bhrnqk', qb, kk).astype(jnp.float32) * hd ** -0.5
    qi = jnp.arange(blk)[:, None] + blk
    kj = jnp.arange(2 * blk)[None, :]
    rel = qi - kj
    band = (rel >= 0) & (rel <= blk)
    has_prev = (jnp.arange(nb) > 0)[:, None, None] | (kj >= blk)[None]
    mask = band[None] & has_prev
    s = jnp.where(mask, s, -jnp.inf)
    m = jnp.max(s, axis=-1, keepdims=True)
    p = jnp.exp(s - m)
    den = jnp.sum(p, axis=-1)
    o = jnp.einsum('bhrnqk,bhrnkd->bhrnqd', p, vv.astype(jnp.float32)) / den[..., None]
    lse = m[..., 0] + jnp.log(den)
    o = o.reshape(bsz, nh, dilation, n_sub, hd).transpose(0, 1, 3, 2, 4)
    o = o.reshape(bsz, nh, length, hd)[:, :, :seq]
    lse = lse.reshape(bsz, nh, dilation, n_sub).transpose(0, 1, 3, 2)
    lse = lse.reshape(bsz, nh, length)[:, :, :seq]
    return o, lse

def _dilated_mixture(q, k, v):
    outs, lses = [], []
    for window, dilation in DILATED_CONFIGS:
        o, lse = _dilated_branch(q, k, v, window, dilation)
        outs.append(o)
        lses.append(lse)
    w = jax.nn.softmax(jnp.stack(lses), axis=0)
    return jnp.sum(w[..., None] * jnp.stack(outs), axis=0)

def _multiscale_pool(u, pool_w, pool_scale):
    bsz, seq, _ = u.shape
    ug = u.reshape(bsz, seq, POOL_GROUPS, POOL_GROUP_DIM).astype(jnp.float32)
    cs = jnp.pad(jnp.cumsum(ug, axis=1), ((0, 0), (1, 0), (0, 0), (0, 0)))
    win = jnp.array(POOL_WINDOWS, dtype=jnp.int32)
    t = jnp.arange(seq, dtype=jnp.int32)[:, None]
    lo = jnp.maximum(t + 1 - win[None, :], 0)
    cnt = jnp.minimum(t + 1, win[None, :]).astype(jnp.float32)
    lower = cs[:, lo, jnp.arange(POOL_GROUPS)[None, :], :]
    pooled = (cs[:, 1:] - lower) / cnt[None, :, :, None] - ug
    mixed = jnp.einsum('bsgc,gcd->bsgd', pooled, pool_w)
    mixed = mixed * pool_scale.reshape(POOL_GROUPS, POOL_GROUP_DIM)
    return mixed.reshape(bsz, seq, POOL_WIDTH).astype(u.dtype)

def _even_mixer(h, positions, w_in, pool_w, pool_scale, w_out):
    bsz, seq, _ = h.shape
    proj = h @ w_in
    q, k, v, u = jnp.split(proj, [A_WIDTH, 2 * A_WIDTH, 3 * A_WIDTH], axis=-1)
    q = _partial_rope(q.reshape(bsz, seq, A_HEADS, A_HEAD_DIM), positions)
    k = _partial_rope(k.reshape(bsz, seq, A_HEADS, A_HEAD_DIM), positions)
    v = v.reshape(bsz, seq, A_HEADS, A_HEAD_DIM)
    o_a = _dilated_mixture(q.transpose(0, 2, 1, 3), k.transpose(0, 2, 1, 3), v.transpose(0, 2, 1, 3))
    o_a = o_a.transpose(0, 2, 1, 3).reshape(bsz, seq, A_WIDTH).astype(h.dtype)
    o_b = _multiscale_pool(u, pool_w, pool_scale)
    return jnp.concatenate([o_a, o_b], axis=-1) @ w_out

def _causal_depthwise_conv(x, w):
    ch = x.shape[-1]
    return lax.conv_general_dilated(
        x, w[:, None, :], window_strides=(1,), padding=[(w.shape[0] - 1, 0)],
        dimension_numbers=('NWC', 'WIO', 'NWC'), feature_group_count=ch)

def _chunk_gated_delta(q, k, v, g, beta):
    bsz, nh, seq, dk = q.shape
    dv = v.shape[-1]
    n = seq // CHUNK
    q = q.reshape(bsz, nh, n, CHUNK, dk) * dk ** -0.5
    k = k.reshape(bsz, nh, n, CHUNK, dk)
    v = v.reshape(bsz, nh, n, CHUNK, dv)
    g = g.reshape(bsz, nh, n, CHUNK)
    beta = beta.reshape(bsz, nh, n, CHUNK)
    gc = jnp.cumsum(g, axis=-1)
    idx = jnp.arange(CHUNK)
    causal = idx[:, None] >= idx[None, :]
    strict = idx[:, None] > idx[None, :]
    decay = jnp.exp(jnp.where(causal, gc[..., :, None] - gc[..., None, :], -jnp.inf))
    kb = k * beta[..., None]
    lmat = jnp.where(strict, jnp.einsum('bhnid,bhnjd->bhnij', kb, k) * decay, 0.0)
    eye = jnp.eye(CHUNK, dtype=jnp.float32)
    rhs = jnp.concatenate([v * beta[..., None], kb * jnp.exp(gc)[..., None]], axis=-1)
    sol = lax.linalg.triangular_solve(lmat + eye, rhs, left_side=True, lower=True,
                                      unit_diagonal=True)
    u, w = sol[..., :dv], sol[..., dv:]
    attn = jnp.einsum('bhnid,bhnjd->bhnij', q, k) * decay
    q_g = q * jnp.exp(gc)[..., None]
    k_g = k * jnp.exp(gc[..., -1:] - gc)[..., None]
    chunk_decay = jnp.exp(gc[..., -1])

    def step(state, xs):
        q_c, k_c, u_c, w_c, a_c, d_c = xs
        v_new = u_c - jnp.einsum('bhck,bhkv->bhcv', w_c, state)
        o_c = jnp.einsum('bhck,bhkv->bhcv', q_c, state) + jnp.einsum('bhij,bhjv->bhiv', a_c, v_new)
        state = state * d_c[..., None, None] + jnp.einsum('bhck,bhcv->bhkv', k_c, v_new)
        return state, o_c

    front = lambda t: jnp.moveaxis(t, 2, 0)
    state0 = jnp.zeros((bsz, nh, dk, dv), jnp.float32)
    _, o = lax.scan(step, state0, (front(q_g), front(k_g), front(u), front(w), front(attn),
                                   front(chunk_decay)))
    return jnp.moveaxis(o, 0, 2).reshape(bsz, nh, seq, dv)

def _odd_mixer(h, w_in, conv_w, a_log, dt_bias, norm_g, w_out):
    bsz, seq, _ = h.shape
    proj = h @ w_in
    qkv, gate, beta_logit, a_logit = jnp.split(
        proj, [3 * DN_WIDTH, 4 * DN_WIDTH, 4 * DN_WIDTH + DN_HEADS], axis=-1)
    qkv = jax.nn.silu(_causal_depthwise_conv(qkv, conv_w))
    q, k, v = jnp.split(qkv, 3, axis=-1)
    heads = lambda t: t.reshape(bsz, seq, DN_HEADS, DN_HEAD_DIM).transpose(0, 2, 1, 3).astype(jnp.float32)
    q, k, v = heads(q), heads(k), heads(v)
    q = q * lax.rsqrt(jnp.sum(q * q, axis=-1, keepdims=True) + EPS)
    k = k * lax.rsqrt(jnp.sum(k * k, axis=-1, keepdims=True) + EPS)
    beta = jax.nn.sigmoid(beta_logit.astype(jnp.float32)).transpose(0, 2, 1)
    g = -(jnp.exp(a_log.astype(jnp.float32))
          * jax.nn.softplus(a_logit.astype(jnp.float32) + dt_bias)).transpose(0, 2, 1)
    o = _chunk_gated_delta(q, k, v, g, beta).transpose(0, 2, 1, 3)
    o = o * lax.rsqrt(jnp.mean(o * o, axis=-1, keepdims=True) + EPS) * norm_g
    o = o * jax.nn.silu(gate.astype(jnp.float32).reshape(bsz, seq, DN_HEADS, DN_HEAD_DIM))
    return o.reshape(bsz, seq, DN_WIDTH).astype(h.dtype) @ w_out

def _swiglu(h, w_gate, w_up, w_down):
    return (jax.nn.silu(h @ w_gate) * (h @ w_up)) @ w_down

def _moe(h, router_w, w_gate, w_up, w_down):
    bsz, seq, d = h.shape
    t = h.reshape(bsz * seq, d)
    logits = (t @ router_w).astype(jnp.float32)
    top_val, top_idx = lax.top_k(logits, TOP_K)
    top_w = jax.nn.softmax(top_val, axis=-1)
    combine = jnp.sum(jax.nn.one_hot(top_idx, N_EXPERTS, dtype=jnp.float32) * top_w[..., None], axis=1)
    out = jnp.zeros((bsz * seq, d), jnp.float32)
    for e in range(N_EXPERTS):
        out = out + combine[:, e:e + 1] * _swiglu(t, w_gate[e], w_up[e], w_down[e]).astype(jnp.float32)
    return out.reshape(bsz, seq, d).astype(h.dtype)

def setup_inputs(seed: int = 0) -> dict:
    key = jax.random.key(seed)
    ks = iter(jax.random.split(key, 40))
    nrm = lambda shape, scale: jax.random.normal(next(ks), shape, jnp.float32) * scale
    gain = lambda shape: 1.0 + 0.1 * jax.random.normal(next(ks), shape, jnp.float32)
    x = nrm((BATCH, SEQ, D_MODEL), 1.0)
    c = nrm((BATCH, D_MODEL), 1.0)
    offs = jax.random.randint(next(ks), (BATCH, 1), 0, 4096, dtype=jnp.int32)
    positions = offs + jnp.arange(SEQ, dtype=jnp.int32)[None, :]
    ada_w = nrm((DEPTH, D_MODEL, 6 * D_MODEL), 0.5 * D_MODEL ** -0.5)
    ada_b = nrm((DEPTH, 6 * D_MODEL), 0.02)
    mix_pre_g = gain((DEPTH, D_MODEL))
    mix_post_g = gain((DEPTH, D_MODEL))
    ffn_pre_g = gain((DEPTH, D_MODEL))
    ffn_post_g = gain((DEPTH, D_MODEL))
    even_w_in = nrm((N_EVEN, D_MODEL, EVEN_IN), D_MODEL ** -0.5)
    even_pool_w = nrm((N_EVEN, POOL_GROUPS, POOL_GROUP_DIM, POOL_GROUP_DIM), POOL_GROUP_DIM ** -0.5)
    even_pool_scale = 0.1 + 0.02 * jax.random.normal(next(ks), (N_EVEN, POOL_WIDTH), jnp.float32)
    even_w_out = nrm((N_EVEN, EVEN_MIX, D_MODEL), EVEN_MIX ** -0.5)
    even_ffn_w_gate = nrm((N_EVEN, D_MODEL, FFN_DIM), D_MODEL ** -0.5)
    even_ffn_w_up = nrm((N_EVEN, D_MODEL, FFN_DIM), D_MODEL ** -0.5)
    even_ffn_w_down = nrm((N_EVEN, FFN_DIM, D_MODEL), FFN_DIM ** -0.5)
    odd_w_in = nrm((N_ODD, D_MODEL, ODD_IN), D_MODEL ** -0.5)
    odd_conv_w = nrm((N_ODD, CONV_WIDTH, 3 * DN_WIDTH), CONV_WIDTH ** -0.5)
    odd_a_log = jnp.log(jax.random.uniform(next(ks), (N_ODD, DN_HEADS), jnp.float32, 1.0, 16.0))
    dt = jnp.exp(jax.random.uniform(next(ks), (N_ODD, DN_HEADS), jnp.float32,
                                    math.log(1e-3), math.log(1e-1)))
    odd_dt_bias = dt + jnp.log(-jnp.expm1(-dt))
    odd_norm_g = gain((N_ODD, DN_HEAD_DIM))
    odd_w_out = nrm((N_ODD, DN_WIDTH, D_MODEL), DN_WIDTH ** -0.5)
    odd_router_w = nrm((N_ODD, D_MODEL, N_EXPERTS), D_MODEL ** -0.5)
    odd_moe_w_gate = nrm((N_ODD, N_EXPERTS, D_MODEL, FFN_DIM), D_MODEL ** -0.5)
    odd_moe_w_up = nrm((N_ODD, N_EXPERTS, D_MODEL, FFN_DIM), D_MODEL ** -0.5)
    odd_moe_w_down = nrm((N_ODD, N_EXPERTS, FFN_DIM, D_MODEL), FFN_DIM ** -0.5)
    return {'x': x, 'c': c, 'positions': positions, 'ada_w': ada_w, 'ada_b': ada_b,
            'mix_pre_g': mix_pre_g, 'mix_post_g': mix_post_g,
            'ffn_pre_g': ffn_pre_g, 'ffn_post_g': ffn_post_g,
            'even_w_in': even_w_in, 'even_pool_w': even_pool_w,
            'even_pool_scale': even_pool_scale, 'even_w_out': even_w_out,
            'even_ffn_w_gate': even_ffn_w_gate, 'even_ffn_w_up': even_ffn_w_up,
            'even_ffn_w_down': even_ffn_w_down,
            'odd_w_in': odd_w_in, 'odd_conv_w': odd_conv_w, 'odd_a_log': odd_a_log,
            'odd_dt_bias': odd_dt_bias, 'odd_norm_g': odd_norm_g, 'odd_w_out': odd_w_out,
            'odd_router_w': odd_router_w, 'odd_moe_w_gate': odd_moe_w_gate,
            'odd_moe_w_up': odd_moe_w_up, 'odd_moe_w_down': odd_moe_w_down}

def reference(x, c, positions, ada_w, ada_b, mix_pre_g, mix_post_g, ffn_pre_g, ffn_post_g,
              even_w_in, even_pool_w, even_pool_scale, even_w_out,
              even_ffn_w_gate, even_ffn_w_up, even_ffn_w_down,
              odd_w_in, odd_conv_w, odd_a_log, odd_dt_bias, odd_norm_g, odd_w_out,
              odd_router_w, odd_moe_w_gate, odd_moe_w_up, odd_moe_w_down):
    c_act = jax.nn.silu(c)
    for layer in range(DEPTH):
        j = layer // 2
        mod = c_act @ ada_w[layer] + ada_b[layer]
        sh1, sc1, gt1, sh2, sc2, gt2 = jnp.split(mod, 6, axis=-1)
        h = _rmsnorm(x, mix_pre_g[layer]) * (1.0 + sc1[:, None, :]) + sh1[:, None, :]
        if layer % 2 == 0:
            y = _even_mixer(h, positions, even_w_in[j], even_pool_w[j], even_pool_scale[j], even_w_out[j])
        else:
            y = _odd_mixer(h, odd_w_in[j], odd_conv_w[j], odd_a_log[j], odd_dt_bias[j],
                           odd_norm_g[j], odd_w_out[j])
        x = x + gt1[:, None, :] * _rmsnorm(y, mix_post_g[layer])
        h = _rmsnorm(x, ffn_pre_g[layer]) * (1.0 + sc2[:, None, :]) + sh2[:, None, :]
        if layer % 2 == 0:
            y = _swiglu(h, even_ffn_w_gate[j], even_ffn_w_up[j], even_ffn_w_down[j])
        else:
            y = _moe(h, odd_router_w[j], odd_moe_w_gate[j], odd_moe_w_up[j], odd_moe_w_down[j])
        x = x + gt2[:, None, :] * _rmsnorm(y, ffn_post_g[layer])
    return x


_drawn_inputs = setup_inputs


def setup_inputs(seed=0):
    import zlib

    import numpy as np

    out = dict(_drawn_inputs(seed))
    spreads = {}
    factors = {}
    for name, (base, spread) in spreads.items():
        noise = np.random.default_rng([zlib.crc32(name.encode()), seed]).standard_normal(out[name].shape)
        drawn = base * np.exp(spread * noise) if base else spread * noise
        out[name] = __import__('jax').numpy.asarray(drawn.astype(out[name].dtype))
    for name, factor in factors.items():
        out[name] = (out[name] * factor).astype(out[name].dtype)
    return out
```

```python
from contextlib import ExitStack

import concourse.bass as bass
from concourse import mybir

F32 = mybir.dt.float32
I32 = mybir.dt.int32
U32 = mybir.dt.uint32
ALU = mybir.AluOpType
ACT = mybir.ActivationFunctionType
AX = mybir.AxisListType

P = 128
TOK = 256
NT = TOK // P
D = 1024
KD = D // P
N = 512
FFN = 3584
NB = FFN // N
HEADS = 8
HD = 64
ROT = 8
POOLG = 4
DH = 128
NE = 8
CONVW = 4
EPS = 1e-6
RING = 7
TILE = 2048
NEG = -1e30
MAGIC = 12582912.0
TWO_PI_HI = 6.28125
TWO_PI_LO = 0.0019353071795864769
ACC_RING = 4
ROWSB = 8 + 96 + 4
EXTRA_MAX = 3

CONST = {}
_at = 0
for _name, _n in [("ident", P), ("ones", P), ("mask", 3 * P), ("upto", P), ("after", P), ("before", P),
                  ("neg", P), ("level", 7 * P), ("iota", 2 * P), ("iota8", 8), ("freq", ROT), ("phase", 2 * NT * ROT)]:
    CONST[_name] = (_at, _n)
    _at += _n
CONST_N = _at


def constants(np):
    out = np.zeros((P, CONST_N), np.float32)

    def put(name, value):
        a, n = CONST[name]
        out[:, a:a + n] = value

    row, col = np.arange(P)[:, None], np.arange(P)[None, :]
    put("ident", row == col)
    put("ones", 1.0)
    i, j = np.arange(TOK)[:, None], np.arange(TOK)[None, :]
    count = ((i >= j) & (i - j <= 128)).astype(np.float64)
    for dilation in (4, 16):
        count += (i >= j) & ((i - j) % dilation == 0)
    log_count = np.where(count > 0, np.log(np.maximum(count, 1)), NEG)
    put("mask", np.concatenate([log_count[:P, :P], log_count[P:, :]], axis=1))
    put("upto", row <= col)
    put("after", row > col)
    put("before", row < col)
    put("neg", np.where(row <= col, 0.0, NEG))
    levels = [(col // (2 * s) == row // (2 * s)) & (col % (2 * s) >= s) & (row % (2 * s) < s)
              for s in (1, 2, 4, 8, 16, 32, 64)]
    put("level", np.concatenate(levels, axis=1))
    put("iota", np.arange(2 * P)[None, :])
    put("iota8", np.arange(8)[None, :])
    put("freq", (np.float32(500000.0) ** (-np.arange(0, 16, 2, dtype=np.float32) / np.float32(16)))[None, :])
    put("phase", np.repeat([0.0, 0.25], NT * ROT)[None, :])
    pool = np.zeros((POOLG, P, 3 * P), np.float32)
    for g, window in enumerate((2, 4, 8, 16)):
        t, s = np.arange(TOK)[None, :], np.arange(TOK)[:, None]
        w = ((t - s >= 0) & (t - s < window)) / np.minimum(t + 1, window) - (t == s)
        pool[g] = np.concatenate([w[:P, :], w[P:, P:]], axis=1)
    return out, pool


def ffn_tiles(kind, between):
    out, between = [], list(between)
    for b in range(NB):
        out += [(kind + "g", b, h) for h in range(2)]
        out += between[:2]
        out += [(kind + "u", b, h) for h in range(2)]
        out += [(kind + "d", b - 1, h) for h in range(2)] if b else []
        out += between[2:4]
        between = between[4:]
    return out + [(kind + "d", NB - 1, h) for h in range(2)]


def halves(kind, ns):
    return [(kind, n, h) for n in ns for h in range(2)]


ADA = [(0, n) for n in range(12)] + [(1, n) for n in range(12)]
ADA_AT = {a: j for j, a in enumerate(ADA)}
ada_halves = [[("ada", j, h) for h in range(2)] for j in range(24)]
STREAM = sum(ada_halves[0:4], []) + halves("ein", [0]) + ada_halves[4] + halves("ein", [1]) + ada_halves[5] + ada_halves[6]
STREAM += halves("ein", [2]) + ada_halves[7] + ada_halves[8] + halves("ein", [3]) + ada_halves[9] + halves("eout", [0, 1])
STREAM += ffn_tiles("f", sum(ada_halves[10:], []))
STREAM += halves("oin", [0, 2, 4, 1, 3, 5, 6, 7]) + halves("oout", [0, 1])
AT = {t: n for n, t in enumerate(STREAM)}
NSTREAM = len(STREAM)
MOE = ffn_tiles("m", [])
MOE_AT = {t: n for n, t in enumerate(MOE)}
NMOE = len(MOE)
assert NMOE % RING == 0 and len(AT) == NSTREAM

ODD_GROUPS = 2


def static_banks():
    out = [(("cols", 0), 6), (("cols", 1), 7)]
    out += [(("ada", j), 7) for j in range(4)]
    out += [(("ht", 0, j), 4 + j % 4) for j in range(4)]
    for n in range(4):
        out += [(("ein", n, t), 2 * (n % 2) + t) for t in range(NT)]
        out += [(("ada", j), 7) for j in {1: [4], 2: [5, 6], 3: [7, 8, 9]}.get(n, [])]
    for g in range(POOLG):
        out += [(("pool", g), 6), (("mix", g), 7)]
    out += [(("qkt", j), 2 + j) for j in range(4)]
    for h in range(HEADS + 2):
        if h < HEADS:
            out += [(("score", h), h % 2)]
        if 1 <= h <= HEADS:
            out += [(("pt", h - 1), 2 + (h - 1) % 2)]
        if h >= 2 and h % 2 == 1:
            out += [(("pv", (h - 2) // 2), 4 + (h - 2) // 2 % 2)]
    out += [(("y", 0, t, n), 2 * t + n) for n in range(2) for t in range(NT)]
    out += [(("ht", 1, j), 4 + j % 4) for j in range(4)]
    for b in range(NB + 1):
        if b < NB:
            out += [(("fg", b, t), 4 + t) for t in range(NT)]
        if b:
            out += [(("ft", b - 1, t), 6 + t) for t in range(NT)]
            out += [(("ada", 10 + 2 * (b - 1) + i), 7) for i in range(2)]
        if b < NB:
            out += [(("fu", b, t), 4 + t) for t in range(NT)]
        if b == 1:
            out += [(("y", 1, t, n), 2 * t + n) for t in range(NT) for n in range(2)]
    out += [(("ht", 2, j), 4 + j % 4) for j in range(4)]
    out += [(("ba",), 4), (("gc",), 5)]
    for g in range(ODD_GROUPS):
        out += [(("oin", g, 0, t), t) for t in range(NT)] + [(("oin", g, 1, t), 4 + t) for t in range(NT)]
        out += [(("rt", g, 0, j), 2 + j) for j in range(2)] + [(("oin", g, 2, t), t) for t in range(NT)]
        out += [(("rt", g, 1, j), 2 + j) for j in range(2)] + [(("rt", g, 2, j), 4 + j) for j in range(2)]
        out += [(("ss", g, 0), 6), (("ss", g, 1), 7)]
        out += [(("decay", g, c), 4 + c) for c in range(2)] + [(("brow", g, c), 6 + c) for c in range(2)]
        out += [(("kk", g, c), 0 + c) for c in range(2)] + [(("kq", g, c), 2 + c) for c in range(2)]
        out += [(("vn", g, c), 4 + c) for c in range(2)] + [(("kn", g), 6)]
        out += [(("x0", g, c), 0 + c) for c in range(2)]
        for s in range(1, 7):
            out += [(("Y", g, s, c), 2 + c) for c in range(2)]
            for c in range(2):
                out += [(("dX", g, s, c), 4 + c)] if s < 6 else []
                out += [(("dU", g, s, c), 6 + c)]
        out += [(("u0", g), 0), (("S1", g), 1), (("kS", g), 2), (("v1", g), 3), (("o0", g), 4), (("qS", g), 5), (("o1", g), 6)]
    out += [(("gate", n, t), 2 * n + t) for n in range(2) for t in range(NT)]
    out += [(("ot", j), 4 + j) for j in range(4)]
    out += [(("y", 2, t, n), 2 * t + n) for n in range(2) for t in range(NT)]
    out += [(("ht", 3, j), 4 + j % 4) for j in range(4)]
    out += [(("route",), 4), (("slot",), 5)]
    return out


def moe_banks():
    out = [(("mh", 0), 2), (("mh", 1), 3), (("mp",), 6)]
    for b in range(NB + 1):
        if b < NB:
            out += [(("mg", b, 0), 2 + 2 * (b % 2))]
        if b:
            out += [(("mt", b - 1, 0), 6 + b % 2)]
        if b < NB:
            out += [(("mu", b, 0), 3 + 2 * (b % 2))]
        if b == 1:
            out += [(("my", n), n) for n in range(2)]
    return out + [(("mo", t, n), 4 + 2 * t + n) for t in range(NT) for n in range(2)]


def ordinals(order):
    used, place = [0] * 8, {}
    for name, bank in order:
        assert name not in place
        place[name] = (bank, used[bank])
        used[bank] += 1
    return place, used


BANK, BANK_USES = ordinals(static_banks())
MOE_BANK, MOE_BANK_USES = ordinals(moe_banks())

RELEASE, MOE_RELEASE = {}, {}


def plan_release():
    n = 0
    for at, (kind, b, h) in enumerate(STREAM):
        if kind == "ada":
            RELEASE[at] = ("ada", 8 * b + 4 * h + 4)
        elif h == 0 or (kind == "fd" and b < NB - 1):
            n += 1
            RELEASE[at] = ("tile", n)
        else:
            g, r = b % 2, b // 2
            RELEASE[at] = ("bank", {"ein": ("ein", b, 1), "eout": ("y", 0, 1, b), "fg": ("fg", b, 1), "fu": ("fu", b, 1),
                                    "fd": ("y", 1, 1, 1), "oin": ("oin", g, r, 1) if b < 6 else ("gate", b - 6, 1),
                                    "oout": ("y", 2, 1, b)}[kind])
    m = 0
    for at, (kind, b, h) in enumerate(MOE):
        if h == 0 or (kind == "md" and b < NB - 1):
            m += 1
            MOE_RELEASE[at] = ("tile", m)
        else:
            MOE_RELEASE[at] = ("bank", ("my", 1) if kind == "md" else (kind, b, 0))
    return n, m


TILES_USED, MOE_TILES_USED = plan_release()
IN_NAMES = ["x", "c", "positions", "ada_w", "ada_b", "mix_pre_g", "mix_post_g", "ffn_pre_g", "ffn_post_g",
            "even_w_in", "even_pool_w", "even_pool_scale", "even_w_out", "even_ffn_w_gate", "even_ffn_w_up",
            "even_ffn_w_down", "odd_w_in", "odd_conv_w", "odd_a_log", "odd_dt_bias", "odd_norm_g", "odd_w_out",
            "odd_router_w", "odd_moe_w_gate", "odd_moe_w_up", "odd_moe_w_down"]


def build_trunk(nc, I, const_dram, pool_dram, out_dram):
    ctx = ExitStack()
    with ctx:
        def sb(name, shape, dt=F32):
            return ctx.enter_context(nc.sbuf_tensor(name, shape, dt))

        def sem(name):
            return ctx.enter_context(nc.semaphore(name))

        ps = [ctx.enter_context(nc.psum_tensor(f"bank{b}", [P, N], F32)) for b in range(8)]
        ring = sb("ring", [P, RING, TILE])
        x = sb("xres", [P, NT, D])
        xn = sb("xn", [P, NT, D])
        hT = sb("hT", [P, KD, TOK])
        A = sb("A", [P, 4, D])
        grow = sb("grow", [P, 4, D])
        consts = sb("consts", [P, CONST_N])
        acc = sb("acc", [P, ACC_RING, N])
        rowsA = sb("rowsA", [P, P])
        rowsB = sb("rowsB", [P, P])
        colA = sb("colA", [P, P])
        colB = sb("colB", [P, P])
        csil = sb("csil", [P, KD])
        shift = sb("shift", [P, 4, KD])
        gain = sb("gain", [P, 4, KD])
        mod_tmp = sb("mod_tmp", [P, 4])
        ss = sb("ss", [P, 4, NT])
        rstd = sb("rstd", [P, 4, NT])
        ssy = sb("ssy", [P, 4, NT, 2])
        rstdy = sb("rstdy", [P, 4, NT])
        half_neg = sb("half_neg", [P, 16])
        posi = sb("posi", [P, NT], I32)
        posf = sb("posf", [P, NT])
        ba_w = sb("ba_w", [P, KD, 16])
        router = sb("router", [P, KD, NE])
        poolw = sb("poolw", [P, POOLG, P])
        alog = sb("alog", [P, HEADS])
        dtb = sb("dtb", [P, HEADS])
        normg = sb("normg", [P, DH])
        scratch = sb("scratch", [P, 14336])

        def view(at, *shape):
            n = 1
            for s in shape:
                n *= s
            assert at + n <= 14336
            ap = scratch[:, at:at + n]
            if len(shape) == 2:
                return ap.rearrange("p (a b) -> p a b", a=shape[0])
            if len(shape) == 3:
                return ap.rearrange("p (a b c) -> p a b c", a=shape[0], b=shape[1])
            return ap

        def const(name, a=0, n=None):
            at, size = CONST[name]
            return consts[:, at + a:at + a + (size if n is None else n)]

        ident, ones = const("ident"), const("ones")

        proj = view(0, NT, 4 * N)
        qkT = view(4096, 8, TOK)
        oT = view(6144, KD, TOK)
        sL = view(8192, 2, 384)
        prob = view(8960, 2, 384)
        pT = view(9728, 4, 384)
        pooled = view(11264, 2, TOK)
        poolc = view(11776, POOLG, 384)
        rope_in = view(13312, 3, 32)
        rope_n = view(13408, 32)
        rope_r = view(13440, 32)
        cs = view(13472, 32)
        rope_t = view(13504, 4, 16, ROT)
        nmax = view(14016, HEADS, 2)
        den = view(14032, HEADS, 2)
        rden = view(14048, HEADS, 2)
        sil = view(0, NT, N)
        act_n = view(1024, NT, N)
        actT = view(2048, NT, 4, P)
        sgate = view(0, NT, D)
        qkvT = view(2048, 3, 4, TOK)
        nat = view(5120, NT, N)
        raw = scratch[:, 6144:6144 + 4 * 260].rearrange("p (h t) -> p h t", h=4)
        conv = view(7184, 4, TOK)
        sq = view(8208, 4, TOK)
        X = view(5120, 2, 4, P)
        U = view(6144, 2, 4, P)
        Y = view(7168, 2, 4, P)
        CT = view(8192, 2, 4, P)
        LT = view(9232, 2, 4, P)
        attnT = view(10256, 2, 4, P)
        ET = view(11280, 2, 4, P)
        vb = view(12304, 2, 4, P)
        kg0 = view(13328, 4, P)
        u0, S1 = X[:, 0], X[:, 1]
        r1, v1 = Y[:, 0], Y[:, 1]
        qs = CT[:, 0]
        small = sb("small", [P, 24, 16])
        ba, beta, gdec = small[:, 0:2, :], small[:, 2, :], small[:, 3, :]
        bt = [small[:, 4 + i, :] for i in range(4)]
        eg = small[:, 8:10, :].rearrange("p a b -> p (a b)")[:, 0:24]
        ssqk = small[:, 10, :].rearrange("p (r b) -> p r b", r=2)
        rqk = small[:, 11, :].rearrange("p (r b) -> p r b", r=2)
        bk = small[:, 12, 0:8]
        kge = small[:, 12, 8:12]
        nbe = small[:, 12, 12:16]
        rsq = small[:, 13, :].rearrange("p (c h) -> p c h", c=2)
        sso = small[:, 14, :].rearrange("p (c h) -> p c h", c=2)
        fo = small[:, 15, :].rearrange("p (c h) -> p c h", c=2)
        f1 = small[:, 16, :].rearrange("p (c h) -> p c h", c=2)
        logit = small[:, 17, :].rearrange("p (t e) -> p t e", t=NT)
        best = small[:, 18, :].rearrange("p (t e) -> p t e", t=NT)
        besti = sb("besti", [P, NT, 8], U32)
        bestf = small[:, 19, :].rearrange("p (t e) -> p t e", t=NT)
        pexp = small[:, 20, :].rearrange("p (k t) -> p k t", k=8)
        sel = small[:, 21, :].rearrange("p (t e) -> p t e", t=NT)
        comb = small[:, 22, :].rearrange("p (t e) -> p t e", t=NT)
        rt = small[:, 23, :].rearrange("p (t e) -> p t e", t=NT)
        pos = sb("pos", [P, 3, NE])
        table = sb("table", [P, 4, NE])
        match = sb("match", [P, EXTRA_MAX, NE])
        tabf = sb("tabf", [P, 4])
        tabi = sb("tabi", [P, 4], I32)
        heT = view(0, KD, P)
        place = view(1024, NT, P)
        placew = view(1280, NT, P)
        placeT = view(1536, NT, P)
        msil = view(1792, 1, N)
        mact = view(2304, 1, N)
        mactT = view(2816, 1, 4, P)
        ye = view(3328, D)
        yout = view(4352, NT, D)

        slot_loaded = [sem(f"slot_loaded{s}") for s in range(RING)]
        tiles_used = sem("tiles_used")
        ada_step = sem("ada_step")
        filled = [sem(f"bank_filled{b}") for b in range(8)]
        emptied = [sem(f"bank_emptied{b}") for b in range(8)]
        const_in = sem("const_in")
        rows_in = sem("rows_in")
        x_in = sem("x_in")
        pos_in = sem("pos_in")
        grow_in = sem("grow_in")
        abias_in = sem("abias_in")
        poolw_in = sem("poolw_in")
        odd_in = sem("odd_in")
        out_done = sem("out_done")
        csil_ready = sem("csil_ready")
        ss_ready = sem("ss_ready")
        rstd_ready = sem("rstd_ready")
        xn_ready = sem("xn_ready")
        ssy_ready = sem("ssy_ready")
        rstdy_ready = sem("rstdy_ready")
        x_ready = sem("x_ready")
        trig_arg = sem("trig_arg")
        trig_ready = sem("trig_ready")
        roped = sem("roped")
        maxed = sem("maxed")
        exped = sem("exped")
        normed = sem("normed")
        ba_dve = sem("ba_dve")
        ba_act = sem("ba_act")
        conv_ready = sem("conv_ready")
        silu_ready = sem("silu_ready")
        sq_ready = sem("sq_ready")
        rqk_ready = sem("rqk_ready")
        rhs_ready = sem("rhs_ready")
        et_act = sem("et_act")
        ct_ready = sem("ct_ready")
        u_ready = sem("u_ready")
        fo_arg = sem("fo_arg")
        fo_ready = sem("fo_ready")
        r_ready = sem("r_ready")
        o_ready = sem("o_ready")
        route_arg = sem("route_arg")
        route_exp = sem("route_exp")
        sel_ready = sem("sel_ready")
        table_ready = sem("table_ready")
        dve_step = sem("dve_step")
        act_step = sem("act_step")
        pool_step = sem("pool_step")
        place_ready = sem("place_ready")
        mo_ready = sem("mo_ready")

        def use(name, it):
            if it is None:
                return BANK[name]
            bank, before = MOE_BANK[name]
            return bank, it * MOE_BANK_USES[bank] + (BANK_USES[bank] + before)

        def bank(name, it=None):
            return ps[use(name, it)[0]]

        def wait_free(pe, name, it=None):
            b, before = use(name, it)
            if it is not None or before:
                pe.wait_ge(emptied[b], before)

        def signal_filled(ins, name, it=None):
            ins.then_inc(filled[use(name, it)[0]], 1)

        def wait_filled(eng, name, it=None):
            b, before = use(name, it)
            eng.wait_ge(filled[b], before + 1)

        def signal_emptied(ins, name, it=None):
            ins.then_inc(emptied[use(name, it)[0]], 1)

        def wait_emptied(eng, name, it=None):
            b, before = use(name, it)
            eng.wait_ge(emptied[b], before + 1)

        def slot(n):
            return n % RING

        def wait_tile(eng, n, it=None):
            if it is None:
                eng.wait_ge(slot_loaded[n % RING], 16 * (n // RING + 1))
            else:
                m = NSTREAM + n
                eng.wait_ge(slot_loaded[m % RING], it * (16 * NMOE // RING) + 16 * (m // RING + 1))

        def wide(s):
            return ring[:, s, :].rearrange("p (k n) -> p k n", n=N)

        def long(s):
            return ring[:, s, :].rearrange("p (k n) -> p k n", n=D)

        def row3(ap, n):
            return ap.unsqueeze(1).to_broadcast([P, n, ap.shape[1]])

        def col3(ap, n):
            return ap.unsqueeze(2).to_broadcast([P, ap.shape[1], n])

        block = ctx.enter_context(nc.Block())

        @block.sync
        def _(sp):
            def wide_source(w, n, h):
                return w.rearrange("(k p) n -> p k n", p=P)[:, 4 * h:4 * h + 4, n * N:(n + 1) * N]

            def long_source(w, n):
                return w.rearrange("(k p) n -> p k n", p=P)[:, 2 * n:2 * n + 2, :]

            def source(kind, n, h):
                if kind == "ada":
                    layer, block_n = ADA[n]
                    return wide_source(I["ada_w"][layer], block_n, h)
                if kind == "fd":
                    return long_source(I["even_ffn_w_down"][0], 2 * n + h)
                w = {"ein": "even_w_in", "eout": "even_w_out", "fg": "even_ffn_w_gate", "fu": "even_ffn_w_up",
                     "oin": "odd_w_in", "oout": "odd_w_out"}[kind]
                return wide_source(I[w][0], n, h)

            def target(n, kind):
                return long(slot(n)) if kind[1:] == "d" else wide(slot(n))

            def wait_slot(how):
                if how[0] == "ada":
                    sp.wait_ge(ada_step, how[1])
                elif how[0] == "tile":
                    sp.wait_ge(tiles_used, how[1])
                else:
                    wait_filled(sp, how[1])

            def wait_moe_slot(how, it):
                if how[0] == "tile":
                    sp.wait_ge(tiles_used, it * MOE_TILES_USED + (TILES_USED + how[1]))
                else:
                    wait_filled(sp, how[1], it)

            for n, (kind, b, h) in enumerate(STREAM):
                if n >= RING:
                    wait_slot(RELEASE[n - RING])
                sp.dma_start(target(n, kind), source(kind, b, h)).then_inc(slot_loaded[slot(n)], 16)

            def expert_tiles(e, it, before):
                for n, (kind, b, h) in enumerate(MOE):
                    m = NSTREAM + n
                    if n >= RING:
                        wait_moe_slot(MOE_RELEASE[n - RING], it)
                    elif before is None:
                        wait_slot(RELEASE[m - RING])
                    else:
                        wait_moe_slot(MOE_RELEASE[NMOE + n - RING], before)
                    w = I[{"mg": "odd_moe_w_gate", "mu": "odd_moe_w_up", "md": "odd_moe_w_down"}[kind]]
                    w = w[0][bass.ds(e, 1), :, :].rearrange("a r c -> (a r) c")
                    src = long_source(w, 2 * b + h) if kind == "md" else wide_source(w, b, h)
                    sp.dma_start(target(m, kind), src).then_inc(slot_loaded[slot(m)], 16)

            expert_tiles(0, 0, None)
            with sp.Fori(1, NE) as i:
                expert_tiles(i, i, i - 1)
            sp.wait_ge(table_ready, 1)
            n_extra = sp.value_load(tabi[0:1, 0:1], min_val=0, max_val=EXTRA_MAX)
            with sp.If(n_extra > 0):
                with sp.Fori(0, n_extra) as i:
                    e = sp.value_load(tabi[0:1, bass.ds(i + 1, 1)], min_val=0, max_val=NE - 1)
                    expert_tiles(e, i + NE, i + (NE - 1))
            for t in range(NT):
                sp.wait_ge(x_ready, 4 * 3 + 2 * t + 2)
                sp.dma_start(out_dram[0, t * P:(t + 1) * P, :], x[:, t, :]).then_inc(out_done, 16)
            sp.wait_ge(out_done, 16 * NT)

        @block.tensor
        def _(pe):
            def dense(names, tile, lhs, it=None, tile_at=None):
                for h in range(2):
                    n = tile + h
                    wait_tile(pe, n, it)
                    w = wide(slot(n if it is None else NSTREAM + n))
                    for kk in range(4):
                        k = 4 * h + kk
                        for t, name in enumerate(names):
                            if k == 0:
                                wait_free(pe, name, it)
                            mm = pe.matmul(bank(name, it)[:, :], lhs(k, t), w[:, kk, :], start=(k == 0), stop=(k == KD - 1))
                            if k == KD - 1:
                                signal_filled(mm, name, it)
                    if h == 0:
                        mm.then_inc(tiles_used, 1)

            def down(name_of, b, tile, lhsT, nt, it=None):
                for h in range(2):
                    n = tile + h
                    wait_tile(pe, n, it)
                    w = long(slot(n if it is None else NSTREAM + n))
                    for kk in range(2):
                        f = 2 * h + kk
                        for t in range(nt):
                            for half in range(2):
                                first, last = b == 0 and f == 0, b == NB - 1 and f == 3
                                name = name_of(t, half)
                                if first:
                                    wait_free(pe, name, it)
                                mm = pe.matmul(bank(name, it)[:, :], lhsT(t, f), w[:, kk, half * N:(half + 1) * N],
                                               start=first, stop=last)
                                if last:
                                    signal_filled(mm, name, it)
                    if not (b == NB - 1 and h == 1):
                        mm.then_inc(tiles_used, 1)

            def transposes(name, sources, it=None):
                wait_free(pe, name, it)
                for i, src in enumerate(sources):
                    mm = pe.transpose(bank(name, it)[:, i * P:(i + 1) * P], src, ident)
                signal_filled(mm, name, it)

            def ada_reduce(j):
                layer, n = ADA[j]
                pe.wait_ge(ada_step, 8 * (j + 1))
                name = ("ada", j)
                wait_free(pe, name)
                a = acc[:, j % ACC_RING, :]
                if n // 2 in (2, 5):
                    mm = pe.matmul(bank(name)[:, :], ones, a, start=True, stop=True)
                else:
                    for c in range(4):
                        mm = pe.matmul(bank(name)[:, c:c + 1], a[:, c * P:(c + 1) * P], ones[:, 0:1], start=True, stop=True)
                signal_filled(mm, name)

            def transpose_h(w):
                for j in range(4):
                    pe.wait_ge(xn_ready, NT * (w + 1))
                    transposes(("ht", w, j), [xn[:, t, c * P:(c + 1) * P] for c in (2 * j, 2 * j + 1) for t in range(NT)])
                for j in range(4):
                    wait_emptied(pe, ("ht", w, j))

            def h_tile(k, t):
                return hT[:, k, t * P:(t + 1) * P]

            pe.wait_ge(const_in, 16)
            pe.wait_ge(rows_in, 96)
            transposes(("cols", 0), [rowsA[:, :]])
            signal_filled(pe.transpose(bank(("cols", 1))[:, 0:ROWSB], rowsB[0:ROWSB, :], ident[0:ROWSB, 0:ROWSB]), ("cols", 1))
            for j in range(4):
                ada_reduce(j)
            transpose_h(0)

            for n in range(4):
                dense([("ein", n, t) for t in range(NT)], AT[("ein", n, 0)], h_tile)
                for j in {1: [4], 2: [5, 6], 3: [7, 8, 9]}.get(n, []):
                    ada_reduce(j)
            pe.wait_ge(poolw_in, 32)
            for g in range(POOLG):
                if g == 0:
                    for t in range(NT):
                        wait_emptied(pe, ("ein", 3, t))
                u = [proj[:, t, 3 * N + g * P:3 * N + (g + 1) * P] for t in range(NT)]
                name = ("pool", g)
                wait_free(pe, name)
                pe.matmul(bank(name)[:, 0:TOK], u[0], poolc[:, g, 0:TOK], start=True, stop=False)
                mm = pe.matmul(bank(name)[:, P:TOK], u[1], poolc[:, g, TOK:3 * P], start=False, stop=True)
                signal_filled(mm, name)
                wait_emptied(pe, name)
                name = ("mix", g)
                wait_free(pe, name)
                signal_filled(pe.matmul(bank(name)[:, 0:TOK], poolw[:, g, :], pooled[:, g % 2, :], start=True, stop=True), name)
            pe.wait_ge(roped, NT)
            for j in range(4):
                transposes(("qkt", j), [proj[:, t, c * P:(c + 1) * P] for c in (2 * j, 2 * j + 1) for t in range(NT)])
            for j in range(4):
                wait_emptied(pe, ("qkt", j))

            def scores(h):
                lo = HD * (h % 2)
                q, k = qkT[lo:lo + HD, h // 2, :], qkT[lo:lo + HD, 4 + h // 2, :]
                name = ("score", h)
                wait_free(pe, name)
                pe.matmul(bank(name)[:, 0:P], q[:, 0:P], k[:, 0:P], start=True, stop=True)
                signal_filled(pe.matmul(bank(name)[:, P:3 * P], q[:, P:TOK], k[:, 0:TOK], start=True, stop=True), name)

            def weigh_values(pair):
                name = ("pv", pair)
                wait_free(pe, name)
                for h in (2 * pair, 2 * pair + 1):
                    wait_emptied(pe, ("pt", h))
                    lo = HD * (h % 2)
                    v = [proj[:, t, 2 * N + h * HD:2 * N + (h + 1) * HD] for t in range(NT)]
                    pe.matmul(bank(name)[lo:lo + HD, 0:TOK], v[0], pT[:, h % 4, 0:TOK], start=True, stop=False)
                    mm = pe.matmul(bank(name)[lo:lo + HD, P:TOK], v[1], pT[:, h % 4, TOK:3 * P], start=False, stop=True)
                signal_filled(mm, name)

            for h in range(HEADS + 2):
                if h < HEADS:
                    scores(h)
                if 1 <= h <= HEADS:
                    pe.wait_ge(normed, h)
                    transposes(("pt", h - 1), [prob[:, (h - 1) % 2, i * P:(i + 1) * P] for i in range(3)])
                if h >= 2 and h % 2 == 1:
                    weigh_values((h - 2) // 2)
            for g in range(POOLG):
                wait_emptied(pe, ("mix", g))
            for pair in range(4):
                wait_emptied(pe, ("pv", pair))
            for n in range(2):
                dense([("y", 0, t, n) for t in range(NT)], AT[("eout", n, 0)], lambda k, t: oT[:, k, t * P:(t + 1) * P])

            transpose_h(1)
            for b in range(NB + 1):
                if b < NB:
                    dense([("fg", b, t) for t in range(NT)], AT[("fg", b, 0)], h_tile)
                if b:
                    for t in range(NT):
                        wait_emptied(pe, ("fu", b - 1, t))
                        transposes(("ft", b - 1, t), [act_n[:, t, f * P:(f + 1) * P] for f in range(4)])
                    for i in range(2):
                        ada_reduce(10 + 2 * (b - 1) + i)
                if b < NB:
                    dense([("fu", b, t) for t in range(NT)], AT[("fu", b, 0)], h_tile)
                if b:
                    for t in range(NT):
                        wait_emptied(pe, ("ft", b - 1, t))
                    down(lambda t, half: ("y", 1, t, half), b - 1, AT[("fd", b - 1, 0)], lambda t, f: actT[:, t, f, :], NT)

            transpose_h(2)
            pe.wait_ge(odd_in, 80)
            wait_free(pe, ("ba",))
            for t in range(NT):
                for k in range(KD):
                    mm = pe.matmul(bank(("ba",))[:, 16 * t:16 * t + 16], h_tile(k, t), ba_w[:, k, :], start=(k == 0), stop=(k == KD - 1))
            signal_filled(mm, ("ba",))
            pe.wait_ge(ba_dve, 9)
            wait_free(pe, ("gc",))
            for c in range(2):
                pe.matmul(bank(("gc",))[:, 8 * c:8 * c + 8], const("upto"), gdec[:, 8 * c:8 * c + 8], start=True, stop=True)
            signal_filled(pe.matmul(bank(("gc",))[:, 16:24], const("after"), gdec[:, 0:8], start=True, stop=True), ("gc",))

            def project(g, r):
                n = 2 * r + g
                dense([("oin", g, r, t) for t in range(NT)], AT[("oin", n, 0)], h_tile)

            def turn(g, r):
                for t in range(NT):
                    wait_emptied(pe, ("oin", g, r, t))
                for j in range(2):
                    transposes(("rt", g, r, j), [nat[:, t, c * P:(c + 1) * P] for c in (2 * j, 2 * j + 1) for t in range(NT)])

            def per_head(name, lhsT, rhs):
                wait_free(pe, name)
                for h in range(4):
                    mm = pe.matmul(bank(name)[:, h * P:(h + 1) * P], lhsT(h), rhs(h), start=True, stop=True)
                signal_filled(mm, name)

            for g in range(ODD_GROUPS):
                project(g, 0)
                project(g, 1)
                turn(g, 0)
                project(g, 2)
                turn(g, 1)
                turn(g, 2)
                q, k, v = (qkvT[:, r] for r in range(3))
                for r in range(2):
                    pe.wait_ge(sq_ready, 2 * g + r + 1)
                    name = ("ss", g, r)
                    wait_free(pe, name)
                    for i in range(8):
                        mm = pe.matmul(bank(name)[:, i:i + 1], sq[:, i % 4, (i // 4) * P:(i // 4 + 1) * P], ones[:, 0:1], start=True, stop=True)
                    signal_filled(mm, name)
                for c in range(2):
                    pe.wait_ge(rhs_ready, 4 * g + c + 1)
                    name = ("decay", g, c)
                    wait_free(pe, name)
                    signal_filled(pe.matmul(bank(name)[:, :], const("after"), Y[:, c].rearrange("p h n -> p (h n)"), start=True, stop=True), name)
                for c in range(2):
                    pe.wait_ge(rhs_ready, 4 * g + 2 + c + 1)
                    name = ("brow", g, c)
                    wait_free(pe, name)
                    signal_filled(pe.matmul(bank(name)[:, :], ones, CT[:, c].rearrange("p h n -> p (h n)"), start=True, stop=True), name)
                pe.wait_ge(silu_ready, 3 * g + 3)
                for c in range(2):
                    cc = slice(c * P, (c + 1) * P)
                    per_head(("kk", g, c), lambda h: k[:, h, cc], lambda h: k[:, h, cc])
                for c in range(2):
                    cc = slice(c * P, (c + 1) * P)
                    per_head(("kq", g, c), lambda h: k[:, h, cc], lambda h: q[:, h, cc])
                for c in range(2):
                    transposes(("vn", g, c), [v[:, h, c * P:(c + 1) * P] for h in range(4)])
                transposes(("kn", g), [k[:, h, 0:P] for h in range(4)])
                for c in range(2):
                    pe.wait_ge(u_ready, 2 * g + c + 1)
                    transposes(("x0", g, c), [U[:, c, h, :] for h in range(4)])
                for s in range(1, 7):
                    for c in range(2):
                        pe.wait_ge(ct_ready, 12 * g + 2 * (s - 1) + c + 1)
                        if s == 1:
                            wait_emptied(pe, ("x0", g, c))
                        else:
                            wait_emptied(pe, ("dX", g, s - 1, c))
                        per_head(("Y", g, s, c), lambda h: CT[:, c, h, :], lambda h: X[:, c, h, :])
                    for c in range(2):
                        wait_emptied(pe, ("Y", g, s, c))
                        if s > 1:
                            wait_emptied(pe, ("dU", g, s - 1, c))
                        if s < 6:
                            per_head(("dX", g, s, c), lambda h: U[:, c, h, :], lambda h: Y[:, c, h, :])
                        per_head(("dU", g, s, c), lambda h: Y[:, c, h, :], lambda h: U[:, c, h, :])
                for c in range(2):
                    wait_emptied(pe, ("dU", g, 6, c))
                    wait_emptied(pe, ("vn", g, c))
                wait_emptied(pe, ("kn", g))
                per_head(("u0", g), lambda h: U[:, 0, h, :], lambda h: vb[:, 0, h, :])
                wait_emptied(pe, ("u0", g))
                per_head(("S1", g), lambda h: kg0[:, h, :], lambda h: u0[:, h, :])
                wait_emptied(pe, ("S1", g))
                per_head(("kS", g), lambda h: k[:, h, P:TOK], lambda h: S1[:, h, :])
                pe.wait_ge(r_ready, g + 1)
                per_head(("v1", g), lambda h: U[:, 1, h, :], lambda h: r1[:, h, :])
                per_head(("o0", g), lambda h: attnT[:, 0, h, :], lambda h: u0[:, h, :])
                per_head(("qS", g), lambda h: q[:, h, P:TOK], lambda h: S1[:, h, :])
                wait_emptied(pe, ("v1", g))
                per_head(("o1", g), lambda h: attnT[:, 1, h, :], lambda h: v1[:, h, :])
            for n in range(2):
                dense([("gate", n, t) for t in range(NT)], AT[("oin", 6 + n, 0)], h_tile)
            pe.wait_ge(o_ready, NT)
            for j in range(4):
                transposes(("ot", j), [xn[:, t, c * P:(c + 1) * P] for c in (2 * j, 2 * j + 1) for t in range(NT)])
            for j in range(4):
                wait_emptied(pe, ("ot", j))
            for n in range(2):
                dense([("y", 2, t, n) for t in range(NT)], AT[("oout", n, 0)], h_tile)

            transpose_h(3)
            wait_free(pe, ("route",))
            for t in range(NT):
                for k in range(KD):
                    mm = pe.matmul(bank(("route",))[:, 8 * t:8 * t + 8], h_tile(k, t), router[:, k, :], start=(k == 0), stop=(k == KD - 1))
            signal_filled(mm, ("route",))
            pe.wait_ge(sel_ready, NT)
            wait_free(pe, ("slot",))
            b = bank(("slot",))
            pe.matmul(b[:, 0:8], const("before"), sel[:, 0, :], start=True, stop=True)
            pe.matmul(b[:, 8:16], const("before"), sel[:, 1, :], start=True, stop=False)
            pe.matmul(b[:, 8:16], ones, sel[:, 0, :], start=False, stop=True)
            pe.matmul(b[:, 16:24], ones, sel[:, 0, :], start=True, stop=False)
            signal_filled(pe.matmul(b[:, 16:24], ones, sel[:, 1, :], start=False, stop=True), ("slot",))

            def expert(it):
                pe.wait_ge(place_ready, it * 4 + 4)
                for j in range(2):
                    name = ("mh", j)
                    wait_free(pe, name, it)
                    for cc in range(4):
                        c = 4 * j + cc
                        for t in range(NT):
                            mm = pe.matmul(bank(name, it)[:, cc * P:(cc + 1) * P], xn[:, t, c * P:(c + 1) * P], place[:, t, :],
                                           start=(t == 0), stop=(t == NT - 1))
                    signal_filled(mm, name, it)
                transposes(("mp",), [placew[:, t, :] for t in range(NT)], it)
                for j in range(2):
                    wait_emptied(pe, ("mh", j), it)
                for b in range(NB + 1):
                    if b < NB:
                        dense([("mg", b, 0)], MOE_AT[("mg", b, 0)], lambda k, t: heT[:, k, :], it)
                    if b:
                        wait_emptied(pe, ("mu", b - 1, 0), it)
                        transposes(("mt", b - 1, 0), [mact[:, 0, f * P:(f + 1) * P] for f in range(4)], it)
                    if b < NB:
                        dense([("mu", b, 0)], MOE_AT[("mu", b, 0)], lambda k, t: heT[:, k, :], it)
                    if b:
                        wait_emptied(pe, ("mt", b - 1, 0), it)
                        down(lambda t, half: ("my", half), b - 1, MOE_AT[("md", b - 1, 0)], lambda t, f: mactT[:, t, f, :], 1, it)
                wait_emptied(pe, ("mp",), it)
                for n in range(2):
                    wait_emptied(pe, ("my", n), it)
                for t in range(NT):
                    for n in range(2):
                        name = ("mo", t, n)
                        wait_free(pe, name, it)
                        signal_filled(pe.matmul(bank(name, it)[:, :], placeT[:, t, :], ye[:, n * N:(n + 1) * N], start=True, stop=True), name, it)

            pe.wait_ge(table_ready, 1)
            n_extra = pe.value_load(tabi[0:1, 0:1], min_val=0, max_val=EXTRA_MAX)
            with pe.Fori(0, NE) as i:
                expert(i)
            with pe.If(n_extra > 0):
                with pe.Fori(0, n_extra) as i:
                    expert(i + NE)

        @block.scalar
        def _(act):
            steps = [0]
            told = {}

            def tell(ins, signal):
                told[id(signal)] = told.get(id(signal), 0) + 1
                ins.then_inc(signal, 1)
                act.wait_ge(signal, told[id(signal)])

            def hand_over(ins, name, it=None):
                signal_emptied(ins, name, it)
                wait_emptied(act, name, it)

            def link(ins):
                steps[0] += 1
                ins.then_inc(act_step, 1)
                act.wait_ge(act_step, steps[0])

            def flat(ap):
                return ap.rearrange("a (r p) -> (a r) p", p=P)

            act.dma_start(consts[:, :], const_dram).then_inc(const_in, 16)
            act.dma_start(rowsA[0:96, :], flat(I["ada_b"])).then_inc(rows_in, 16)
            act.dma_start(rowsA[96:112, :], flat(I["mix_pre_g"])).then_inc(rows_in, 16)
            act.dma_start(rowsA[112:128, :], flat(I["ffn_pre_g"])).then_inc(rows_in, 16)
            act.dma_start(rowsB[0:8, :], flat(I["c"])).then_inc(rows_in, 16)
            act.dma_start(rowsB[8:104, :], flat(I["odd_conv_w"][0])).then_inc(rows_in, 16)
            act.dma_start(rowsB[104:108, :], flat(I["even_pool_scale"])).then_inc(rows_in, 16)
            act.dma_start(x[:, :, :], I["x"][0].rearrange("(t p) d -> p t d", p=P)).then_inc(x_in, 16)
            with nc.allow_non_contiguous_dma(reason="256 positions"):
                act.dma_start(posi[:, :], I["positions"][0].rearrange("(t p) -> p t", p=P)).then_inc(pos_in, 16)
            for i in range(4):
                g = I["mix_post_g" if i % 2 == 0 else "ffn_post_g"]
                act.dma_start(grow[:, i, :], g[i // 2].partition_broadcast(P)).then_inc(grow_in, 16)
            for i in range(4):
                part = 2 if i % 2 == 0 else 5
                act.dma_start(A[:, i, :], I["ada_b"][i // 2, part * D:(part + 1) * D].partition_broadcast(P)).then_inc(abias_in, 16)
            act.dma_start(poolw[:, :, :], I["even_pool_w"][0].rearrange("g c d -> c g d")).then_inc(poolw_in, 16)
            act.dma_start(poolc[:, :, :], pool_dram.rearrange("g p n -> p g n")).then_inc(poolw_in, 16)
            act.dma_start(ba_w[:, :, :], I["odd_w_in"][0].rearrange("(k p) n -> p k n", p=P)[:, :, 4 * D:4 * D + 16]).then_inc(odd_in, 16)
            act.dma_start(router[:, :, :], I["odd_router_w"][0].rearrange("(k p) n -> p k n", p=P)).then_inc(odd_in, 16)
            act.dma_start(alog[:, :], I["odd_a_log"][0].partition_broadcast(P)).then_inc(odd_in, 16)
            act.dma_start(dtb[:, :], I["odd_dt_bias"][0].partition_broadcast(P)).then_inc(odd_in, 16)
            act.dma_start(normg[:, :], I["odd_norm_g"][0].partition_broadcast(P)).then_inc(odd_in, 16)

            def square_sums(w):
                if w == 0:
                    act.wait_ge(x_in, 16)
                for t in range(NT):
                    if w:
                        act.wait_ge(x_ready, 4 * (w - 1) + 2 * t + 2)
                    tell(act.activation(xn[:, t, :], x[:, t, :], ACT.Square, accum_out=ss[:, w, t:t + 1]), ss_ready)

            def modulate_even(w):
                for j in (0, 2):
                    name = ("ht", w, j)
                    wait_filled(act, name)
                    for cc in range(2):
                        c = 2 * j + cc
                        ins = act.activation(hT[:, c, :], bank(name)[:, cc * TOK:(cc + 1) * TOK], ACT.Identity,
                                             bias=shift[:, w, c:c + 1], scale=gain[:, w, c:c + 1])
                    hand_over(ins, name)

            def y_square_sums(w):
                for t in range(NT):
                    for n in range(2):
                        wait_filled(act, ("y", w, t, n))
                        tell(act.activation(xn[:, t, n * N:(n + 1) * N], bank(("y", w, t, n))[:, :], ACT.Square,
                             accum_out=ssy[:, w, t, n:n + 1]), ssy_ready)

            def copy_out(name, out, it=None, width=N, func=ACT.Copy):
                wait_filled(act, name, it)
                hand_over(act.activation(out, bank(name, it)[:, 0:width], func), name, it)

            copy_out(("cols", 1), colB[:, 0:ROWSB], width=ROWSB)
            wait_emptied(act, ("cols", 1))
            tell(act.activation(csil[:, :], colB[:, 0:KD], ACT.Silu), csil_ready)
            square_sums(0)
            act.wait_ge(trig_arg, 1)
            tell(act.activation(cs, rope_r, ACT.Sin), trig_ready)
            modulate_even(0)

            for n in range(4):
                for t in range(NT):
                    copy_out(("ein", n, t), proj[:, t, n * N:(n + 1) * N])
            for g in range(POOLG):
                copy_out(("pool", g), pooled[:, g % 2, :], width=TOK)
                name = ("mix", g)
                wait_filled(act, name)
                hand_over(act.activation(oT[:, 4 + g, :], bank(name)[:, 0:TOK], ACT.Copy, scale=colB[:, 104 + g:105 + g]), name)
            for j in (0, 2):
                copy_out(("qkt", j), qkT[:, 2 * j:2 * j + 2, :].rearrange("p c t -> p (c t)"))
            for h in range(HEADS + 2):
                if h < HEADS:
                    act.wait_ge(maxed, h + 1)
                    for i, (a, b) in enumerate(((0, P), (P, 3 * P))):
                        tell(act.activation(prob[:, h % 2, a:b], sL[:, h % 2, a:b], ACT.Exp, bias=nmax[:, h, i:i + 1],
                             accum_out=den[:, h, i:i + 1]), exped)
                if 1 <= h <= HEADS:
                    copy_out(("pt", h - 1), pT[:, (h - 1) % 4, :], width=3 * P)
                if h >= 2 and h % 2 == 1:
                    pair = (h - 2) // 2
                    copy_out(("pv", pair), oT[:, pair, :], width=TOK)
            y_square_sums(0)

            square_sums(1)
            modulate_even(1)
            for b in range(NB + 1):
                if b < NB:
                    for t in range(NT):
                        wait_filled(act, ("fg", b, t))
                        ins = act.activation(sil[:, t, :], bank(("fg", b, t))[:, :], ACT.Silu)
                        hand_over(ins, ("fg", b, t))
                if b:
                    for t in range(NT):
                        copy_out(("ft", b - 1, t), actT[:, t, :, :].rearrange("p f n -> p (f n)"))
            y_square_sums(1)

            square_sums(2)
            modulate_even(2)
            act.wait_ge(ba_dve, 4)
            tell(act.activation(bt[0], bt[0], ACT.Exp), ba_act)
            act.wait_ge(odd_in, 80)
            tell(act.activation(bt[3][:, 0:8], alog[:, :], ACT.Exp), ba_act)
            tell(act.activation(bt[1], bt[1], ACT.Exp), ba_act)
            tell(act.activation(bt[1], bt[1], ACT.Ln, bias=1.0), ba_act)
            name = ("gc",)
            wait_filled(act, name)
            hand_over(act.activation(eg, bank(name)[:, 0:24], ACT.Exp), name)
            for g in range(ODD_GROUPS):
                def natural(r):
                    for t in range(NT):
                        name = ("oin", g, r, t)
                        wait_filled(act, name)
                        if r:
                            wait_filled(act, ("rt", g, r - 1, 1))
                        hand_over(act.activation(nat[:, t, :], bank(name)[:, :], ACT.Copy), name)

                def activate(r):
                    act.wait_ge(conv_ready, 3 * g + r + 1)
                    tell(act.activation(qkvT[:, r].rearrange("p h t -> p (h t)"), conv[:, :, :].rearrange("p h t -> p (h t)"), ACT.Silu), silu_ready)
                    if r < 2:
                        act.wait_ge(silu_ready, 3 * g + r + 1)
                        if r == 1:
                            wait_filled(act, ("ss", g, 0))
                        tell(act.activation(sq[:, :, :].rearrange("p h t -> p (h t)"), qkvT[:, r].rearrange("p h t -> p (h t)"), ACT.Square), sq_ready)

                natural(0)
                natural(1)
                activate(0)
                natural(2)
                activate(1)
                activate(2)
                for c in range(2):
                    wait_emptied(act, ("decay", g, c))
                    e = ET[:, c].rearrange("p h n -> p (h n)")
                    tell(act.activation(e, e, ACT.Exp), et_act)
                for s in range(1, 7):
                    for c in range(2):
                        copy_out(("Y", g, s, c), Y[:, c].rearrange("p h n -> p (h n)"))
                copy_out(("u0", g), u0.rearrange("p h n -> p (h n)"))
                copy_out(("S1", g), S1.rearrange("p h n -> p (h n)"))
                copy_out(("v1", g), v1.rearrange("p h n -> p (h n)"))
                copy_out(("o0", g), xn[:, 0, g * N:(g + 1) * N])
            for n in range(2):
                for t in range(NT):
                    copy_out(("gate", n, t), sgate[:, t, n * N:(n + 1) * N], func=ACT.Silu)
            for j in (0, 2):
                copy_out(("ot", j), hT[:, 2 * j:2 * j + 2, :].rearrange("p c t -> p (c t)"))
            y_square_sums(2)

            square_sums(3)
            modulate_even(3)
            act.wait_ge(route_arg, 1)
            tell(act.activation(pexp[:, 1, :], pexp[:, 0, :], ACT.Exp), route_exp)

            def expert(it):
                name = ("mh", 0)
                wait_filled(act, name, it)
                for cc in range(4):
                    ins = act.activation(heT[:, cc, :], bank(name, it)[:, cc * P:(cc + 1) * P], ACT.Identity,
                                         bias=shift[:, 3, cc:cc + 1], scale=gain[:, 3, cc:cc + 1])
                hand_over(ins, name, it)
                copy_out(("mp",), placeT[:, :, :].rearrange("p t n -> p (t n)"), it, width=TOK)
                for b in range(NB + 1):
                    if b < NB:
                        wait_filled(act, ("mg", b, 0), it)
                        if b:
                            wait_emptied(act, ("mu", b - 1, 0), it)
                        hand_over(act.activation(msil[:, 0, :], bank(("mg", b, 0), it)[:, :], ACT.Silu), ("mg", b, 0), it)
                    if b:
                        copy_out(("mt", b - 1, 0), mactT[:, 0, :, :].rearrange("p f n -> p (f n)"), it)
                copy_out(("my", 0), ye[:, 0:N], it)

            act.wait_ge(table_ready, 1)
            n_extra = act.value_load(tabi[0:1, 0:1], min_val=0, max_val=EXTRA_MAX)
            with act.Fori(0, NE) as i:
                expert(i)
            with act.If(n_extra > 0):
                with act.Fori(0, n_extra) as i:
                    expert(i + NE)
            for t in range(NT):
                act.wait_ge(mo_ready, t + 1)
                tell(act.activation(xn[:, t, :], yout[:, t, :], ACT.Square, accum_out=ssy[:, 3, t, 0:1]), ssy_ready)

        @block.gpsimd
        def _(pool):
            steps = [0]
            told = {}

            def tell(ins, signal):
                told[id(signal)] = told.get(id(signal), 0) + 1
                ins.then_inc(signal, 1)
                pool.wait_ge(signal, told[id(signal)])

            def hand_over(ins, name, it=None):
                signal_emptied(ins, name, it)
                wait_emptied(pool, name, it)

            def link(ins):
                steps[0] += 1
                ins.then_inc(pool_step, 1)
                pool.wait_ge(pool_step, steps[0])

            link(pool.memset(half_neg[:, :], -0.5))

            def x_rstd(w):
                pool.wait_ge(ss_ready, NT * (w + 1))
                link(pool.tensor_scalar(rstd[:, w, :], ss[:, w, :], 1.0 / D, EPS, ALU.mult, ALU.add))
                tell(pool.tensor_tensor(rstd[:, w, :], rstd[:, w, :], half_neg[:, 0:NT], ALU.pow), rstd_ready)

            def y_rstd(w):
                pool.wait_ge(ssy_ready, 4 * w + (2 if w == 3 else 4))
                if w < 3:
                    link(pool.tensor_tensor(rstdy[:, w, :], ssy[:, w, :, 0], ssy[:, w, :, 1], ALU.add))
                    link(pool.tensor_scalar(rstdy[:, w, :], rstdy[:, w, :], 1.0 / D, EPS, ALU.mult, ALU.add))
                else:
                    link(pool.tensor_scalar(rstdy[:, w, :], ssy[:, w, :, 0], 1.0 / D, EPS, ALU.mult, ALU.add))
                tell(pool.tensor_tensor(rstdy[:, w, :], rstdy[:, w, :], half_neg[:, 0:NT], ALU.pow), rstdy_ready)

            x_rstd(0)
            y_rstd(0)
            x_rstd(1)
            y_rstd(1)
            x_rstd(2)
            for g in range(ODD_GROUPS):
                for r in range(2):
                    wait_emptied(pool, ("ss", g, r))
                    tell(pool.tensor_tensor(rqk[:, r, :], ssqk[:, r, :], half_neg[:, 0:8], ALU.pow), rqk_ready)
                for s in range(1, 7):
                    for c in range(2):
                        if s == 1:
                            wait_emptied(pool, ("kk", g, c))
                        else:
                            wait_filled(pool, ("Y", g, s - 1, c))
                        tell(pool.tensor_tensor(CT[:, c], LT[:, c], row3(const("level", s * P, P), 4), ALU.mult), ct_ready)
            pool.wait_ge(fo_arg, 1)
            tell(pool.tensor_tensor(fo.rearrange("p c h -> p (c h)"), fo.rearrange("p c h -> p (c h)"), half_neg[:, :], ALU.pow), fo_ready)
            y_rstd(2)
            x_rstd(3)
            y_rstd(3)

        @block.vector
        def _(dve):
            steps = [0]
            told = {}

            def tell(ins, signal):
                told[id(signal)] = told.get(id(signal), 0) + 1
                ins.then_inc(signal, 1)
                dve.wait_ge(signal, told[id(signal)])

            def hand_over(ins, name, it=None):
                signal_emptied(ins, name, it)
                wait_emptied(dve, name, it)

            def link(ins):
                steps[0] += 1
                ins.then_inc(dve_step, 1)
                dve.wait_ge(dve_step, steps[0])

            tt, ts, stt = dve.tensor_tensor, dve.tensor_scalar, dve.scalar_tensor_tensor

            def copy_out(name, out, it=None, width=N):
                wait_filled(dve, name, it)
                hand_over(dve.tensor_copy(out, bank(name, it)[:, 0:width]), name, it)

            def ada_sum(j):
                if j >= ACC_RING:
                    wait_filled(dve, ("ada", j - ACC_RING))
                a = acc[:, j % ACC_RING, :]
                for k in range(KD):
                    n = AT[("ada", j, k // 4)]
                    if k % 4 == 0:
                        wait_tile(dve, n)
                    w = wide(slot(n))[:, k % 4, :]
                    if k == 0:
                        ins = ts(a, w, csil[:, 0:1], None, ALU.mult)
                    else:
                        dve.wait_ge(ada_step, 8 * j + k)
                        ins = stt(out=a, in0=w, scalar=csil[:, k:k + 1], in1=a, op0=ALU.mult, op1=ALU.add)
                    ins.then_inc(ada_step, 1)

            def ada_take(j):
                layer, n = ADA[j]
                part, name = n // 2, ("ada", j)
                w = 2 * layer + (part >= 3)
                wait_filled(dve, name)
                if part in (2, 5):
                    a = A[:, w, (n % 2) * N:(n % 2 + 1) * N]
                    hand_over(tt(a, a, bank(name)[:, :], ALU.add), name)
                    link(tt(a, a, grow[:, w, (n % 2) * N:(n % 2 + 1) * N], ALU.mult))
                    return
                bias = colA[:, 48 * layer + 4 * n:48 * layer + 4 * n + 4]
                lo = 4 * (n % 2)
                if part in (0, 3):
                    hand_over(tt(shift[:, w, lo:lo + 4], bank(name)[:, 0:4], bias, ALU.add), name)
                else:
                    hand_over(tt(mod_tmp[:, :], bank(name)[:, 0:4], bias, ALU.add), name)
                    g = (96 if part == 1 else 112) + 8 * layer + lo
                    link(stt(out=gain[:, w, lo:lo + 4], in0=mod_tmp[:, :], scalar=1.0, in1=colA[:, g:g + 4], op0=ALU.add, op1=ALU.mult))

            def norm_x(w):
                dve.wait_ge(rstd_ready, w + 1)
                for t in range(NT):
                    tell(ts(xn[:, t, :], x[:, t, :], rstd[:, w, t:t + 1], None, ALU.mult), xn_ready)

            def modulate_odd(w):
                for j in (1, 3):
                    name = ("ht", w, j)
                    wait_filled(dve, name)
                    for cc in range(2):
                        c = 2 * j + cc
                        ins = ts(hT[:, c, :], bank(name)[:, cc * TOK:(cc + 1) * TOK], gain[:, w, c:c + 1], shift[:, w, c:c + 1], ALU.mult, ALU.add)
                    hand_over(ins, name)

            def add_y(w):
                dve.wait_ge(rstdy_ready, w + 1)
                for t in range(NT):
                    for n in range(2):
                        cols = slice(n * N, (n + 1) * N)
                        if w < 3:
                            name = ("y", w, t, n)
                            ins = stt(out=xn[:, t, cols], in0=bank(name)[:, :], scalar=rstdy[:, w, t:t + 1], in1=A[:, w, cols], op0=ALU.mult, op1=ALU.mult)
                            hand_over(ins, name)
                        else:
                            link(stt(out=xn[:, t, cols], in0=yout[:, t, cols], scalar=rstdy[:, w, t:t + 1], in1=A[:, w, cols], op0=ALU.mult, op1=ALU.mult))
                        tell(tt(x[:, t, cols], x[:, t, cols], xn[:, t, cols], ALU.add), x_ready)

            copy_out(("cols", 0), colA[:, :], width=P)
            dve.wait_ge(pos_in, 16)
            link(dve.tensor_copy(posf[:, :], posi[:, :]))
            ang, ang2 = rope_in[:, 0, :], rope_in[:, 1, :]
            for t in range(NT):
                for half in range(2):
                    at = half * NT * ROT + t * ROT
                    link(ts(ang[:, at:at + ROT], const("freq"), posf[:, t:t + 1], None, ALU.mult))
            link(stt(out=rope_n, in0=ang, scalar=0.15915494309189535, in1=const("phase"), op0=ALU.mult, op1=ALU.add))
            link(ts(rope_n, rope_n, MAGIC, None, ALU.add))
            link(ts(rope_n, rope_n, -MAGIC, None, ALU.add))
            link(stt(out=ang2, in0=rope_n, scalar=-TWO_PI_HI, in1=ang, op0=ALU.mult, op1=ALU.add))
            link(stt(out=ang2, in0=rope_n, scalar=-TWO_PI_LO, in1=ang2, op0=ALU.mult, op1=ALU.add))
            link(stt(out=ang2, in0=const("phase"), scalar=6.283185307179586, in1=ang2, op0=ALU.mult, op1=ALU.add))
            tell(ts(rope_r, ang2, 3.1415925, -3.1415925, ALU.min, ALU.max), trig_arg)
            dve.wait_ge(csil_ready, 1)
            wait_emptied(dve, ("cols", 0))
            dve.wait_ge(abias_in, 64)
            dve.wait_ge(grow_in, 64)
            for j in range(4):
                ada_sum(j)
                if j:
                    ada_take(j - 1)
            ada_take(3)
            dve.wait_ge(x_in, 16)
            norm_x(0)
            modulate_odd(0)

            ada_sum(4)
            ada_sum(5)
            ada_take(4)
            for n in range(2):
                for t in range(NT):
                    wait_emptied(dve, ("ein", n, t))
            dve.wait_ge(trig_ready, 1)

            def rope(t):
                qk = proj[:, t, 0:2 * N].rearrange("p (h d) -> p h d", d=HD)
                x1, x2 = qk[:, :, 0:ROT], qk[:, :, ROT:2 * ROT]
                sin = row3(cs[:, t * ROT:(t + 1) * ROT], 16)
                cos = row3(cs[:, (NT + t) * ROT:(NT + t + 1) * ROT], 16)
                tt(rope_t[:, 0], x1, cos, ALU.mult)
                tt(rope_t[:, 1], x2, sin, ALU.mult)
                tt(rope_t[:, 2], x2, cos, ALU.mult)
                link(tt(rope_t[:, 3], x1, sin, ALU.mult))
                link(tt(x1, rope_t[:, 0], rope_t[:, 1], ALU.subtract))
                tell(tt(x2, rope_t[:, 2], rope_t[:, 3], ALU.add), roped)

            for t in range(NT):
                rope(t)
            ada_sum(6)
            ada_take(5)
            ada_sum(7)
            ada_take(6)
            ada_sum(8)
            ada_take(7)
            ada_sum(9)
            ada_take(8)
            ada_take(9)
            for j in (1, 3):
                copy_out(("qkt", j), qkT[:, 2 * j:2 * j + 2, :].rearrange("p c t -> p (c t)"))
            for h in range(HEADS + 1):
                if h < HEADS:
                    name = ("score", h)
                    wait_filled(dve, name)
                    s = sL[:, h % 2, :]
                    ins = stt(out=s, in0=bank(name)[:, 0:3 * P], scalar=HD ** -0.5, in1=const("mask"), op0=ALU.mult, op1=ALU.add)
                    hand_over(ins, name)
                    link(dve.tensor_reduce(nmax[:, h, 0:1], s[:, 0:P], AX.X, ALU.max, negate=True))
                    tell(dve.tensor_reduce(nmax[:, h, 1:2], s[:, P:3 * P], AX.X, ALU.max, negate=True), maxed)
                if h:
                    g = h - 1
                    dve.wait_ge(exped, 2 * h)
                    link(dve.reciprocal(rden[:, g, :], den[:, g, :]))
                    link(ts(prob[:, g % 2, 0:P], prob[:, g % 2, 0:P], rden[:, g, 0:1], None, ALU.mult))
                    tell(ts(prob[:, g % 2, P:3 * P], prob[:, g % 2, P:3 * P], rden[:, g, 1:2], None, ALU.mult), normed)
            add_y(0)

            norm_x(1)
            modulate_odd(1)
            for b in range(NB):
                j = 10 + 2 * b
                if b:
                    ada_take(j - 2)
                    ada_take(j - 1)
                for t in range(NT):
                    name = ("fu", b, t)
                    wait_emptied(dve, ("fg", b, t))
                    wait_filled(dve, name)
                    ins = tt(act_n[:, t, :], sil[:, t, :], bank(name)[:, :], ALU.mult)
                    hand_over(ins, name)
                for i in range(2):
                    ada_sum(j + i)
            ada_take(22)
            ada_take(23)
            add_y(1)

            norm_x(2)
            modulate_odd(2)
            dve.wait_ge(odd_in, 80)
            name = ("ba",)
            wait_filled(dve, name)
            hand_over(dve.tensor_copy(ba.rearrange("p t n -> p (t n)"), bank(name)[:, 0:32]), name)

            def gate_step(ins):
                gate_n[0] += 1
                ins.then_inc(ba_dve, 1)
                dve.wait_ge(ba_dve, gate_n[0])

            gate_n = [0]
            z = bt[2].rearrange("p (t h) -> p t h", t=NT)
            gate_step(ts(bt[0].rearrange("p (t h) -> p t h", t=NT), ba[:, :, 0:8], -1.0, None, ALU.mult))
            gate_step(tt(z, ba[:, :, 8:16], row3(dtb[:, :], NT), ALU.add))
            gate_step(stt(out=bt[1], in0=bt[2], scalar=-1.0, in1=bt[2], op0=ALU.mult, op1=ALU.min))
            gate_step(ts(bt[2], bt[2], 0.0, None, ALU.max))
            dve.wait_ge(ba_act, 1)
            gate_step(ts(bt[0], bt[0], 1.0, None, ALU.add))
            gate_step(dve.reciprocal(beta, bt[0]))
            dve.wait_ge(ba_act, 4)
            gate_step(tt(gdec, bt[1], bt[2], ALU.add))
            g3 = gdec.rearrange("p (t h) -> p t h", t=NT)
            gate_step(tt(g3, g3, row3(bt[3][:, 0:8], NT), ALU.mult))
            gate_step(ts(gdec, gdec, -1.0, None, ALU.mult))
            wait_emptied(dve, ("gc",))
            for g in range(ODD_GROUPS):
                heads = slice(4 * g, 4 * g + 4)
                if g:
                    wait_filled(dve, ("o1", g - 1))
                link(dve.memset(raw[:, :, 0:3], 0.0))
                for r in range(3):
                    for j in range(2):
                        name = ("rt", g, r, j)
                        wait_filled(dve, name)
                        ins = dve.tensor_copy(raw[:, 2 * j:2 * j + 2, 3:3 + TOK], bank(name)[:, :].rearrange("p (h t) -> p h t", h=2))
                        hand_over(ins, name)
                    if 3 * g + r:
                        dve.wait_ge(silu_ready, 3 * g + r)
                    for w in range(CONVW):
                        for h in range(4):
                            col = colB[:, 8 + 24 * w + 8 * r + 4 * g + h:9 + 24 * w + 8 * r + 4 * g + h]
                            src = raw[:, h, w:w + TOK]
                            if w == 0:
                                ins = ts(conv[:, h, :], src, col, None, ALU.mult)
                            else:
                                ins = stt(out=conv[:, h, :], in0=src, scalar=col, in1=conv[:, h, :], op0=ALU.mult, op1=ALU.add)
                            if w == CONVW - 1 and h == 3:
                                tell(ins, conv_ready)
                            elif h == 3:
                                link(ins)
                dve.wait_ge(conv_ready, 3 * g + 3)
                dve.wait_ge(silu_ready, 3 * g + 3)
                for r in range(2):
                    name = ("ss", g, r)
                    wait_filled(dve, name)
                    hand_over(ts(ssqk[:, r, :], bank(name)[:, 0:8], EPS, None, ALU.add), name)
                for c in range(2):
                    gd = gdec[:, 8 * c + 4 * g:8 * c + 4 * g + 4]
                    tell(tt(Y[:, c], row3(const("upto"), 4), col3(gd, P), ALU.mult), rhs_ready)
                dve.wait_ge(rqk_ready, 2 * g + 2)
                rk = rqk[:, 1, :]
                for c in range(2):
                    link(tt(bk[:, 4 * c:4 * c + 4], rk[:, 4 * c:4 * c + 4], beta[:, 8 * c + 4 * g:8 * c + 4 * g + 4], ALU.mult))
                    link(ts(rsq[:, c, heads], rqk[:, 0, 4 * c:4 * c + 4], DH ** -0.5, None, ALU.mult))
                for c in range(2):
                    tell(tt(CT[:, c], row3(ident, 4), col3(bk[:, 4 * c:4 * c + 4], P), ALU.mult), rhs_ready)
                link(tt(kge, rk[:, 0:4], eg[:, 16 + 4 * g:20 + 4 * g], ALU.mult))
                link(tt(nbe, bk[:, 4:8], eg[:, 8 + 4 * g:12 + 4 * g], ALU.mult))
                for c in range(2):
                    name = ("decay", g, c)
                    wait_filled(dve, name)
                    ins = tt(ET[:, c], bank(name)[:, :].rearrange("p (h n) -> p h n", h=4), row3(const("neg"), 4), ALU.add)
                    hand_over(ins, name)
                for c in range(2):
                    name = ("brow", g, c)
                    wait_filled(dve, name)
                    dve.wait_ge(et_act, 2 * g + c + 1)
                    ins = tt(LT[:, c], ET[:, c], bank(name)[:, :].rearrange("p (h n) -> p h n", h=4), ALU.mult)
                    hand_over(ins, name)
                for c in range(2):
                    name = ("kk", g, c)
                    wait_filled(dve, name)
                    for h in range(4):
                        ins = stt(out=LT[:, c, h, :], in0=bank(name)[:, h * P:(h + 1) * P], scalar=rk[:, 4 * c + h:4 * c + h + 1], in1=LT[:, c, h, :],
                                  op0=ALU.mult, op1=ALU.mult)
                    hand_over(ins, name)
                    link(tt(U[:, c], LT[:, c], row3(const("level", 0, P), 4), ALU.mult))
                    tell(tt(U[:, c], row3(ident, 4), U[:, c], ALU.subtract), u_ready)
                for c in range(2):
                    name = ("kq", g, c)
                    wait_filled(dve, name)
                    for h in range(4):
                        ins = stt(out=attnT[:, c, h, :], in0=bank(name)[:, h * P:(h + 1) * P], scalar=rk[:, 4 * c + h:4 * c + h + 1], in1=ET[:, c, h, :],
                                  op0=ALU.mult, op1=ALU.mult)
                    hand_over(ins, name)
                for c in range(2):
                    name = ("vn", g, c)
                    wait_filled(dve, name)
                    ins = tt(vb[:, c], bank(name)[:, :].rearrange("p (h n) -> p h n", h=4), col3(beta[:, 8 * c + 4 * g:8 * c + 4 * g + 4], P), ALU.mult)
                    hand_over(ins, name)
                name = ("kn", g)
                wait_filled(dve, name)
                hand_over(tt(kg0, bank(name)[:, :].rearrange("p (h n) -> p h n", h=4), col3(kge, P), ALU.mult), name)
                for c in range(2):
                    copy_out(("x0", g, c), X[:, c].rearrange("p h n -> p (h n)"))
                for s in range(1, 7):
                    for c in range(2):
                        for what, M in (("dX", X), ("dU", U)):
                            if what == "dX" and s == 6:
                                continue
                            name = (what, g, s, c)
                            wait_filled(dve, name)
                            if s > 1:
                                wait_emptied(dve, (what, g, s - 1, c))
                            elif what == "dX":
                                wait_emptied(dve, ("x0", g, c))
                            else:
                                dve.wait_ge(u_ready, 2 * g + c + 1)
                            m = M[:, c].rearrange("p h n -> p (h n)")
                            hand_over(tt(m, m, bank(name)[:, :], ALU.subtract), name)
                name = ("kS", g)
                wait_filled(dve, name)
                hand_over(tt(r1, bank(name)[:, :].rearrange("p (h n) -> p h n", h=4), col3(nbe, P), ALU.mult), name)
                wait_emptied(dve, ("vn", g, 1))
                tell(tt(r1, vb[:, 1], r1, ALU.subtract), r_ready)
                name = ("qS", g)
                wait_filled(dve, name)
                hand_over(tt(qs, bank(name)[:, :].rearrange("p (h n) -> p h n", h=4), col3(eg[:, 8 + 4 * g:12 + 4 * g], P), ALU.mult), name)
                name = ("o1", g)
                wait_filled(dve, name)
                hand_over(tt(xn[:, 1, g * N:(g + 1) * N], qs.rearrange("p h n -> p (h n)"), bank(name)[:, :], ALU.add), name)
            for g in range(ODD_GROUPS):
                wait_emptied(dve, ("o0", g))
            for t in range(NT):
                o = xn[:, t, :]
                o2 = scratch[:, 2048:3072]
                wait_filled(dve, ("o1", ODD_GROUPS - 1))
                link(tt(o2, o, o, ALU.mult))
                link(dve.tensor_reduce(sso[:, t, :], o2.rearrange("p (h n) -> p h n", n=DH), AX.X, ALU.add))
            link(tt(f1, rsq, rsq, ALU.mult))
            link(tt(f1, f1, sso, ALU.mult))
            tell(ts(fo, f1, 1.0 / DH, EPS, ALU.mult, ALU.add), fo_arg)
            dve.wait_ge(fo_ready, 1)
            link(tt(fo, fo, rsq, ALU.mult))
            for t in range(NT):
                o3 = xn[:, t, :].rearrange("p (h n) -> p h n", n=DH)
                link(tt(o3, o3, col3(fo[:, t, :], DH), ALU.mult))
                link(tt(o3, o3, row3(normg[:, :], HEADS), ALU.mult))
                for n in range(2):
                    wait_emptied(dve, ("gate", n, t))
                tell(tt(xn[:, t, :], xn[:, t, :], sgate[:, t, :], ALU.mult), o_ready)
            for j in (1, 3):
                copy_out(("ot", j), hT[:, 2 * j:2 * j + 2, :].rearrange("p c t -> p (c t)"))
            add_y(2)

            norm_x(3)
            modulate_odd(3)
            name = ("route",)
            wait_filled(dve, name)
            hand_over(dve.tensor_copy(logit.rearrange("p t e -> p (t e)"), bank(name)[:, 0:16]), name)
            for t in range(NT):
                link(dve.max(best[:, t, :], logit[:, t, :]))
                link(dve.max_index(besti[:, t, :], best[:, t, :], logit[:, t, :]))
            link(dve.tensor_copy(bestf, besti[:, :, :]))
            tell(tt(pexp[:, 0, :], best[:, :, 1], best[:, :, 0], ALU.subtract), route_arg)
            dve.wait_ge(route_exp, 1)
            link(ts(pexp[:, 2, :], pexp[:, 1, :], 1.0, None, ALU.add))
            link(dve.reciprocal(pexp[:, 3, :], pexp[:, 2, :]))
            link(tt(pexp[:, 4, :], pexp[:, 3, :], pexp[:, 1, :], ALU.mult))
            for t in range(NT):
                first, second = bestf[:, t, 0:1], bestf[:, t, 1:2]
                link(ts(sel[:, t, :], const("iota8"), first, None, ALU.is_equal))
                link(ts(comb[:, t, :], sel[:, t, :], pexp[:, 3, t:t + 1], None, ALU.mult))
                link(ts(rt[:, t, :], const("iota8"), second, None, ALU.is_equal))
                link(stt(out=comb[:, t, :], in0=rt[:, t, :], scalar=pexp[:, 4, t:t + 1], in1=comb[:, t, :], op0=ALU.mult, op1=ALU.add))
                tell(tt(sel[:, t, :], sel[:, t, :], rt[:, t, :], ALU.add), sel_ready)
            name = ("slot",)
            wait_filled(dve, name)
            hand_over(dve.tensor_copy(pos[:, :, :].rearrange("p t e -> p (t e)"), bank(name)[:, 0:24]), name)
            over, upto = table[:, 0, :], table[:, 1, :]
            link(ts(over, pos[:, 2, :], float(P), None, ALU.is_gt))
            link(dve.tensor_tensor_scan(upto, over, over, 0.0, ALU.add, ALU.max))
            link(dve.tensor_copy(tabf[:, 0:1], upto[:, NE - 1:NE]))
            for j in range(EXTRA_MAX):
                link(ts(match[:, j, :], upto, float(j + 1), None, ALU.is_equal))
                link(tt(match[:, j, :], match[:, j, :], over, ALU.mult))
                link(tt(match[:, j, :], match[:, j, :], const("iota8"), ALU.mult))
                link(dve.tensor_reduce(tabf[:, 1 + j:2 + j], match[:, j, :], AX.X, ALU.add))
            link(dve.memset(yout[:, :, :].rearrange("p t d -> p (t d)"), 0.0))
            tell(dve.tensor_copy(tabi[:, :], tabf[:, :]), table_ready)
            dve.wait_ge(table_ready, 1)

            def expert(it, e, first_slot):
                for t in range(NT):
                    at, on, weight = (a[:, t, bass.ds(e, 1)] for a in (pos, sel, comb))
                    slots = const("iota", first_slot, P)
                    ts(place[:, t, :], slots, at, on, ALU.is_equal, ALU.mult).then_inc(place_ready, 1)
                    ts(placew[:, t, :], slots, at, weight, ALU.is_equal, ALU.mult).then_inc(place_ready, 1)
                name = ("mh", 1)
                wait_filled(dve, name, it)
                for cc in range(4):
                    c = 4 + cc
                    ins = ts(heT[:, c, :], bank(name, it)[:, cc * P:(cc + 1) * P], gain[:, 3, c:c + 1], shift[:, 3, c:c + 1], ALU.mult, ALU.add)
                hand_over(ins, name, it)
                for b in range(NB):
                    wait_emptied(dve, ("mg", b, 0), it)
                    wait_filled(dve, ("mu", b, 0), it)
                    ins = tt(mact[:, 0, :], msil[:, 0, :], bank(("mu", b, 0), it)[:, :], ALU.mult)
                    hand_over(ins, ("mu", b, 0), it)
                copy_out(("my", 1), ye[:, N:D], it)
                for t in range(NT):
                    for n in range(2):
                        name = ("mo", t, n)
                        wait_filled(dve, name, it)
                        y = yout[:, t, n * N:(n + 1) * N]
                        hand_over(tt(y, y, bank(name, it)[:, :], ALU.add), name, it)

            n_extra = dve.value_load(tabi[0:1, 0:1], min_val=0, max_val=EXTRA_MAX)
            with dve.Fori(0, NE) as i:
                expert(i, i, 0)
            with dve.If(n_extra > 0):
                with dve.Fori(0, n_extra) as i:
                    e = dve.value_load(tabi[0:1, bass.ds(i + 1, 1)], min_val=0, max_val=NE - 1)
                    expert(i + NE, e, P)
            dve.nop().then_inc(mo_ready, 1)
            dve.nop().then_inc(mo_ready, 1)
            add_y(3)


def kernel(**inputs):
    import numpy as np
    import concourse.bacc as bacc
    from concourse.bass_utils import run_bass_kernel_spmd

    nc = bacc.Bacc("TRN2", target_bir_lowering=False, num_devices=1)
    arrays, aps = {}, {}

    def give(name, a):
        arrays[name] = a
        return nc.dram_tensor(name, a.shape, mybir.dt.from_np(a.dtype), kind="ExternalInput").ap()

    for name in IN_NAMES:
        aps[name] = give(f"in_{name}", np.ascontiguousarray(inputs[name]))
    table, pool = constants(np)
    const_dram, pool_dram = give("in_constants", table), give("in_pool_windows", pool)
    out = nc.dram_tensor("out_x", (1, TOK, D), F32, kind="ExternalOutput").ap()
    build_trunk(nc, aps, const_dram, pool_dram, out)
    result = run_bass_kernel_spmd(nc, [arrays], core_ids=[0])
    return result.results[0]["out_x"]
```

```python
from contextlib import ExitStack

import concourse.bass as bass
from concourse import mybir

F32 = mybir.dt.float32
F32R = mybir.dt.float32r
I32 = mybir.dt.int32
U32 = mybir.dt.uint32
ALU = mybir.AluOpType
ACT = mybir.ActivationFunctionType
AX = mybir.AxisListType

P = 128
TOK = 256
NT = TOK // P
D = 1024
KD = D // P
N = 512
FFN = 3584
NB = FFN // N
HEADS = 8
HD = 64
ROT = 8
POOLG = 4
DH = 128
NE = 8
CONVW = 4
EPS = 1e-6
RING = 6
HALF = 1024
PARTS = 4
TILE = 2048
NEG = -1e30
MAGIC = 12582912.0
TWO_PI_HI = 6.28125
TWO_PI_LO = 0.0019353071795864769
ACC_RING = 2
A_RING = 3
ROWSB = 8 + 96 + 4
SCRATCH = 10240
EXTRA_MAX = 3

CONST = {}
_at = 0
for _name, _n in [("ident", P), ("ones", P), ("mask", 3 * P), ("upto", P), ("after", P), ("before", P),
                  ("neg", P), ("level", 7 * P), ("iota", 2 * P), ("iota8", 8), ("freq", ROT), ("phase", 2 * NT * ROT)]:
    CONST[_name] = (_at, _n)
    _at += _n
CONST_N = _at


def constants(np):
    out = np.zeros((P, CONST_N), np.float32)

    def put(name, value):
        a, n = CONST[name]
        out[:, a:a + n] = value

    row, col = np.arange(P)[:, None], np.arange(P)[None, :]
    put("ident", row == col)
    put("ones", 1.0)
    i, j = np.arange(TOK)[:, None], np.arange(TOK)[None, :]
    count = ((i >= j) & (i - j <= 128)).astype(np.float64)
    for dilation in (4, 16):
        count += (i >= j) & ((i - j) % dilation == 0)
    log_count = np.where(count > 0, np.log(np.maximum(count, 1)), NEG)
    put("mask", np.concatenate([log_count[:P, :P], log_count[P:, :]], axis=1))
    put("upto", row <= col)
    put("after", row > col)
    put("before", row < col)
    put("neg", np.where(row <= col, 0.0, NEG))
    levels = [(col // (2 * s) == row // (2 * s)) & (col % (2 * s) >= s) & (row % (2 * s) < s)
              for s in (1, 2, 4, 8, 16, 32, 64)]
    put("level", np.concatenate(levels, axis=1))
    put("iota", np.arange(2 * P)[None, :])
    put("iota8", np.arange(8)[None, :])
    put("freq", (np.float32(500000.0) ** (-np.arange(0, 16, 2, dtype=np.float32) / np.float32(16)))[None, :])
    put("phase", np.repeat([0.0, 0.25], NT * ROT)[None, :])
    pool = np.zeros((POOLG, P, 3 * P), np.float32)
    for g, window in enumerate((2, 4, 8, 16)):
        t, s = np.arange(TOK)[None, :], np.arange(TOK)[:, None]
        w = ((t - s >= 0) & (t - s < window)) / np.minimum(t + 1, window) - (t == s)
        pool[g] = np.concatenate([w[:P, :], w[P:, P:]], axis=1)
    return out, pool


def ffn_tiles(kind, between):
    out, between = [], list(between)
    for b in range(NB):
        out += [(kind + "g", b, h) for h in range(2)]
        out += between[:2]
        out += [(kind + "u", b, h) for h in range(2)]
        out += [(kind + "d", b - 1, h) for h in range(2)] if b else []
        out += between[2:4]
        between = between[4:]
    return out + [(kind + "d", NB - 1, h) for h in range(2)]


def halves(kind, ns):
    return [(kind, n, h) for n in ns for h in range(2)]


ADA = [(0, n) for n in range(12)] + [(1, n) for n in range(12)]
ADA_AT = {a: j for j, a in enumerate(ADA)}
ada_halves = [[("ada", j, h) for h in range(2)] for j in range(24)]
STREAM = sum(ada_halves[0:4], []) + halves("ein", [0]) + ada_halves[4] + halves("ein", [1]) + ada_halves[5] + ada_halves[6]
STREAM += halves("ein", [2]) + ada_halves[7] + ada_halves[8] + halves("ein", [3]) + ada_halves[9] + halves("eout", [0, 1])
STREAM += ffn_tiles("f", sum(ada_halves[10:], []))
STREAM += halves("oin", [0, 2, 4, 1, 3, 5, 6, 7]) + halves("oout", [0, 1])
AT = {t: n for n, t in enumerate(STREAM)}
NSTREAM = len(STREAM)
MOE = ffn_tiles("m", [])
MOE_AT = {t: n for n, t in enumerate(MOE)}
NMOE = len(MOE)
assert NMOE % RING == 0 and len(AT) == NSTREAM

DENSE = [t for t in STREAM if t[0] != "ada"]
HALF_AT = {t: 2 * n for n, t in enumerate(DENSE)}
NHALF = 2 * len(DENSE)
MOE_HALF_AT = {t: 2 * n for n, t in enumerate(MOE)}
NMOE_HALF = 2 * NMOE
assert NHALF % PARTS == 0 and NMOE_HALF % PARTS == 0

ODD_GROUPS = 2


def static_banks():
    out = [(("cols", 0), 6), (("cols", 1), 7)]
    out += [(("ada", j), 7) for j in range(4)]
    out += [(("ht", 0, j), 4 + j % 4) for j in range(4)]
    for n in range(4):
        out += [(("ein", n, t), 2 * (n % 2) + t) for t in range(NT)]
        out += [(("ada", j), 7) for j in {1: [4], 2: [5, 6], 3: [7, 8, 9]}.get(n, [])]
    for g in range(POOLG):
        out += [(("pool", g), 6), (("mix", g), 7)]
    out += [(("qkt", j), 2 + j) for j in range(4)]
    for h in range(HEADS + 2):
        if h < HEADS:
            out += [(("score", h), h % 2)]
        if 1 <= h <= HEADS:
            out += [(("pt", h - 1), 2 + (h - 1) % 2)]
        if h >= 2 and h % 2 == 1:
            out += [(("pv", (h - 2) // 2), 4 + (h - 2) // 2 % 2)]
    out += [(("y", 0, t, n), 2 * t + n) for n in range(2) for t in range(NT)]
    out += [(("ht", 1, j), 4 + j % 4) for j in range(4)]
    for b in range(NB + 1):
        if b:
            out += [(("ada", 8 + 2 * b), 7)]
        if b < NB:
            out += [(("fg", b, t), 4 + t) for t in range(NT)]
        if b:
            out += [(("ft", b - 1, 0), 6), (("ada", 9 + 2 * b), 7)]
        if b < NB:
            out += [(("fu", b, t), 4 + t) for t in range(NT)]
        if b:
            out += [(("ft", b - 1, 1), 6)]
        if b == 1:
            out += [(("y", 1, t, n), 2 * t + n) for t in range(NT) for n in range(2)]
    out += [(("ht", 2, j), 4 + j % 4) for j in range(4)]
    out += [(("ba",), 4), (("gc",), 5)]
    for g in range(ODD_GROUPS):
        out += [(("oin", g, 0, t), t) for t in range(NT)] + [(("oin", g, 1, t), 4 + t) for t in range(NT)]
        out += [(("rt", g, 0, j), 2 + j) for j in range(2)] + [(("oin", g, 2, t), t) for t in range(NT)]
        out += [(("rt", g, 1, j), 2 + j) for j in range(2)] + [(("rt", g, 2, j), 4 + j) for j in range(2)]
        out += [(("ss", g, 0), 6), (("ss", g, 1), 7)]
        out += [(("decay", g, c), 4 + c) for c in range(2)] + [(("brow", g, c), 6 + c) for c in range(2)]
        out += [(("kk", g, c), 0 + c) for c in range(2)] + [(("kq", g, c), 2 + c) for c in range(2)]
        out += [(("vn", g, c), 4 + c) for c in range(2)] + [(("kn", g), 6)]
        out += [(("x0", g, c), 0 + c) for c in range(2)]
        for s in range(1, 7):
            out += [(("Y", g, s, c), 2 + c) for c in range(2)]
            for c in range(2):
                out += [(("dX", g, s, c), 4 + c)] if s < 6 else []
                out += [(("dU", g, s, c), 6 + c)]
        out += [(("u0", g), 0), (("S1", g), 1), (("kS", g), 2), (("v1", g), 3), (("o0", g), 4), (("qS", g), 5), (("o1", g), 6)]
    out += [(("gate", n, t), 2 * n + t) for n in range(2) for t in range(NT)]
    out += [(("ot", j), 4 + j) for j in range(4)]
    out += [(("y", 2, t, n), 2 * t + n) for n in range(2) for t in range(NT)]
    out += [(("ht", 3, j), 4 + j % 4) for j in range(4)]
    out += [(("route",), 4), (("slot",), 5)]
    return out


def moe_banks():
    out = [(("mh", 0), 2), (("mh", 1), 3), (("mp",), 6)]
    for b in range(NB + 1):
        if b < NB:
            out += [(("mg", b, 0), 2 + 2 * (b % 2))]
        if b:
            out += [(("mt", b - 1, 0), 6 + b % 2)]
        if b < NB:
            out += [(("mu", b, 0), 3 + 2 * (b % 2))]
        if b == 1:
            out += [(("my", n), n) for n in range(2)]
    return out + [(("mo", t, n), 4 + 2 * t + n) for t in range(NT) for n in range(2)]


def ordinals(order):
    used, place = [0] * 8, {}
    for name, bank in order:
        assert name not in place
        place[name] = (bank, used[bank])
        used[bank] += 1
    return place, used


BANK, BANK_USES = ordinals(static_banks())
MOE_BANK, MOE_BANK_USES = ordinals(moe_banks())

def half_ends(tiles, name_of):
    out, n = [], 0
    for kind, b, h in tiles:
        for part in range(2):
            name = name_of(kind, b) if h == 1 and part == 1 else None
            n += name is None
            out.append(("bank", name) if name else ("count", n))
    return out, n


def last_product(kind, b):
    if kind == "fd":
        return ("y", 1, 1, 1) if b == NB - 1 else None
    if kind == "md":
        return ("my", 1) if b == NB - 1 else None
    return {"ein": ("ein", b, 1), "eout": ("y", 0, 1, b), "fg": ("fg", b, 1), "fu": ("fu", b, 1), "mg": ("mg", b, 0), "mu": ("mu", b, 0),
            "oin": ("oin", b % 2, b // 2, 1) if b < 6 else ("gate", b - 6, 1), "oout": ("y", 2, 1, b)}[kind]


HALF_END, HALVES_COUNTED = half_ends(DENSE, last_product)
MOE_HALF_END, MOE_HALVES_COUNTED = half_ends(MOE, last_product)
IN_NAMES = ["x", "c", "positions", "ada_w", "ada_b", "mix_pre_g", "mix_post_g", "ffn_pre_g", "ffn_post_g",
            "even_w_in", "even_pool_w", "even_pool_scale", "even_w_out", "even_ffn_w_gate", "even_ffn_w_up",
            "even_ffn_w_down", "odd_w_in", "odd_conv_w", "odd_a_log", "odd_dt_bias", "odd_norm_g", "odd_w_out",
            "odd_router_w", "odd_moe_w_gate", "odd_moe_w_up", "odd_moe_w_down"]


def build_trunk(nc, I, const_dram, pool_dram, out_dram):
    ctx = ExitStack()
    with ctx:
        def sb(name, shape, dt=F32):
            return ctx.enter_context(nc.sbuf_tensor(name, shape, dt))

        def sem(name):
            return ctx.enter_context(nc.semaphore(name))

        ps = [ctx.enter_context(nc.psum_tensor(f"bank{b}", [P, N], F32)) for b in range(8)]
        ring = sb("ring", [P, RING, TILE])
        x = sb("xres", [P, NT, D])
        xn = sb("xn", [P, NT, D])
        hT = sb("hT", [P, KD, TOK])
        A = sb("A", [P, A_RING, D])
        grow = sb("grow", [P, D])
        wh = sb("wh", [P, PARTS, HALF], F32R)
        wl = sb("wl", [P, PARTS, HALF], F32R)
        LH = sb("LH", [P, KD, TOK], F32R)
        LL = sb("LL", [P, KD, TOK], F32R)
        actTh = sb("actTh", [P, NT, 4, P], F32R)
        actTl = sb("actTl", [P, NT, 4, P], F32R)
        consts = sb("consts", [P, CONST_N])
        acc = sb("acc", [P, ACC_RING, N])
        rowsA = sb("rowsA", [P, P])
        rowsB = sb("rowsB", [P, P])
        colA = sb("colA", [P, P])
        colB = sb("colB", [P, P])
        csil = sb("csil", [P, KD])
        shift = sb("shift", [P, 4, KD])
        gain = sb("gain", [P, 4, KD])
        mod_tmp = sb("mod_tmp", [P, 4])
        ss = sb("ss", [P, 4, NT])
        rstd = sb("rstd", [P, 4, NT])
        ssy = sb("ssy", [P, 4, NT, 2])
        rstdy = sb("rstdy", [P, 4, NT])
        half_neg = sb("half_neg", [P, 16])
        posi = sb("posi", [P, NT], I32)
        posf = sb("posf", [P, NT])
        ba_w = sb("ba_w", [P, KD, 16])
        router = sb("router", [P, KD, NE])
        alog = sb("alog", [P, HEADS])
        dtb = sb("dtb", [P, HEADS])
        normg = sb("normg", [P, DH])
        scratch = sb("scratch", [P, SCRATCH])

        def view(at, *shape):
            n = 1
            for s in shape:
                n *= s
            assert at + n <= SCRATCH
            ap = scratch[:, at:at + n]
            if len(shape) == 2:
                return ap.rearrange("p (a b) -> p a b", a=shape[0])
            if len(shape) == 3:
                return ap.rearrange("p (a b c) -> p a b c", a=shape[0], b=shape[1])
            return ap

        def const(name, a=0, n=None):
            at, size = CONST[name]
            return consts[:, at + a:at + a + (size if n is None else n)]

        ident, ones = const("ident"), const("ones")

        proj = view(0, NT, 4 * N)
        qkT = view(4096, 8, TOK)
        sL = view(6144, 2, 384)
        pooled = view(6144, 2, TOK)
        prob = view(6912, 2, 384)
        poolw = view(6912, POOLG, P)
        pT = view(7680, 4, 384)
        poolc = view(7680, POOLG, 384)
        rope_in = view(9216, 3, 32)
        rope_n = view(9312, 32)
        rope_r = view(9344, 32)
        cs = view(9376, 32)
        rope_t = view(9408, 4, 16, ROT)
        nmax = view(9920, HEADS, 2)
        den = view(9936, HEADS, 2)
        rden = view(9952, HEADS, 2)
        oT = hT
        sil = view(0, NT, N)
        act_n = view(1024, NT, N)
        qkvT = view(0, 3, 4, TOK)
        nat = view(3072, NT, N)
        raw = scratch[:, 4096:4096 + 4 * 260].rearrange("p (h t) -> p h t", h=4)
        conv = view(5136, 4, TOK)
        sq = view(6160, 4, TOK)
        X = view(3072, 2, 4, P)
        U = view(4096, 2, 4, P)
        Y = view(5120, 2, 4, P)
        CT = view(6144, 2, 4, P)
        LT = view(7168, 2, 4, P)
        attnT = view(8192, 2, 4, P)
        ET = view(9216, 2, 4, P)
        vb = qkvT[:, 2].rearrange("p h (c n) -> p c h n", c=2)
        kg0 = ET[:, 0]
        sgate = view(3072, NT, D)
        u0, S1 = X[:, 0], X[:, 1]
        r1, v1 = Y[:, 0], Y[:, 1]
        qs = CT[:, 0]
        small = sb("small", [P, 24, 16])
        ba, beta, gdec = small[:, 0:2, :], small[:, 2, :], small[:, 3, :]
        bt = [small[:, 4 + i, :] for i in range(4)]
        eg = small[:, 8:10, :].rearrange("p a b -> p (a b)")[:, 0:24]
        ssqk = small[:, 10, :].rearrange("p (r b) -> p r b", r=2)
        rqk = small[:, 11, :].rearrange("p (r b) -> p r b", r=2)
        bk = small[:, 12, 0:8]
        kge = small[:, 12, 8:12]
        nbe = small[:, 12, 12:16]
        rsq = small[:, 13, :].rearrange("p (c h) -> p c h", c=2)
        sso = small[:, 14, :].rearrange("p (c h) -> p c h", c=2)
        fo = small[:, 15, :].rearrange("p (c h) -> p c h", c=2)
        f1 = small[:, 16, :].rearrange("p (c h) -> p c h", c=2)
        logit = small[:, 17, :].rearrange("p (t e) -> p t e", t=NT)
        best = small[:, 18, :].rearrange("p (t e) -> p t e", t=NT)
        besti = sb("besti", [P, NT, 8], U32)
        bestf = small[:, 19, :].rearrange("p (t e) -> p t e", t=NT)
        pexp = small[:, 20, :].rearrange("p (k t) -> p k t", k=8)
        sel = small[:, 21, :].rearrange("p (t e) -> p t e", t=NT)
        comb = small[:, 22, :].rearrange("p (t e) -> p t e", t=NT)
        rt = small[:, 23, :].rearrange("p (t e) -> p t e", t=NT)
        pos = sb("pos", [P, 3, NE])
        table = sb("table", [P, 4, NE])
        match = sb("match", [P, EXTRA_MAX, NE])
        tabf = sb("tabf", [P, 4])
        tabi = sb("tabi", [P, 4], I32)
        heT = view(0, KD, P)
        place = view(1024, NT, P)
        placew = view(1280, NT, P)
        placeT = view(1536, NT, P)
        msil = view(1792, 1, N)
        mact = view(2304, 1, N)
        ye = view(3328, D)
        yout = view(4352, NT, D)

        slot_loaded = [sem(f"slot_loaded{s}") for s in range(RING)]
        hi_ready = sem("hi_ready")
        lo_ready = sem("lo_ready")
        half_used = sem("half_used")
        lhs_hi = sem("lhs_hi")
        lhs_lo = sem("lhs_lo")
        act_hi = sem("act_hi")
        gate_row_ready = sem("gate_row_ready")
        ada_step = sem("ada_step")
        filled = [sem(f"bank_filled{b}") for b in range(8)]
        emptied = [sem(f"bank_emptied{b}") for b in range(8)]
        const_in = sem("const_in")
        rows_in = sem("rows_in")
        x_in = sem("x_in")
        pos_in = sem("pos_in")
        grow_in = sem("grow_in")
        abias_in = sem("abias_in")
        poolw_in = sem("poolw_in")
        odd_in = sem("odd_in")
        out_done = sem("out_done")
        csil_ready = sem("csil_ready")
        ss_ready = sem("ss_ready")
        rstd_ready = sem("rstd_ready")
        xn_ready = sem("xn_ready")
        ssy_ready = sem("ssy_ready")
        rstdy_ready = sem("rstdy_ready")
        x_ready = sem("x_ready")
        trig_arg = sem("trig_arg")
        trig_ready = sem("trig_ready")
        roped = sem("roped")
        maxed = sem("maxed")
        exped = sem("exped")
        normed = sem("normed")
        ba_dve = sem("ba_dve")
        ba_act = sem("ba_act")
        conv_ready = sem("conv_ready")
        silu_ready = sem("silu_ready")
        sq_ready = sem("sq_ready")
        rqk_ready = sem("rqk_ready")
        rhs_ready = sem("rhs_ready")
        et_act = sem("et_act")
        ct_ready = sem("ct_ready")
        u_ready = sem("u_ready")
        fo_arg = sem("fo_arg")
        fo_ready = sem("fo_ready")
        r_ready = sem("r_ready")
        o_ready = sem("o_ready")
        route_arg = sem("route_arg")
        route_exp = sem("route_exp")
        sel_ready = sem("sel_ready")
        table_ready = sem("table_ready")
        dve_step = sem("dve_step")
        act_step = sem("act_step")
        pool_step = sem("pool_step")
        place_ready = sem("place_ready")
        mo_ready = sem("mo_ready")

        def use(name, it):
            if it is None:
                return BANK[name]
            bank, before = MOE_BANK[name]
            return bank, it * MOE_BANK_USES[bank] + (BANK_USES[bank] + before)

        def bank(name, it=None):
            return ps[use(name, it)[0]]

        def wait_free(pe, name, it=None):
            b, before = use(name, it)
            if it is not None or before:
                pe.wait_ge(emptied[b], before)

        def signal_filled(ins, name, it=None):
            ins.then_inc(filled[use(name, it)[0]], 1)

        def wait_filled(eng, name, it=None):
            b, before = use(name, it)
            eng.wait_ge(filled[b], before + 1)

        def signal_emptied(ins, name, it=None):
            ins.then_inc(emptied[use(name, it)[0]], 1)

        def wait_emptied(eng, name, it=None):
            b, before = use(name, it)
            eng.wait_ge(emptied[b], before + 1)

        def slot(n):
            return n % RING

        def wait_tile(eng, n, it=None):
            if it is None:
                eng.wait_ge(slot_loaded[n % RING], 16 * (n // RING + 1))
            else:
                m = NSTREAM + n
                eng.wait_ge(slot_loaded[m % RING], it * (16 * NMOE // RING) + 16 * (m // RING + 1))

        def wide(s):
            return ring[:, s, :].rearrange("p (k n) -> p k n", n=N)

        def long(s):
            return ring[:, s, :].rearrange("p (k n) -> p k n", n=D)

        def wait_parts(eng, g, it=None):
            if it is None:
                eng.wait_ge(lo_ready, g + 1)
            else:
                eng.wait_ge(lo_ready, it * NMOE_HALF + (NHALF + g + 1))

        def half_of_tile(g, it=None):
            tiles, at = (DENSE, AT) if it is None else (MOE, MOE_AT)
            n = at[tiles[g // 2]]
            s = slot(n if it is None else NSTREAM + n)
            return ring[:, s, (g % 2) * HALF:(g % 2 + 1) * HALF], n

        def wait_parts_free(eng, g, it=None):
            if it is None:
                if g < PARTS:
                    return
                how, value = HALF_END[g - PARTS]
                if how == "count":
                    eng.wait_ge(half_used, value)
                else:
                    wait_filled(eng, value)
            elif g == PARTS - 1:
                wait_filled(eng, ("mh", 0), it)
            elif g < PARTS:
                eng.wait_ge(half_used, it * MOE_HALVES_COUNTED + (HALVES_COUNTED - (PARTS - 1) + g + 1))
            else:
                how, value = MOE_HALF_END[g - PARTS]
                if how == "count":
                    eng.wait_ge(half_used, it * MOE_HALVES_COUNTED + (HALVES_COUNTED + value))
                else:
                    wait_filled(eng, value, it)

        def last_half(kind, b, it=None):
            return (HALF_AT if it is None else MOE_HALF_AT)[(kind, b, 1)] + 1

        def ahead(kind, b, it=None):
            return min(last_half(kind, b, it) + PARTS, NHALF if it is None else NMOE_HALF)

        LHS_USES = {("h", 0): 0, ("o", 0): 1, ("h", 1): 2, ("h", 2): 3, ("o", 2): 4}

        def lhs_count(use, pairs):
            return 4 * LHS_USES[use] + pairs

        def row3(ap, n):
            return ap.unsqueeze(1).to_broadcast([P, n, ap.shape[1]])

        def col3(ap, n):
            return ap.unsqueeze(2).to_broadcast([P, ap.shape[1], n])

        block = ctx.enter_context(nc.Block())

        @block.sync
        def _(sp):
            def wide_source(w, n, h):
                return w.rearrange("(k p) n -> p k n", p=P)[:, 4 * h:4 * h + 4, n * N:(n + 1) * N]

            def long_source(w, n):
                return w.rearrange("(k p) n -> p k n", p=P)[:, 2 * n:2 * n + 2, :]

            def source(kind, n, h):
                if kind == "ada":
                    layer, block_n = ADA[n]
                    return wide_source(I["ada_w"][layer], block_n, h)
                if kind == "fd":
                    return long_source(I["even_ffn_w_down"][0], 2 * n + h)
                w = {"ein": "even_w_in", "eout": "even_w_out", "fg": "even_ffn_w_gate", "fu": "even_ffn_w_up",
                     "oin": "odd_w_in", "oout": "odd_w_out"}[kind]
                return wide_source(I[w][0], n, h)

            def target(n, kind):
                return long(slot(n)) if kind[1:] == "d" else wide(slot(n))

            def wait_slot(n):
                kind, b, h = STREAM[n]
                if kind == "ada":
                    sp.wait_ge(ada_step, 8 * b + 4 * h + 4)
                else:
                    wait_parts(sp, HALF_AT[STREAM[n]] + 1)

            for n, (kind, b, h) in enumerate(STREAM):
                if n >= RING:
                    wait_slot(n - RING)
                sp.dma_start(target(n, kind), source(kind, b, h)).then_inc(slot_loaded[slot(n)], 16)

            def expert_tiles(e, it, before):
                for n, (kind, b, h) in enumerate(MOE):
                    m = NSTREAM + n
                    if n >= RING:
                        wait_parts(sp, 2 * (n - RING) + 1, it)
                    elif before is None:
                        wait_slot(m - RING)
                    else:
                        wait_parts(sp, 2 * (NMOE + n - RING) + 1, before)
                    w = I[{"mg": "odd_moe_w_gate", "mu": "odd_moe_w_up", "md": "odd_moe_w_down"}[kind]]
                    w = w[0][bass.ds(e, 1), :, :].rearrange("a r c -> (a r) c")
                    src = long_source(w, 2 * b + h) if kind == "md" else wide_source(w, b, h)
                    sp.dma_start(target(m, kind), src).then_inc(slot_loaded[slot(m)], 16)

            expert_tiles(0, 0, None)
            with sp.Fori(1, NE) as i:
                expert_tiles(i, i, i - 1)
            sp.wait_ge(table_ready, 1)
            n_extra = sp.value_load(tabi[0:1, 0:1], min_val=0, max_val=EXTRA_MAX)
            with sp.If(n_extra > 0):
                with sp.Fori(0, n_extra) as i:
                    e = sp.value_load(tabi[0:1, bass.ds(i + 1, 1)], min_val=0, max_val=NE - 1)
                    expert_tiles(e, i + NE, i + (NE - 1))
            for t in range(NT):
                sp.wait_ge(x_ready, 4 * 3 + 2 * t + 2)
                sp.dma_start(out_dram[0, t * P:(t + 1) * P, :], x[:, t, :]).then_inc(out_done, 16)
            sp.wait_ge(out_done, 16 * NT)

        @block.tensor
        def _(pe):
            def three_passes(out, hi, lo, w, cols, start, stop):
                pe.matmul(out, hi, wh[:, w, cols], start=start, stop=False)
                pe.matmul(out, hi, wl[:, w, cols], start=False, stop=False)
                return pe.matmul(out, lo, wh[:, w, cols], start=False, stop=stop)

            def dense(names, tile, lhs, it=None):
                first_half = (HALF_AT if it is None else MOE_HALF_AT)[tile]
                for part in range(4):
                    g = first_half + part
                    wait_parts(pe, g, it)
                    for kk in range(2):
                        k = 2 * part + kk
                        for t, name in enumerate(names):
                            if k == 0:
                                wait_free(pe, name, it)
                            hi, lo = lhs(k, t)
                            mm = three_passes(bank(name, it)[:, :], hi, lo, g % PARTS, slice(kk * N, (kk + 1) * N), k == 0, k == KD - 1)
                            if k == KD - 1:
                                signal_filled(mm, name, it)
                    if part < 3:
                        mm.then_inc(half_used, 1)

            def down(name_of, b, tile, nt, it=None):
                first_half = (HALF_AT if it is None else MOE_HALF_AT)[tile]
                for f in range(4):
                    g = first_half + f
                    wait_parts(pe, g, it)
                    for t in range(nt):
                        for half in range(2):
                            first, last = b == 0 and f == 0, b == NB - 1 and f == 3
                            name = name_of(t, half)
                            if first:
                                wait_free(pe, name, it)
                            mm = three_passes(bank(name, it)[:, :], actTh[:, t, f, :], actTl[:, t, f, :], g % PARTS,
                                              slice(half * N, (half + 1) * N), first, last)
                            if last:
                                signal_filled(mm, name, it)
                    if not last:
                        mm.then_inc(half_used, 1)

            def transposes(name, sources, it=None):
                wait_free(pe, name, it)
                for i, src in enumerate(sources):
                    mm = pe.transpose(bank(name, it)[:, i * P:(i + 1) * P], src, ident)
                signal_filled(mm, name, it)

            def ada_reduce(j):
                layer, n = ADA[j]
                pe.wait_ge(ada_step, 8 * (j + 1))
                name = ("ada", j)
                wait_free(pe, name)
                a = acc[:, j % ACC_RING, :]
                if n // 2 in (2, 5):
                    mm = pe.matmul(bank(name)[:, :], ones, a, start=True, stop=True)
                else:
                    for c in range(4):
                        mm = pe.matmul(bank(name)[:, c:c + 1], a[:, c * P:(c + 1) * P], ones[:, 0:1], start=True, stop=True)
                signal_filled(mm, name)

            def transpose_h(w):
                for j in range(4):
                    pe.wait_ge(xn_ready, NT * (w + 1))
                    transposes(("ht", w, j), [xn[:, t, c * P:(c + 1) * P] for c in (2 * j, 2 * j + 1) for t in range(NT)])

            def h_tile(k, t):
                return hT[:, k, t * P:(t + 1) * P]

            def lhs_tile(k, t):
                return LH[:, k, t * P:(t + 1) * P], LL[:, k, t * P:(t + 1) * P]

            def wait_lhs(use):
                pe.wait_ge(lhs_lo, lhs_count(use, 4))

            pe.wait_ge(const_in, 16)
            pe.wait_ge(rows_in, 96)
            transposes(("cols", 0), [rowsA[:, :]])
            signal_filled(pe.transpose(bank(("cols", 1))[:, 0:ROWSB], rowsB[0:ROWSB, :], ident[0:ROWSB, 0:ROWSB]), ("cols", 1))
            for j in range(4):
                ada_reduce(j)
            transpose_h(0)

            wait_lhs(("h", 0))
            for n in range(4):
                dense([("ein", n, t) for t in range(NT)], ("ein", n, 0), lhs_tile)
                for j in {1: [4], 2: [5, 6], 3: [7, 8, 9]}.get(n, []):
                    ada_reduce(j)
            pe.wait_ge(poolw_in, 32)
            for g in range(POOLG):
                if g == 0:
                    for t in range(NT):
                        wait_emptied(pe, ("ein", 3, t))
                u = [proj[:, t, 3 * N + g * P:3 * N + (g + 1) * P] for t in range(NT)]
                name = ("pool", g)
                wait_free(pe, name)
                pe.matmul(bank(name)[:, 0:TOK], u[0], poolc[:, g, 0:TOK], start=True, stop=False)
                mm = pe.matmul(bank(name)[:, P:TOK], u[1], poolc[:, g, TOK:3 * P], start=False, stop=True)
                signal_filled(mm, name)
                wait_emptied(pe, name)
                name = ("mix", g)
                wait_free(pe, name)
                signal_filled(pe.matmul(bank(name)[:, 0:TOK], poolw[:, g, :], pooled[:, g % 2, :], start=True, stop=True), name)
            pe.wait_ge(roped, NT)
            for j in range(4):
                transposes(("qkt", j), [proj[:, t, c * P:(c + 1) * P] for c in (2 * j, 2 * j + 1) for t in range(NT)])
            for j in range(4):
                wait_emptied(pe, ("qkt", j))

            def scores(h):
                lo = HD * (h % 2)
                q, k = qkT[lo:lo + HD, h // 2, :], qkT[lo:lo + HD, 4 + h // 2, :]
                name = ("score", h)
                wait_free(pe, name)
                pe.matmul(bank(name)[:, 0:P], q[:, 0:P], k[:, 0:P], start=True, stop=True)
                signal_filled(pe.matmul(bank(name)[:, P:3 * P], q[:, P:TOK], k[:, 0:TOK], start=True, stop=True), name)

            def weigh_values(pair):
                name = ("pv", pair)
                wait_free(pe, name)
                for h in (2 * pair, 2 * pair + 1):
                    wait_emptied(pe, ("pt", h))
                    lo = HD * (h % 2)
                    v = [proj[:, t, 2 * N + h * HD:2 * N + (h + 1) * HD] for t in range(NT)]
                    pe.matmul(bank(name)[lo:lo + HD, 0:TOK], v[0], pT[:, h % 4, 0:TOK], start=True, stop=False)
                    mm = pe.matmul(bank(name)[lo:lo + HD, P:TOK], v[1], pT[:, h % 4, TOK:3 * P], start=False, stop=True)
                signal_filled(mm, name)

            for h in range(HEADS + 2):
                if h < HEADS:
                    scores(h)
                if 1 <= h <= HEADS:
                    pe.wait_ge(normed, h)
                    transposes(("pt", h - 1), [prob[:, (h - 1) % 2, i * P:(i + 1) * P] for i in range(3)])
                if h >= 2 and h % 2 == 1:
                    weigh_values((h - 2) // 2)
            for g in range(POOLG):
                wait_emptied(pe, ("mix", g))
            wait_lhs(("o", 0))
            for n in range(2):
                dense([("y", 0, t, n) for t in range(NT)], ("eout", n, 0), lhs_tile)

            transpose_h(1)
            wait_lhs(("h", 1))
            def turn_inner(b, t):
                wait_emptied(pe, ("fu", b, t))
                transposes(("ft", b, t), [act_n[:, t, f * P:(f + 1) * P] for f in range(4)])

            for b in range(NB + 1):
                if b:
                    ada_reduce(8 + 2 * b)
                if b < NB:
                    dense([("fg", b, t) for t in range(NT)], ("fg", b, 0), lhs_tile)
                if b:
                    turn_inner(b - 1, 0)
                    ada_reduce(9 + 2 * b)
                if b < NB:
                    dense([("fu", b, t) for t in range(NT)], ("fu", b, 0), lhs_tile)
                if b:
                    turn_inner(b - 1, 1)
                    for t in range(NT):
                        wait_emptied(pe, ("ft", b - 1, t))
                    down(lambda t, half: ("y", 1, t, half), b - 1, ("fd", b - 1, 0), NT)

            transpose_h(2)
            for j in range(4):
                wait_emptied(pe, ("ht", 2, j))
            pe.wait_ge(odd_in, 80)
            wait_free(pe, ("ba",))
            for t in range(NT):
                for k in range(KD):
                    mm = pe.matmul(bank(("ba",))[:, 16 * t:16 * t + 16], h_tile(k, t), ba_w[:, k, :], start=(k == 0), stop=(k == KD - 1))
            signal_filled(mm, ("ba",))
            pe.wait_ge(ba_dve, 9)
            wait_free(pe, ("gc",))
            for c in range(2):
                pe.matmul(bank(("gc",))[:, 8 * c:8 * c + 8], const("upto"), gdec[:, 8 * c:8 * c + 8], start=True, stop=True)
            signal_filled(pe.matmul(bank(("gc",))[:, 16:24], const("after"), gdec[:, 0:8], start=True, stop=True), ("gc",))

            wait_lhs(("h", 2))

            def project(g, r):
                n = 2 * r + g
                dense([("oin", g, r, t) for t in range(NT)], ("oin", n, 0), lhs_tile)

            def turn(g, r):
                for t in range(NT):
                    wait_emptied(pe, ("oin", g, r, t))
                for j in range(2):
                    transposes(("rt", g, r, j), [nat[:, t, c * P:(c + 1) * P] for c in (2 * j, 2 * j + 1) for t in range(NT)])

            def per_head(name, lhsT, rhs):
                wait_free(pe, name)
                for h in range(4):
                    mm = pe.matmul(bank(name)[:, h * P:(h + 1) * P], lhsT(h), rhs(h), start=True, stop=True)
                signal_filled(mm, name)

            for g in range(ODD_GROUPS):
                project(g, 0)
                project(g, 1)
                turn(g, 0)
                project(g, 2)
                turn(g, 1)
                turn(g, 2)
                q, k, v = (qkvT[:, r] for r in range(3))
                for r in range(2):
                    pe.wait_ge(sq_ready, 2 * g + r + 1)
                    name = ("ss", g, r)
                    wait_free(pe, name)
                    for i in range(8):
                        mm = pe.matmul(bank(name)[:, i:i + 1], sq[:, i % 4, (i // 4) * P:(i // 4 + 1) * P], ones[:, 0:1], start=True, stop=True)
                    signal_filled(mm, name)
                for c in range(2):
                    pe.wait_ge(rhs_ready, 4 * g + c + 1)
                    name = ("decay", g, c)
                    wait_free(pe, name)
                    signal_filled(pe.matmul(bank(name)[:, :], const("after"), Y[:, c].rearrange("p h n -> p (h n)"), start=True, stop=True), name)
                for c in range(2):
                    pe.wait_ge(rhs_ready, 4 * g + 2 + c + 1)
                    name = ("brow", g, c)
                    wait_free(pe, name)
                    signal_filled(pe.matmul(bank(name)[:, :], ones, CT[:, c].rearrange("p h n -> p (h n)"), start=True, stop=True), name)
                pe.wait_ge(silu_ready, 3 * g + 3)
                for c in range(2):
                    cc = slice(c * P, (c + 1) * P)
                    per_head(("kk", g, c), lambda h: k[:, h, cc], lambda h: k[:, h, cc])
                for c in range(2):
                    cc = slice(c * P, (c + 1) * P)
                    per_head(("kq", g, c), lambda h: k[:, h, cc], lambda h: q[:, h, cc])
                for c in range(2):
                    transposes(("vn", g, c), [v[:, h, c * P:(c + 1) * P] for h in range(4)])
                transposes(("kn", g), [k[:, h, 0:P] for h in range(4)])
                for c in range(2):
                    pe.wait_ge(u_ready, 2 * g + c + 1)
                    transposes(("x0", g, c), [U[:, c, h, :] for h in range(4)])
                for s in range(1, 7):
                    for c in range(2):
                        pe.wait_ge(ct_ready, 12 * g + 2 * (s - 1) + c + 1)
                        if s == 1:
                            wait_emptied(pe, ("x0", g, c))
                        else:
                            wait_emptied(pe, ("dX", g, s - 1, c))
                        per_head(("Y", g, s, c), lambda h: CT[:, c, h, :], lambda h: X[:, c, h, :])
                    for c in range(2):
                        wait_emptied(pe, ("Y", g, s, c))
                        if s > 1:
                            wait_emptied(pe, ("dU", g, s - 1, c))
                        if s < 6:
                            per_head(("dX", g, s, c), lambda h: U[:, c, h, :], lambda h: Y[:, c, h, :])
                        per_head(("dU", g, s, c), lambda h: Y[:, c, h, :], lambda h: U[:, c, h, :])
                for c in range(2):
                    wait_emptied(pe, ("dU", g, 6, c))
                    wait_emptied(pe, ("vn", g, c))
                wait_emptied(pe, ("kn", g))
                per_head(("u0", g), lambda h: U[:, 0, h, :], lambda h: vb[:, 0, h, :])
                wait_emptied(pe, ("u0", g))
                per_head(("S1", g), lambda h: kg0[:, h, :], lambda h: u0[:, h, :])
                wait_emptied(pe, ("S1", g))
                per_head(("kS", g), lambda h: k[:, h, P:TOK], lambda h: S1[:, h, :])
                pe.wait_ge(r_ready, g + 1)
                per_head(("v1", g), lambda h: U[:, 1, h, :], lambda h: r1[:, h, :])
                per_head(("o0", g), lambda h: attnT[:, 0, h, :], lambda h: u0[:, h, :])
                per_head(("qS", g), lambda h: q[:, h, P:TOK], lambda h: S1[:, h, :])
                wait_emptied(pe, ("v1", g))
                per_head(("o1", g), lambda h: attnT[:, 1, h, :], lambda h: v1[:, h, :])
            for n in range(2):
                dense([("gate", n, t) for t in range(NT)], ("oin", 6 + n, 0), lhs_tile)
            pe.wait_ge(o_ready, NT)
            for j in range(4):
                transposes(("ot", j), [xn[:, t, c * P:(c + 1) * P] for c in (2 * j, 2 * j + 1) for t in range(NT)])
            wait_lhs(("o", 2))
            for n in range(2):
                dense([("y", 2, t, n) for t in range(NT)], ("oout", n, 0), lhs_tile)

            transpose_h(3)
            for j in range(4):
                wait_emptied(pe, ("ht", 3, j))
            wait_free(pe, ("route",))
            for t in range(NT):
                for k in range(KD):
                    mm = pe.matmul(bank(("route",))[:, 8 * t:8 * t + 8], h_tile(k, t), router[:, k, :], start=(k == 0), stop=(k == KD - 1))
            signal_filled(mm, ("route",))
            pe.wait_ge(sel_ready, NT)
            wait_free(pe, ("slot",))
            b = bank(("slot",))
            pe.matmul(b[:, 0:8], const("before"), sel[:, 0, :], start=True, stop=True)
            pe.matmul(b[:, 8:16], const("before"), sel[:, 1, :], start=True, stop=False)
            pe.matmul(b[:, 8:16], ones, sel[:, 0, :], start=False, stop=True)
            pe.matmul(b[:, 16:24], ones, sel[:, 0, :], start=True, stop=False)
            signal_filled(pe.matmul(b[:, 16:24], ones, sel[:, 1, :], start=False, stop=True), ("slot",))

            def expert(it):
                pe.wait_ge(place_ready, it * 4 + 4)
                for j in range(2):
                    name = ("mh", j)
                    wait_free(pe, name, it)
                    for cc in range(4):
                        c = 4 * j + cc
                        for t in range(NT):
                            mm = pe.matmul(bank(name, it)[:, cc * P:(cc + 1) * P], xn[:, t, c * P:(c + 1) * P], place[:, t, :],
                                           start=(t == 0), stop=(t == NT - 1))
                    signal_filled(mm, name, it)
                transposes(("mp",), [placew[:, t, :] for t in range(NT)], it)
                pe.wait_ge(lhs_lo, it * 2 + (lhs_count(("o", 2), 4) + 2))
                for b in range(NB + 1):
                    if b < NB:
                        dense([("mg", b, 0)], ("mg", b, 0), lhs_tile, it)
                    if b:
                        wait_emptied(pe, ("mu", b - 1, 0), it)
                        transposes(("mt", b - 1, 0), [mact[:, 0, f * P:(f + 1) * P] for f in range(4)], it)
                    if b < NB:
                        dense([("mu", b, 0)], ("mu", b, 0), lhs_tile, it)
                    if b:
                        wait_emptied(pe, ("mt", b - 1, 0), it)
                        down(lambda t, half: ("my", half), b - 1, ("md", b - 1, 0), 1, it)
                wait_emptied(pe, ("mp",), it)
                for n in range(2):
                    wait_emptied(pe, ("my", n), it)
                for t in range(NT):
                    for n in range(2):
                        name = ("mo", t, n)
                        wait_free(pe, name, it)
                        signal_filled(pe.matmul(bank(name, it)[:, :], placeT[:, t, :], ye[:, n * N:(n + 1) * N], start=True, stop=True), name, it)

            pe.wait_ge(table_ready, 1)
            n_extra = pe.value_load(tabi[0:1, 0:1], min_val=0, max_val=EXTRA_MAX)
            with pe.Fori(0, NE) as i:
                expert(i)
            with pe.If(n_extra > 0):
                with pe.Fori(0, n_extra) as i:
                    expert(i + NE)

        @block.scalar
        def _(act):
            steps = [0]
            told = {}

            def tell(ins, signal):
                told[id(signal)] = told.get(id(signal), 0) + 1
                ins.then_inc(signal, 1)
                act.wait_ge(signal, told[id(signal)])

            def hand_over(ins, name, it=None):
                signal_emptied(ins, name, it)
                wait_emptied(act, name, it)

            def link(ins):
                steps[0] += 1
                ins.then_inc(act_step, 1)
                act.wait_ge(act_step, steps[0])

            def flat(ap):
                return ap.rearrange("a (r p) -> (a r) p", p=P)

            act.dma_start(consts[:, :], const_dram).then_inc(const_in, 16)
            act.dma_start(rowsA[0:96, :], flat(I["ada_b"])).then_inc(rows_in, 16)
            act.dma_start(rowsA[96:112, :], flat(I["mix_pre_g"])).then_inc(rows_in, 16)
            act.dma_start(rowsA[112:128, :], flat(I["ffn_pre_g"])).then_inc(rows_in, 16)
            act.dma_start(rowsB[0:8, :], flat(I["c"])).then_inc(rows_in, 16)
            act.dma_start(rowsB[8:104, :], flat(I["odd_conv_w"][0])).then_inc(rows_in, 16)
            act.dma_start(rowsB[104:108, :], flat(I["even_pool_scale"])).then_inc(rows_in, 16)
            act.dma_start(x[:, :, :], I["x"][0].rearrange("(t p) d -> p t d", p=P)).then_inc(x_in, 16)
            with nc.allow_non_contiguous_dma(reason="256 positions"):
                act.dma_start(posi[:, :], I["positions"][0].rearrange("(t p) -> p t", p=P)).then_inc(pos_in, 16)
            act.dma_start(poolw[:, :, :], I["even_pool_w"][0].rearrange("g c d -> c g d")).then_inc(poolw_in, 16)
            act.dma_start(poolc[:, :, :], pool_dram.rearrange("g p n -> p g n")).then_inc(poolw_in, 16)
            act.dma_start(ba_w[:, :, :], I["odd_w_in"][0].rearrange("(k p) n -> p k n", p=P)[:, :, 4 * D:4 * D + 16]).then_inc(odd_in, 16)
            act.dma_start(router[:, :, :], I["odd_router_w"][0].rearrange("(k p) n -> p k n", p=P)).then_inc(odd_in, 16)
            act.dma_start(alog[:, :], I["odd_a_log"][0].partition_broadcast(P)).then_inc(odd_in, 16)
            act.dma_start(dtb[:, :], I["odd_dt_bias"][0].partition_broadcast(P)).then_inc(odd_in, 16)
            act.dma_start(normg[:, :], I["odd_norm_g"][0].partition_broadcast(P)).then_inc(odd_in, 16)

            split_at = [0]

            def split_until(end, it=None):
                for g in range(split_at[0], end):
                    w, n = half_of_tile(g, it)
                    wait_tile(act, n, it)
                    wait_parts_free(act, g, it)
                    act.activation(wh[:, g % PARTS, :], w, ACT.Copy).then_inc(hi_ready, 1)
                split_at[0] = end

            def split_lhs(src, name_of):
                for j in range(4):
                    wait_emptied(act, name_of(j))
                    act.activation(LH[:, 2 * j:2 * j + 2, :].rearrange("p c t -> p (c t)"), src[:, 2 * j:2 * j + 2, :].rearrange("p c t -> p (c t)"),
                                   ACT.Copy).then_inc(lhs_hi, 1)

            def square_sums(w):
                if w == 0:
                    act.wait_ge(x_in, 16)
                for t in range(NT):
                    if w:
                        act.wait_ge(x_ready, 4 * (w - 1) + 2 * t + 2)
                    tell(act.activation(xn[:, t, :], x[:, t, :], ACT.Square, accum_out=ss[:, w, t:t + 1]), ss_ready)

            def modulate_even(w):
                for j in (0, 2):
                    name = ("ht", w, j)
                    wait_filled(act, name)
                    for cc in range(2):
                        c = 2 * j + cc
                        ins = act.activation(hT[:, c, :], bank(name)[:, cc * TOK:(cc + 1) * TOK], ACT.Identity,
                                             bias=shift[:, w, c:c + 1], scale=gain[:, w, c:c + 1])
                    hand_over(ins, name)

            def y_square_sums(w):
                for t in range(NT):
                    for n in range(2):
                        wait_filled(act, ("y", w, t, n))
                        tell(act.activation(xn[:, t, n * N:(n + 1) * N], bank(("y", w, t, n))[:, :], ACT.Square,
                             accum_out=ssy[:, w, t, n:n + 1]), ssy_ready)

            def copy_out(name, out, it=None, width=N, func=ACT.Copy):
                wait_filled(act, name, it)
                hand_over(act.activation(out, bank(name, it)[:, 0:width], func), name, it)

            copy_out(("cols", 1), colB[:, 0:ROWSB], width=ROWSB)
            wait_emptied(act, ("cols", 1))
            tell(act.activation(csil[:, :], colB[:, 0:KD], ACT.Silu), csil_ready)
            square_sums(0)
            act.wait_ge(trig_arg, 1)
            tell(act.activation(cs, rope_r, ACT.Sin), trig_ready)
            modulate_even(0)
            split_lhs(hT, lambda j: ("ht", 0, j))

            for n in range(4):
                split_until(ahead("ein", n))
                for t in range(NT):
                    copy_out(("ein", n, t), proj[:, t, n * N:(n + 1) * N])
            for g in range(POOLG):
                copy_out(("pool", g), pooled[:, g % 2, :], width=TOK)
                name = ("mix", g)
                wait_filled(act, name)
                hand_over(act.activation(oT[:, 4 + g, :], bank(name)[:, 0:TOK], ACT.Copy, scale=colB[:, 104 + g:105 + g]), name)
            for j in (0, 2):
                copy_out(("qkt", j), qkT[:, 2 * j:2 * j + 2, :].rearrange("p c t -> p (c t)"))
            for h in range(HEADS + 2):
                if h < HEADS:
                    act.wait_ge(maxed, h + 1)
                    for i, (a, b) in enumerate(((0, P), (P, 3 * P))):
                        tell(act.activation(prob[:, h % 2, a:b], sL[:, h % 2, a:b], ACT.Exp, bias=nmax[:, h, i:i + 1],
                             accum_out=den[:, h, i:i + 1]), exped)
                if 1 <= h <= HEADS:
                    copy_out(("pt", h - 1), pT[:, (h - 1) % 4, :], width=3 * P)
                if h >= 2 and h % 2 == 1:
                    pair = (h - 2) // 2
                    copy_out(("pv", pair), oT[:, pair, :], width=TOK)
            split_lhs(oT, lambda j: ("pv", 2 * j + 1) if j < 2 else ("mix", 2 * j - 3))
            split_until(ahead("eout", 1))
            y_square_sums(0)

            square_sums(1)
            modulate_even(1)
            split_lhs(hT, lambda j: ("ht", 1, j))
            for b in range(NB + 1):
                if b < NB:
                    split_until(ahead("fg", b))
                    for t in range(NT):
                        wait_filled(act, ("fg", b, t))
                        ins = act.activation(sil[:, t, :], bank(("fg", b, t))[:, :], ACT.Silu)
                        hand_over(ins, ("fg", b, t))
                else:
                    split_until(ahead("fd", NB - 2))
                if b:
                    for t in range(NT):
                        name = ("ft", b - 1, t)
                        if b < NB and t == 1:
                            split_until(ahead("fu", b))
                        wait_filled(act, name)
                        if b > 1 and t == 0:
                            act.wait_ge(half_used, HALF_END[HALF_AT[("fd", b - 2, 1)] + 1][1])
                        act.activation(actTh[:, t, :, :].rearrange("p f n -> p (f n)"), bank(name)[:, :], ACT.Copy).then_inc(act_hi, 1)
            split_until(ahead("fd", NB - 1))
            y_square_sums(1)

            square_sums(2)
            modulate_even(2)
            split_lhs(hT, lambda j: ("ht", 2, j))
            act.wait_ge(ba_dve, 4)
            tell(act.activation(bt[0], bt[0], ACT.Exp), ba_act)
            act.wait_ge(odd_in, 80)
            tell(act.activation(bt[3][:, 0:8], alog[:, :], ACT.Exp), ba_act)
            tell(act.activation(bt[1], bt[1], ACT.Exp), ba_act)
            tell(act.activation(bt[1], bt[1], ACT.Ln, bias=1.0), ba_act)
            name = ("gc",)
            wait_filled(act, name)
            hand_over(act.activation(eg, bank(name)[:, 0:24], ACT.Exp), name)
            for g in range(ODD_GROUPS):
                def natural(r):
                    split_until(ahead("oin", 2 * r + g))
                    for t in range(NT):
                        name = ("oin", g, r, t)
                        wait_filled(act, name)
                        if r:
                            wait_filled(act, ("rt", g, r - 1, 1))
                        hand_over(act.activation(nat[:, t, :], bank(name)[:, :], ACT.Copy), name)

                def activate(r):
                    act.wait_ge(conv_ready, 3 * g + r + 1)
                    tell(act.activation(qkvT[:, r].rearrange("p h t -> p (h t)"), conv[:, :, :].rearrange("p h t -> p (h t)"), ACT.Silu), silu_ready)
                    if r < 2:
                        act.wait_ge(silu_ready, 3 * g + r + 1)
                        if r == 1:
                            wait_filled(act, ("ss", g, 0))
                        tell(act.activation(sq[:, :, :].rearrange("p h t -> p (h t)"), qkvT[:, r].rearrange("p h t -> p (h t)"), ACT.Square), sq_ready)

                natural(0)
                natural(1)
                activate(0)
                natural(2)
                activate(1)
                activate(2)
                for c in range(2):
                    wait_emptied(act, ("decay", g, c))
                    e = ET[:, c].rearrange("p h n -> p (h n)")
                    tell(act.activation(e, e, ACT.Exp), et_act)
                for s in range(1, 7):
                    for c in range(2):
                        copy_out(("Y", g, s, c), Y[:, c].rearrange("p h n -> p (h n)"))
                copy_out(("u0", g), u0.rearrange("p h n -> p (h n)"))
                copy_out(("S1", g), S1.rearrange("p h n -> p (h n)"))
                copy_out(("v1", g), v1.rearrange("p h n -> p (h n)"))
                copy_out(("o0", g), xn[:, 0, g * N:(g + 1) * N])
            for n in range(2):
                split_until(ahead("oin", 6 + n))
                for t in range(NT):
                    copy_out(("gate", n, t), sgate[:, t, n * N:(n + 1) * N], func=ACT.Silu)
            for j in (0, 2):
                copy_out(("ot", j), hT[:, 2 * j:2 * j + 2, :].rearrange("p c t -> p (c t)"))
            split_lhs(hT, lambda j: ("ot", j))
            split_until(NHALF)
            y_square_sums(2)

            square_sums(3)
            modulate_even(3)
            act.wait_ge(route_arg, 1)
            tell(act.activation(pexp[:, 1, :], pexp[:, 0, :], ACT.Exp), route_exp)

            def expert(it):
                split_at[0] = 0
                split_until(PARTS, it)
                name = ("mh", 0)
                wait_filled(act, name, it)
                for cc in range(4):
                    ins = act.activation(heT[:, cc, :], bank(name, it)[:, cc * P:(cc + 1) * P], ACT.Identity,
                                         bias=shift[:, 3, cc:cc + 1], scale=gain[:, 3, cc:cc + 1])
                hand_over(ins, name, it)
                for j in range(2):
                    wait_emptied(act, ("mh", j), it)
                    act.activation(LH[:, 4 * j:4 * j + 4, 0:P], heT[:, 4 * j:4 * j + 4, :], ACT.Copy).then_inc(lhs_hi, 1)
                copy_out(("mp",), placeT[:, :, :].rearrange("p t n -> p (t n)"), it, width=TOK)
                for b in range(NB + 1):
                    if b < NB:
                        split_until(ahead("mg", b, it), it)
                        wait_filled(act, ("mg", b, 0), it)
                        if b:
                            wait_emptied(act, ("mu", b - 1, 0), it)
                        hand_over(act.activation(msil[:, 0, :], bank(("mg", b, 0), it)[:, :], ACT.Silu), ("mg", b, 0), it)
                    else:
                        split_until(ahead("md", NB - 2, it), it)
                    if b:
                        name = ("mt", b - 1, 0)
                        wait_filled(act, name, it)
                        if b > 1:
                            act.wait_ge(half_used, it * MOE_HALVES_COUNTED + (HALVES_COUNTED + MOE_HALF_END[MOE_HALF_AT[("md", b - 2, 1)] + 1][1]))
                        act.activation(actTh[:, 0, :, :].rearrange("p f n -> p (f n)"), bank(name, it)[:, :], ACT.Copy).then_inc(act_hi, 1)
                split_until(NMOE_HALF, it)
                copy_out(("my", 0), ye[:, 0:N], it)

            act.wait_ge(table_ready, 1)
            n_extra = act.value_load(tabi[0:1, 0:1], min_val=0, max_val=EXTRA_MAX)
            with act.Fori(0, NE) as i:
                expert(i)
            with act.If(n_extra > 0):
                with act.Fori(0, n_extra) as i:
                    expert(i + NE)
            for t in range(NT):
                act.wait_ge(mo_ready, t + 1)
                tell(act.activation(xn[:, t, :], yout[:, t, :], ACT.Square, accum_out=ssy[:, 3, t, 0:1]), ssy_ready)

        @block.gpsimd
        def _(pool):
            steps = [0]
            told = {}

            def tell(ins, signal):
                told[id(signal)] = told.get(id(signal), 0) + 1
                ins.then_inc(signal, 1)
                pool.wait_ge(signal, told[id(signal)])

            def hand_over(ins, name, it=None):
                signal_emptied(ins, name, it)
                wait_emptied(pool, name, it)

            def link(ins):
                steps[0] += 1
                ins.then_inc(pool_step, 1)
                pool.wait_ge(pool_step, steps[0])

            link(pool.memset(half_neg[:, :], -0.5))

            def x_rstd(w):
                pool.wait_ge(ss_ready, NT * (w + 1))
                link(pool.tensor_scalar(rstd[:, w, :], ss[:, w, :], 1.0 / D, EPS, ALU.mult, ALU.add))
                tell(pool.tensor_tensor(rstd[:, w, :], rstd[:, w, :], half_neg[:, 0:NT], ALU.pow), rstd_ready)

            def y_rstd(w):
                pool.wait_ge(ssy_ready, 4 * w + (2 if w == 3 else 4))
                if w < 3:
                    link(pool.tensor_tensor(rstdy[:, w, :], ssy[:, w, :, 0], ssy[:, w, :, 1], ALU.add))
                    link(pool.tensor_scalar(rstdy[:, w, :], rstdy[:, w, :], 1.0 / D, EPS, ALU.mult, ALU.add))
                else:
                    link(pool.tensor_scalar(rstdy[:, w, :], ssy[:, w, :, 0], 1.0 / D, EPS, ALU.mult, ALU.add))
                tell(pool.tensor_tensor(rstdy[:, w, :], rstdy[:, w, :], half_neg[:, 0:NT], ALU.pow), rstdy_ready)

            def load_gate_rows(w):
                if w:
                    pool.wait_ge(gate_row_ready, 2 * w)
                pool.dma_start(grow[:, :], I["mix_post_g" if w % 2 == 0 else "ffn_post_g"][w // 2].partition_broadcast(P)).then_inc(grow_in, 16)
                if w >= A_RING:
                    pool.wait_ge(x_ready, 4 * (w - A_RING + 1))
                part = 2 if w % 2 == 0 else 5
                pool.dma_start(A[:, w % A_RING, :], I["ada_b"][w // 2, part * D:(part + 1) * D].partition_broadcast(P)).then_inc(abias_in, 16)

            load_gate_rows(0)
            x_rstd(0)
            load_gate_rows(1)
            y_rstd(0)
            x_rstd(1)
            load_gate_rows(2)
            load_gate_rows(3)
            y_rstd(1)
            x_rstd(2)
            for g in range(ODD_GROUPS):
                for r in range(2):
                    wait_emptied(pool, ("ss", g, r))
                    tell(pool.tensor_tensor(rqk[:, r, :], ssqk[:, r, :], half_neg[:, 0:8], ALU.pow), rqk_ready)
                for s in range(1, 7):
                    for c in range(2):
                        if s == 1:
                            wait_emptied(pool, ("kk", g, c))
                        else:
                            wait_filled(pool, ("Y", g, s - 1, c))
                        tell(pool.tensor_tensor(CT[:, c], LT[:, c], row3(const("level", s * P, P), 4), ALU.mult), ct_ready)
            pool.wait_ge(fo_arg, 1)
            tell(pool.tensor_tensor(fo.rearrange("p c h -> p (c h)"), fo.rearrange("p c h -> p (c h)"), half_neg[:, :], ALU.pow), fo_ready)
            y_rstd(2)
            x_rstd(3)
            y_rstd(3)

        @block.vector
        def _(dve):
            steps = [0]
            told = {}

            def tell(ins, signal):
                told[id(signal)] = told.get(id(signal), 0) + 1
                ins.then_inc(signal, 1)
                dve.wait_ge(signal, told[id(signal)])

            def hand_over(ins, name, it=None):
                signal_emptied(ins, name, it)
                wait_emptied(dve, name, it)

            def link(ins):
                steps[0] += 1
                ins.then_inc(dve_step, 1)
                dve.wait_ge(dve_step, steps[0])

            tt, ts, stt = dve.tensor_tensor, dve.tensor_scalar, dve.scalar_tensor_tensor

            def copy_out(name, out, it=None, width=N):
                wait_filled(dve, name, it)
                hand_over(dve.tensor_copy(out, bank(name, it)[:, 0:width]), name, it)

            def ada_sum(j):
                if j >= ACC_RING:
                    wait_filled(dve, ("ada", j - ACC_RING))
                a = acc[:, j % ACC_RING, :]
                for k in range(KD):
                    n = AT[("ada", j, k // 4)]
                    if k % 4 == 0:
                        wait_tile(dve, n)
                    w = wide(slot(n))[:, k % 4, :]
                    if k == 0:
                        ins = ts(a, w, csil[:, 0:1], None, ALU.mult)
                    else:
                        dve.wait_ge(ada_step, 8 * j + k)
                        ins = stt(out=a, in0=w, scalar=csil[:, k:k + 1], in1=a, op0=ALU.mult, op1=ALU.add)
                    ins.then_inc(ada_step, 1)

            def ada_take(j):
                layer, n = ADA[j]
                part, name = n // 2, ("ada", j)
                w = 2 * layer + (part >= 3)
                wait_filled(dve, name)
                if part in (2, 5):
                    dve.wait_ge(abias_in, 16 * (w + 1))
                    dve.wait_ge(grow_in, 16 * (w + 1))
                    a = A[:, w % A_RING, (n % 2) * N:(n % 2 + 1) * N]
                    hand_over(tt(a, a, bank(name)[:, :], ALU.add), name)
                    tell(tt(a, a, grow[:, (n % 2) * N:(n % 2 + 1) * N], ALU.mult), gate_row_ready)
                    return
                bias = colA[:, 48 * layer + 4 * n:48 * layer + 4 * n + 4]
                lo = 4 * (n % 2)
                if part in (0, 3):
                    hand_over(tt(shift[:, w, lo:lo + 4], bank(name)[:, 0:4], bias, ALU.add), name)
                else:
                    hand_over(tt(mod_tmp[:, :], bank(name)[:, 0:4], bias, ALU.add), name)
                    g = (96 if part == 1 else 112) + 8 * layer + lo
                    link(stt(out=gain[:, w, lo:lo + 4], in0=mod_tmp[:, :], scalar=1.0, in1=colA[:, g:g + 4], op0=ALU.add, op1=ALU.mult))

            stream_at, split_at, taken = [0], [0], [0]

            def take_until(j):
                for i in range(taken[0], j):
                    ada_take(i)
                taken[0] = max(taken[0], j)

            def split_half(g, it=None):
                w, n = half_of_tile(g, it)
                s = g % PARTS
                dve.wait_ge(hi_ready, g + 1 if it is None else it * NMOE_HALF + (NHALF + g + 1))
                wait_tile(dve, n, it)
                tt(wl[:, s, :], w, wh[:, s, :].bitcast(F32), ALU.subtract).then_inc(lo_ready, 1)

            def advance(end):
                while split_at[0] < end or (end == NHALF and stream_at[0] < NSTREAM):
                    kind, b, h = STREAM[stream_at[0]]
                    if kind == "ada":
                        take_until(b - 1)
                        ada_sum(b)
                        stream_at[0] += 2
                    else:
                        g = split_at[0]
                        split_half(g)
                        split_at[0] += 1
                        stream_at[0] += g % 2

            def split_lhs(src, use):
                for j in range(4):
                    dve.wait_ge(lhs_hi, lhs_count(use, j + 1))
                    out, value, hi = (a[:, 2 * j:2 * j + 2, :] for a in (LL, src, LH))
                    tt(out, value, hi.bitcast(F32), ALU.subtract).then_inc(lhs_lo, 1)

            def norm_x(w):
                dve.wait_ge(rstd_ready, w + 1)
                for t in range(NT):
                    tell(ts(xn[:, t, :], x[:, t, :], rstd[:, w, t:t + 1], None, ALU.mult), xn_ready)

            def modulate_odd(w):
                for j in (1, 3):
                    name = ("ht", w, j)
                    wait_filled(dve, name)
                    for cc in range(2):
                        c = 2 * j + cc
                        ins = ts(hT[:, c, :], bank(name)[:, cc * TOK:(cc + 1) * TOK], gain[:, w, c:c + 1], shift[:, w, c:c + 1], ALU.mult, ALU.add)
                    hand_over(ins, name)

            def add_y(w):
                dve.wait_ge(rstdy_ready, w + 1)
                for t in range(NT):
                    for n in range(2):
                        cols = slice(n * N, (n + 1) * N)
                        if w < 3:
                            name = ("y", w, t, n)
                            ins = stt(out=xn[:, t, cols], in0=bank(name)[:, :], scalar=rstdy[:, w, t:t + 1], in1=A[:, w % A_RING, cols], op0=ALU.mult, op1=ALU.mult)
                            hand_over(ins, name)
                        else:
                            link(stt(out=xn[:, t, cols], in0=yout[:, t, cols], scalar=rstdy[:, w, t:t + 1], in1=A[:, w % A_RING, cols], op0=ALU.mult, op1=ALU.mult))
                        tell(tt(x[:, t, cols], x[:, t, cols], xn[:, t, cols], ALU.add), x_ready)

            copy_out(("cols", 0), colA[:, :], width=P)
            dve.wait_ge(pos_in, 16)
            link(dve.tensor_copy(posf[:, :], posi[:, :]))
            ang, ang2 = rope_in[:, 0, :], rope_in[:, 1, :]
            for t in range(NT):
                for half in range(2):
                    at = half * NT * ROT + t * ROT
                    link(ts(ang[:, at:at + ROT], const("freq"), posf[:, t:t + 1], None, ALU.mult))
            link(stt(out=rope_n, in0=ang, scalar=0.15915494309189535, in1=const("phase"), op0=ALU.mult, op1=ALU.add))
            link(ts(rope_n, rope_n, MAGIC, None, ALU.add))
            link(ts(rope_n, rope_n, -MAGIC, None, ALU.add))
            link(stt(out=ang2, in0=rope_n, scalar=-TWO_PI_HI, in1=ang, op0=ALU.mult, op1=ALU.add))
            link(stt(out=ang2, in0=rope_n, scalar=-TWO_PI_LO, in1=ang2, op0=ALU.mult, op1=ALU.add))
            link(stt(out=ang2, in0=const("phase"), scalar=6.283185307179586, in1=ang2, op0=ALU.mult, op1=ALU.add))
            tell(ts(rope_r, ang2, 3.1415925, -3.1415925, ALU.min, ALU.max), trig_arg)
            dve.wait_ge(csil_ready, 1)
            wait_emptied(dve, ("cols", 0))
            for j in range(4):
                take_until(j - 1)
                ada_sum(j)
            stream_at[0] = 8
            take_until(4)
            dve.wait_ge(x_in, 16)
            norm_x(0)
            modulate_odd(0)
            split_lhs(hT, ("h", 0))

            advance(ahead("ein", 1))
            for n in range(2):
                for t in range(NT):
                    wait_emptied(dve, ("ein", n, t))
            dve.wait_ge(trig_ready, 1)

            def rope(t):
                qk = proj[:, t, 0:2 * N].rearrange("p (h d) -> p h d", d=HD)
                x1, x2 = qk[:, :, 0:ROT], qk[:, :, ROT:2 * ROT]
                sin = row3(cs[:, t * ROT:(t + 1) * ROT], 16)
                cos = row3(cs[:, (NT + t) * ROT:(NT + t + 1) * ROT], 16)
                tt(rope_t[:, 0], x1, cos, ALU.mult)
                tt(rope_t[:, 1], x2, sin, ALU.mult)
                tt(rope_t[:, 2], x2, cos, ALU.mult)
                link(tt(rope_t[:, 3], x1, sin, ALU.mult))
                link(tt(x1, rope_t[:, 0], rope_t[:, 1], ALU.subtract))
                tell(tt(x2, rope_t[:, 2], rope_t[:, 3], ALU.add), roped)

            for t in range(NT):
                rope(t)
            advance(ahead("ein", 3))
            take_until(10)
            for j in (1, 3):
                copy_out(("qkt", j), qkT[:, 2 * j:2 * j + 2, :].rearrange("p c t -> p (c t)"))
            for h in range(HEADS + 1):
                if h < HEADS:
                    name = ("score", h)
                    wait_filled(dve, name)
                    s = sL[:, h % 2, :]
                    ins = stt(out=s, in0=bank(name)[:, 0:3 * P], scalar=HD ** -0.5, in1=const("mask"), op0=ALU.mult, op1=ALU.add)
                    hand_over(ins, name)
                    link(dve.tensor_reduce(nmax[:, h, 0:1], s[:, 0:P], AX.X, ALU.max, negate=True))
                    tell(dve.tensor_reduce(nmax[:, h, 1:2], s[:, P:3 * P], AX.X, ALU.max, negate=True), maxed)
                if h:
                    g = h - 1
                    dve.wait_ge(exped, 2 * h)
                    link(dve.reciprocal(rden[:, g, :], den[:, g, :]))
                    link(ts(prob[:, g % 2, 0:P], prob[:, g % 2, 0:P], rden[:, g, 0:1], None, ALU.mult))
                    tell(ts(prob[:, g % 2, P:3 * P], prob[:, g % 2, P:3 * P], rden[:, g, 1:2], None, ALU.mult), normed)
            split_lhs(oT, ("o", 0))
            advance(ahead("eout", 1))
            add_y(0)

            norm_x(1)
            modulate_odd(1)
            split_lhs(hT, ("h", 1))

            def split_inner(b, t):
                name = ("ft", b, t)
                dve.wait_ge(act_hi, NT * b + t + 1)
                wait_filled(dve, name)
                ins = tt(actTl[:, t, :, :].rearrange("p f n -> p (f n)"), bank(name)[:, :], actTh[:, t, :, :].rearrange("p f n -> p (f n)").bitcast(F32), ALU.subtract)
                signal_emptied(ins, name)

            for b in range(NB):
                advance(ahead("fg", b))
                if b:
                    split_inner(b - 1, 0)
                advance(ahead("fu", b))
                if b:
                    split_inner(b - 1, 1)
                for t in range(NT):
                    name = ("fu", b, t)
                    wait_emptied(dve, ("fg", b, t))
                    wait_filled(dve, name)
                    ins = tt(act_n[:, t, :], sil[:, t, :], bank(name)[:, :], ALU.mult)
                    hand_over(ins, name)
            advance(ahead("fd", NB - 2))
            take_until(23)
            for t in range(NT):
                split_inner(NB - 1, t)
            take_until(24)
            advance(ahead("fd", NB - 1))
            add_y(1)

            norm_x(2)
            modulate_odd(2)
            split_lhs(hT, ("h", 2))
            dve.wait_ge(odd_in, 80)
            name = ("ba",)
            wait_filled(dve, name)
            hand_over(dve.tensor_copy(ba.rearrange("p t n -> p (t n)"), bank(name)[:, 0:32]), name)

            def gate_step(ins):
                gate_n[0] += 1
                ins.then_inc(ba_dve, 1)
                dve.wait_ge(ba_dve, gate_n[0])

            gate_n = [0]
            z = bt[2].rearrange("p (t h) -> p t h", t=NT)
            gate_step(ts(bt[0].rearrange("p (t h) -> p t h", t=NT), ba[:, :, 0:8], -1.0, None, ALU.mult))
            gate_step(tt(z, ba[:, :, 8:16], row3(dtb[:, :], NT), ALU.add))
            gate_step(stt(out=bt[1], in0=bt[2], scalar=-1.0, in1=bt[2], op0=ALU.mult, op1=ALU.min))
            gate_step(ts(bt[2], bt[2], 0.0, None, ALU.max))
            dve.wait_ge(ba_act, 1)
            gate_step(ts(bt[0], bt[0], 1.0, None, ALU.add))
            gate_step(dve.reciprocal(beta, bt[0]))
            dve.wait_ge(ba_act, 4)
            gate_step(tt(gdec, bt[1], bt[2], ALU.add))
            g3 = gdec.rearrange("p (t h) -> p t h", t=NT)
            gate_step(tt(g3, g3, row3(bt[3][:, 0:8], NT), ALU.mult))
            gate_step(ts(gdec, gdec, -1.0, None, ALU.mult))
            wait_emptied(dve, ("gc",))
            for g in range(ODD_GROUPS):
                heads = slice(4 * g, 4 * g + 4)
                if g:
                    wait_filled(dve, ("o1", g - 1))
                link(dve.memset(raw[:, :, 0:3], 0.0))
                for r in range(3):
                    advance(ahead("oin", 2 * min(r + 1, 2) + g))
                    for j in range(2):
                        name = ("rt", g, r, j)
                        wait_filled(dve, name)
                        ins = dve.tensor_copy(raw[:, 2 * j:2 * j + 2, 3:3 + TOK], bank(name)[:, :].rearrange("p (h t) -> p h t", h=2))
                        hand_over(ins, name)
                    if 3 * g + r:
                        dve.wait_ge(silu_ready, 3 * g + r)
                    for w in range(CONVW):
                        for h in range(4):
                            col = colB[:, 8 + 24 * w + 8 * r + 4 * g + h:9 + 24 * w + 8 * r + 4 * g + h]
                            src = raw[:, h, w:w + TOK]
                            if w == 0:
                                ins = ts(conv[:, h, :], src, col, None, ALU.mult)
                            else:
                                ins = stt(out=conv[:, h, :], in0=src, scalar=col, in1=conv[:, h, :], op0=ALU.mult, op1=ALU.add)
                            if w == CONVW - 1 and h == 3:
                                tell(ins, conv_ready)
                            elif h == 3:
                                link(ins)
                dve.wait_ge(conv_ready, 3 * g + 3)
                dve.wait_ge(silu_ready, 3 * g + 3)
                for r in range(2):
                    name = ("ss", g, r)
                    wait_filled(dve, name)
                    hand_over(ts(ssqk[:, r, :], bank(name)[:, 0:8], EPS, None, ALU.add), name)
                for c in range(2):
                    gd = gdec[:, 8 * c + 4 * g:8 * c + 4 * g + 4]
                    tell(tt(Y[:, c], row3(const("upto"), 4), col3(gd, P), ALU.mult), rhs_ready)
                dve.wait_ge(rqk_ready, 2 * g + 2)
                rk = rqk[:, 1, :]
                for c in range(2):
                    link(tt(bk[:, 4 * c:4 * c + 4], rk[:, 4 * c:4 * c + 4], beta[:, 8 * c + 4 * g:8 * c + 4 * g + 4], ALU.mult))
                    link(ts(rsq[:, c, heads], rqk[:, 0, 4 * c:4 * c + 4], DH ** -0.5, None, ALU.mult))
                for c in range(2):
                    tell(tt(CT[:, c], row3(ident, 4), col3(bk[:, 4 * c:4 * c + 4], P), ALU.mult), rhs_ready)
                link(tt(kge, rk[:, 0:4], eg[:, 16 + 4 * g:20 + 4 * g], ALU.mult))
                link(tt(nbe, bk[:, 4:8], eg[:, 8 + 4 * g:12 + 4 * g], ALU.mult))
                for c in range(2):
                    name = ("decay", g, c)
                    wait_filled(dve, name)
                    ins = tt(ET[:, c], bank(name)[:, :].rearrange("p (h n) -> p h n", h=4), row3(const("neg"), 4), ALU.add)
                    hand_over(ins, name)
                for c in range(2):
                    name = ("brow", g, c)
                    wait_filled(dve, name)
                    dve.wait_ge(et_act, 2 * g + c + 1)
                    ins = tt(LT[:, c], ET[:, c], bank(name)[:, :].rearrange("p (h n) -> p h n", h=4), ALU.mult)
                    hand_over(ins, name)
                for c in range(2):
                    name = ("kk", g, c)
                    wait_filled(dve, name)
                    for h in range(4):
                        ins = stt(out=LT[:, c, h, :], in0=bank(name)[:, h * P:(h + 1) * P], scalar=rk[:, 4 * c + h:4 * c + h + 1], in1=LT[:, c, h, :],
                                  op0=ALU.mult, op1=ALU.mult)
                    hand_over(ins, name)
                    link(tt(U[:, c], LT[:, c], row3(const("level", 0, P), 4), ALU.mult))
                    tell(tt(U[:, c], row3(ident, 4), U[:, c], ALU.subtract), u_ready)
                for c in range(2):
                    name = ("kq", g, c)
                    wait_filled(dve, name)
                    for h in range(4):
                        ins = stt(out=attnT[:, c, h, :], in0=bank(name)[:, h * P:(h + 1) * P], scalar=rk[:, 4 * c + h:4 * c + h + 1], in1=ET[:, c, h, :],
                                  op0=ALU.mult, op1=ALU.mult)
                    hand_over(ins, name)
                for c in range(2):
                    name = ("vn", g, c)
                    wait_filled(dve, name)
                    ins = tt(vb[:, c], bank(name)[:, :].rearrange("p (h n) -> p h n", h=4), col3(beta[:, 8 * c + 4 * g:8 * c + 4 * g + 4], P), ALU.mult)
                    hand_over(ins, name)
                name = ("kn", g)
                wait_filled(dve, name)
                hand_over(tt(kg0, bank(name)[:, :].rearrange("p (h n) -> p h n", h=4), col3(kge, P), ALU.mult), name)
                for c in range(2):
                    copy_out(("x0", g, c), X[:, c].rearrange("p h n -> p (h n)"))
                for s in range(1, 7):
                    for c in range(2):
                        for what, M in (("dX", X), ("dU", U)):
                            if what == "dX" and s == 6:
                                continue
                            name = (what, g, s, c)
                            wait_filled(dve, name)
                            if s > 1:
                                wait_emptied(dve, (what, g, s - 1, c))
                            elif what == "dX":
                                wait_emptied(dve, ("x0", g, c))
                            else:
                                dve.wait_ge(u_ready, 2 * g + c + 1)
                            m = M[:, c].rearrange("p h n -> p (h n)")
                            hand_over(tt(m, m, bank(name)[:, :], ALU.subtract), name)
                name = ("kS", g)
                wait_filled(dve, name)
                hand_over(tt(r1, bank(name)[:, :].rearrange("p (h n) -> p h n", h=4), col3(nbe, P), ALU.mult), name)
                wait_emptied(dve, ("vn", g, 1))
                tell(tt(r1, vb[:, 1], r1, ALU.subtract), r_ready)
                name = ("qS", g)
                wait_filled(dve, name)
                hand_over(tt(qs, bank(name)[:, :].rearrange("p (h n) -> p h n", h=4), col3(eg[:, 8 + 4 * g:12 + 4 * g], P), ALU.mult), name)
                name = ("o1", g)
                wait_filled(dve, name)
                hand_over(tt(xn[:, 1, g * N:(g + 1) * N], qs.rearrange("p h n -> p (h n)"), bank(name)[:, :], ALU.add), name)
            advance(ahead("oin", 7))
            for g in range(ODD_GROUPS):
                wait_emptied(dve, ("o0", g))
            for t in range(NT):
                o = xn[:, t, :]
                o2 = scratch[:, 0:D]
                wait_filled(dve, ("o1", ODD_GROUPS - 1))
                link(tt(o2, o, o, ALU.mult))
                link(dve.tensor_reduce(sso[:, t, :], o2.rearrange("p (h n) -> p h n", n=DH), AX.X, ALU.add))
            link(tt(f1, rsq, rsq, ALU.mult))
            link(tt(f1, f1, sso, ALU.mult))
            tell(ts(fo, f1, 1.0 / DH, EPS, ALU.mult, ALU.add), fo_arg)
            dve.wait_ge(fo_ready, 1)
            link(tt(fo, fo, rsq, ALU.mult))
            for t in range(NT):
                o3 = xn[:, t, :].rearrange("p (h n) -> p h n", n=DH)
                link(tt(o3, o3, col3(fo[:, t, :], DH), ALU.mult))
                link(tt(o3, o3, row3(normg[:, :], HEADS), ALU.mult))
                for n in range(2):
                    wait_emptied(dve, ("gate", n, t))
                tell(tt(xn[:, t, :], xn[:, t, :], sgate[:, t, :], ALU.mult), o_ready)
            for j in (1, 3):
                copy_out(("ot", j), hT[:, 2 * j:2 * j + 2, :].rearrange("p c t -> p (c t)"))
            split_lhs(hT, ("o", 2))
            advance(NHALF)
            add_y(2)

            norm_x(3)
            modulate_odd(3)
            name = ("route",)
            wait_filled(dve, name)
            hand_over(dve.tensor_copy(logit.rearrange("p t e -> p (t e)"), bank(name)[:, 0:16]), name)
            for t in range(NT):
                link(dve.max(best[:, t, :], logit[:, t, :]))
                link(dve.max_index(besti[:, t, :], best[:, t, :], logit[:, t, :]))
            link(dve.tensor_copy(bestf, besti[:, :, :]))
            tell(tt(pexp[:, 0, :], best[:, :, 1], best[:, :, 0], ALU.subtract), route_arg)
            dve.wait_ge(route_exp, 1)
            link(ts(pexp[:, 2, :], pexp[:, 1, :], 1.0, None, ALU.add))
            link(dve.reciprocal(pexp[:, 3, :], pexp[:, 2, :]))
            link(tt(pexp[:, 4, :], pexp[:, 3, :], pexp[:, 1, :], ALU.mult))
            for t in range(NT):
                first, second = bestf[:, t, 0:1], bestf[:, t, 1:2]
                link(ts(sel[:, t, :], const("iota8"), first, None, ALU.is_equal))
                link(ts(comb[:, t, :], sel[:, t, :], pexp[:, 3, t:t + 1], None, ALU.mult))
                link(ts(rt[:, t, :], const("iota8"), second, None, ALU.is_equal))
                link(stt(out=comb[:, t, :], in0=rt[:, t, :], scalar=pexp[:, 4, t:t + 1], in1=comb[:, t, :], op0=ALU.mult, op1=ALU.add))
                tell(tt(sel[:, t, :], sel[:, t, :], rt[:, t, :], ALU.add), sel_ready)
            name = ("slot",)
            wait_filled(dve, name)
            hand_over(dve.tensor_copy(pos[:, :, :].rearrange("p t e -> p (t e)"), bank(name)[:, 0:24]), name)
            over, upto = table[:, 0, :], table[:, 1, :]
            link(ts(over, pos[:, 2, :], float(P), None, ALU.is_gt))
            link(dve.tensor_tensor_scan(upto, over, over, 0.0, ALU.add, ALU.max))
            link(dve.tensor_copy(tabf[:, 0:1], upto[:, NE - 1:NE]))
            for j in range(EXTRA_MAX):
                link(ts(match[:, j, :], upto, float(j + 1), None, ALU.is_equal))
                link(tt(match[:, j, :], match[:, j, :], over, ALU.mult))
                link(tt(match[:, j, :], match[:, j, :], const("iota8"), ALU.mult))
                link(dve.tensor_reduce(tabf[:, 1 + j:2 + j], match[:, j, :], AX.X, ALU.add))
            link(dve.memset(yout[:, :, :].rearrange("p t d -> p (t d)"), 0.0))
            tell(dve.tensor_copy(tabi[:, :], tabf[:, :]), table_ready)
            dve.wait_ge(table_ready, 1)

            def expert(it, e, first_slot):
                for t in range(NT):
                    at, on, weight = (a[:, t, bass.ds(e, 1)] for a in (pos, sel, comb))
                    slots = const("iota", first_slot, P)
                    ts(place[:, t, :], slots, at, on, ALU.is_equal, ALU.mult).then_inc(place_ready, 1)
                    ts(placew[:, t, :], slots, at, weight, ALU.is_equal, ALU.mult).then_inc(place_ready, 1)
                split_at[0] = 0

                def split_until(end):
                    for g in range(split_at[0], end):
                        split_half(g, it)
                    split_at[0] = end

                split_until(PARTS)
                name = ("mh", 1)
                wait_filled(dve, name, it)
                for cc in range(4):
                    c = 4 + cc
                    ins = ts(heT[:, c, :], bank(name, it)[:, cc * P:(cc + 1) * P], gain[:, 3, c:c + 1], shift[:, 3, c:c + 1], ALU.mult, ALU.add)
                hand_over(ins, name, it)
                for j in range(2):
                    dve.wait_ge(lhs_hi, it * 2 + (lhs_count(("o", 2), 4) + j + 1))
                    out, value, hi = LL[:, 4 * j:4 * j + 4, 0:P], heT[:, 4 * j:4 * j + 4, :], LH[:, 4 * j:4 * j + 4, 0:P]
                    tt(out, value, hi.bitcast(F32), ALU.subtract).then_inc(lhs_lo, 1)

                def split_inner(b):
                    name = ("mt", b, 0)
                    dve.wait_ge(act_hi, it * NB + (NT * NB + b + 1))
                    wait_filled(dve, name, it)
                    ins = tt(actTl[:, 0, :, :].rearrange("p f n -> p (f n)"), bank(name, it)[:, :], actTh[:, 0, :, :].rearrange("p f n -> p (f n)").bitcast(F32), ALU.subtract)
                    signal_emptied(ins, name, it)

                for b in range(NB):
                    if b:
                        split_until(ahead("mg", b, it))
                        split_inner(b - 1)
                    split_until(ahead("mu", b, it))
                    wait_emptied(dve, ("mg", b, 0), it)
                    wait_filled(dve, ("mu", b, 0), it)
                    ins = tt(mact[:, 0, :], msil[:, 0, :], bank(("mu", b, 0), it)[:, :], ALU.mult)
                    hand_over(ins, ("mu", b, 0), it)
                split_until(ahead("md", NB - 2, it))
                split_inner(NB - 1)
                split_until(NMOE_HALF)
                copy_out(("my", 1), ye[:, N:D], it)
                for t in range(NT):
                    for n in range(2):
                        name = ("mo", t, n)
                        wait_filled(dve, name, it)
                        y = yout[:, t, n * N:(n + 1) * N]
                        hand_over(tt(y, y, bank(name, it)[:, :], ALU.add), name, it)

            n_extra = dve.value_load(tabi[0:1, 0:1], min_val=0, max_val=EXTRA_MAX)
            with dve.Fori(0, NE) as i:
                expert(i, i, 0)
            with dve.If(n_extra > 0):
                with dve.Fori(0, n_extra) as i:
                    e = dve.value_load(tabi[0:1, bass.ds(i + 1, 1)], min_val=0, max_val=NE - 1)
                    expert(i + NE, e, P)
            dve.nop().then_inc(mo_ready, 1)
            dve.nop().then_inc(mo_ready, 1)
            add_y(3)


def kernel(**inputs):
    import numpy as np
    import concourse.bacc as bacc
    from concourse.bass_utils import run_bass_kernel_spmd

    nc = bacc.Bacc("TRN2", target_bir_lowering=False, num_devices=1)
    arrays, aps = {}, {}

    def give(name, a):
        arrays[name] = a
        return nc.dram_tensor(name, a.shape, mybir.dt.from_np(a.dtype), kind="ExternalInput").ap()

    for name in IN_NAMES:
        aps[name] = give(f"in_{name}", np.ascontiguousarray(inputs[name]))
    table, pool = constants(np)
    const_dram, pool_dram = give("in_constants", table), give("in_pool_windows", pool)
    out = nc.dram_tensor("out_x", (1, TOK, D), F32, kind="ExternalOutput").ap()
    build_trunk(nc, aps, const_dram, pool_dram, out)
    result = run_bass_kernel_spmd(nc, [arrays], core_ids=[0])
    return result.results[0]["out_x"]
```

```python
from contextlib import ExitStack

import concourse.bass as bass
from concourse import mybir

F32 = mybir.dt.float32
F32R = mybir.dt.float32r
I32 = mybir.dt.int32
U32 = mybir.dt.uint32
ALU = mybir.AluOpType
ACT = mybir.ActivationFunctionType
AX = mybir.AxisListType

P = 128
TOK = 256
NT = TOK // P
D = 1024
KD = D // P
N = 512
FFN = 3584
NB = FFN // N
HEADS = 8
HD = 64
ROT = 8
POOLG = 4
DH = 128
NE = 8
CONVW = 4
EPS = 1e-6
RING = 6
HALF = 1024
PARTS = 4
TILE = 2048
NEG = -1e30
MAGIC = 12582912.0
TWO_PI_HI = 6.28125
TWO_PI_LO = 0.0019353071795864769
ACC_RING = 2
A_RING = 3
ROWSB = 8 + 96 + 4
SCRATCH = 10240
EXTRA_MAX = 3

CONST = {}
_at = 0
for _name, _n in [("ident", P), ("ones", P), ("mask", 3 * P), ("upto", P), ("after", P), ("before", P),
                  ("neg", P), ("level", 7 * P), ("iota", 2 * P), ("iota8", 8), ("freq", ROT), ("phase", 2 * NT * ROT)]:
    CONST[_name] = (_at, _n)
    _at += _n
CONST_N = _at
FIRST_CONSTS = 2 * P


def constants(np):
    out = np.zeros((P, CONST_N), np.float32)

    def put(name, value):
        a, n = CONST[name]
        out[:, a:a + n] = value

    row, col = np.arange(P)[:, None], np.arange(P)[None, :]
    put("ident", row == col)
    put("ones", 1.0)
    i, j = np.arange(TOK)[:, None], np.arange(TOK)[None, :]
    count = ((i >= j) & (i - j <= 128)).astype(np.float64)
    for dilation in (4, 16):
        count += (i >= j) & ((i - j) % dilation == 0)
    log_count = np.where(count > 0, np.log(np.maximum(count, 1)), NEG)
    put("mask", np.concatenate([log_count[:P, :P], log_count[P:, :]], axis=1))
    put("upto", row <= col)
    put("after", row > col)
    put("before", row < col)
    put("neg", np.where(row <= col, 0.0, NEG))
    levels = [(col // (2 * s) == row // (2 * s)) & (col % (2 * s) >= s) & (row % (2 * s) < s)
              for s in (1, 2, 4, 8, 16, 32, 64)]
    put("level", np.concatenate(levels, axis=1))
    put("iota", np.arange(2 * P)[None, :])
    put("iota8", np.arange(8)[None, :])
    put("freq", (np.float32(500000.0) ** (-np.arange(0, 16, 2, dtype=np.float32) / np.float32(16)))[None, :])
    put("phase", np.repeat([0.0, 0.25], NT * ROT)[None, :])
    pool = np.zeros((POOLG, P, 3 * P), np.float32)
    for g, window in enumerate((2, 4, 8, 16)):
        t, s = np.arange(TOK)[None, :], np.arange(TOK)[:, None]
        w = ((t - s >= 0) & (t - s < window)) / np.minimum(t + 1, window) - (t == s)
        pool[g] = np.concatenate([w[:P, :], w[P:, P:]], axis=1)
    return out, pool


def ffn_tiles(kind, between):
    out, between = [], list(between)
    for b in range(NB):
        out += [(kind + "g", b, h) for h in range(2)]
        out += between[:2]
        out += [(kind + "u", b, h) for h in range(2)]
        out += [(kind + "d", b - 1, h) for h in range(2)] if b else []
        out += between[2:4]
        between = between[4:]
    return out + [(kind + "d", NB - 1, h) for h in range(2)]


def halves(kind, ns):
    return [(kind, n, h) for n in ns for h in range(2)]


ADA = [(0, n) for n in range(12)] + [(1, n) for n in range(12)]
ada_halves = [[("ada", j, h) for h in range(2)] for j in range(24)]
STREAM = sum(ada_halves[0:4], [])
for _kind, _n, _j in [("ein", 0, 4), ("ein", 1, 5), ("ein", 2, 6), ("ein", 3, 7), ("eout", 0, 8), ("eout", 1, 9)]:
    STREAM += halves(_kind, [_n]) + ada_halves[_j]
STREAM += ffn_tiles("f", sum(ada_halves[10:], []))
STREAM += halves("oin", [0, 2, 4, 6, 1, 3, 5, 7]) + halves("oout", [0, 1])
AT = {t: n for n, t in enumerate(STREAM)}
NSTREAM = len(STREAM)
MOE = ffn_tiles("m", [])
MOE_AT = {t: n for n, t in enumerate(MOE)}
NMOE = len(MOE)
assert NMOE % RING == 0 and len(AT) == NSTREAM

DENSE = [t for t in STREAM if t[0] != "ada"]
HALF_AT = {t: 2 * n for n, t in enumerate(DENSE)}
NHALF = 2 * len(DENSE)
MOE_HALF_AT = {t: 2 * n for n, t in enumerate(MOE)}
NMOE_HALF = 2 * NMOE
assert NHALF % PARTS == 0 and NMOE_HALF % PARTS == 0

ODD_GROUPS = 2


def static_banks():
    out = [(("cols", 0), 6), (("cols", 1), 7)]
    out += [(("ada", j), 7) for j in range(4)]
    out += [(("ht", 0, j), 4 + j % 4) for j in range(4)]
    for n in range(4):
        out += [(("ein", n, t), 2 * (n % 2) + t) for t in range(NT)]
        out += [(("ada", j), 7) for j in {1: [4], 2: [5], 3: [6]}.get(n, [])]
    out += [(("qkt", j), 2 + j) for j in range(4)]
    out += [(("score", 0), 0)]
    for h in range(HEADS + 2):
        if h + 1 < HEADS:
            out += [(("score", h + 1), (h + 1) % 2)]
        if h % 2 == 0 and h // 2 < POOLG:
            out += [(("pool", h // 2), 6)]
        if h % 2 == 1 and h // 2 < POOLG:
            out += [(("mix", h // 2), 7)]
        if 1 <= h <= HEADS:
            out += [(("pt", h - 1), 2 + (h - 1) % 2)]
        if h >= 2 and h % 2 == 1:
            out += [(("pv", (h - 2) // 2), 4 + (h - 2) // 2 % 2)]
    out += [(("ada", 7), 7)] + [(("y", 0, t, n), 2 * t + n) for n in range(2) for t in range(NT)] + [(("ada", j), 7) for j in (8, 9)]
    out += [(("ht", 1, j), 4 + j % 4) for j in range(4)]
    for b in range(NB + 1):
        if b:
            out += [(("ada", 8 + 2 * b), 7)]
        if b < NB:
            out += [(("fg", b, t), 4 + t) for t in range(NT)]
        if b:
            out += [(("ft", b - 1, 0), 6), (("ada", 9 + 2 * b), 7)]
        if b < NB:
            out += [(("fu", b, t), 4 + t) for t in range(NT)]
        if b:
            out += [(("ft", b - 1, 1), 6)]
        if b == 1:
            out += [(("y", 1, t, n), 2 * t + n) for t in range(NT) for n in range(2)]
    out += [(("ht", 2, j), 4 + j % 4) for j in range(4)]
    out += [(("ba",), 4)]
    for g in range(ODD_GROUPS):
        out += [(("oin", g, 0, t), t) for t in range(NT)] + [(("oin", g, 1, t), 4 + t) for t in range(NT)]
        out += [(("rt", g, 0, j), 2 + j) for j in range(2)] + [(("oin", g, 2, t), t) for t in range(NT)] + ([] if g else [(("gc",), 6)])
        out += [(("rt", g, 1, j), 2 + j) for j in range(2)] + [(("gate", g, t), 6 + t) for t in range(NT)]
        out += [(("rt", g, 2, j), 4 + j) for j in range(2)] + [(("ss", g, 0), 2), (("ss", g, 1), 3)]
        out += [(("decay", g, c), 4 + c) for c in range(2)] + [(("brow", g, c), 6 + c) for c in range(2)]
        out += [(("kk", g, c), 0 + c) for c in range(2)] + [(("kq", g, c), 2 + c) for c in range(2)]
        out += [(("vn", g, c), 4 + c) for c in range(2)] + [(("kn", g), 6)]
        out += [(("x0", g, c), 0 + c) for c in range(2)]
        for s in range(1, 7):
            out += [(("Y", g, s, c), 2 + c) for c in range(2)]
            if g == 1 and s == 5:
                out += [(("ot", j), j) for j in range(2)]
            for c in range(2):
                out += [(("dX", g, s, c), 4 + c)] if s < 6 else []
                out += [(("dU", g, s, c), 6 + c)]
        out += [(("u0", g), 0), (("S1", g), 1), (("kS", g), 2), (("v1", g), 3), (("o0", g), 4), (("qS", g), 5), (("o1", g), 6)]
    out += [(("ot", j), 2 + j) for j in (2, 3)]
    out += [(("y", 2, t, n), 2 * t + n) for n in range(2) for t in range(NT)]
    out += [(("ht", 3, j), 4 + j % 4) for j in range(4)]
    out += [(("route",), 4), (("slot",), 5), (("mh", 0), 6), (("mh", 1), 7)]
    return out


def moe_banks():
    out = []
    for b in range(NB + 1):
        if b < NB:
            out += [(("mg", b, 0), 2 + 2 * (b % 2))]
        if b:
            out += [(("mt", b - 1, 0), 6 + b % 2)]
        if b == 1:
            out += [(("mp",), 6)]
        if b == NB:
            out += [(("mh", 0), 4)]
        if b < NB:
            out += [(("mu", b, 0), 3 + 2 * (b % 2))]
        if b == 1:
            out += [(("my", n), n) for n in range(2)]
    out += [(("mh", 1), 5)]
    return out + [(("mo", t, n), 4 + 2 * t + n) for t in range(NT) for n in range(2)]


def ordinals(order):
    used, place = [0] * 8, {}
    for name, bank in order:
        assert name not in place
        place[name] = (bank, used[bank])
        used[bank] += 1
    return place, used


BANK, BANK_USES = ordinals(static_banks())
MOE_BANK, MOE_BANK_USES = ordinals(moe_banks())

def half_ends(tiles, name_of):
    out, n = [], 0
    for kind, b, h in tiles:
        for part in range(2):
            name = name_of(kind, b) if h == 1 and part == 1 else None
            n += name is None
            out.append(("bank", name) if name else ("count", n))
    return out, n


def last_product(kind, b):
    if kind == "fd":
        return ("y", 1, 1, 1) if b == NB - 1 else None
    if kind == "md":
        return ("my", 1) if b == NB - 1 else None
    return {"ein": ("ein", b, 1), "eout": ("y", 0, 1, b), "fg": ("fg", b, 1), "fu": ("fu", b, 1), "mg": ("mg", b, 0), "mu": ("mu", b, 0),
            "oin": ("oin", b % 2, b // 2, 1) if b < 6 else ("gate", b - 6, 1), "oout": ("y", 2, 1, b)}[kind]


HALF_END, HALVES_COUNTED = half_ends(DENSE, last_product)
MOE_HALF_END, MOE_HALVES_COUNTED = half_ends(MOE, last_product)
IN_NAMES = ["x", "c", "positions", "ada_w", "ada_b", "mix_pre_g", "mix_post_g", "ffn_pre_g", "ffn_post_g",
            "even_w_in", "even_pool_w", "even_pool_scale", "even_w_out", "even_ffn_w_gate", "even_ffn_w_up",
            "even_ffn_w_down", "odd_w_in", "odd_conv_w", "odd_a_log", "odd_dt_bias", "odd_norm_g", "odd_w_out",
            "odd_router_w", "odd_moe_w_gate", "odd_moe_w_up", "odd_moe_w_down"]


def build_trunk(nc, I, const_dram, pool_dram, out_dram):
    ctx = ExitStack()
    with ctx:
        def sb(name, shape, dt=F32):
            return ctx.enter_context(nc.sbuf_tensor(name, shape, dt))

        def sem(name):
            return ctx.enter_context(nc.semaphore(name))

        ps = [ctx.enter_context(nc.psum_tensor(f"bank{b}", [P, N], F32)) for b in range(8)]
        ring = sb("ring", [P, RING, TILE])
        x = sb("xres", [P, NT, D])
        xn = sb("xn", [P, NT, D])
        hT = sb("hT", [P, KD, TOK])
        A = sb("A", [P, A_RING, D])
        grow = sb("grow", [P, D])
        wh = sb("wh", [P, PARTS, HALF], F32R)
        wl = sb("wl", [P, PARTS, HALF], F32R)
        LH = sb("LH", [P, KD, TOK], F32R)
        LL = sb("LL", [P, KD, TOK], F32R)
        actTh = sb("actTh", [P, NT, 4, P], F32R)
        actTl = sb("actTl", [P, NT, 4, P], F32R)
        consts = sb("consts", [P, CONST_N])
        acc = sb("acc", [P, ACC_RING, N])
        rowsA = sb("rowsA", [P, P])
        rowsB = sb("rowsB", [P, P])
        colA = sb("colA", [P, P])
        colB = sb("colB", [P, P])
        csil = sb("csil", [P, KD])
        shift = sb("shift", [P, 4, KD])
        gain = sb("gain", [P, 4, KD])
        mod_tmp = sb("mod_tmp", [P, 4])
        ss = sb("ss", [P, 4, NT])
        rstd = sb("rstd", [P, 4, NT])
        ssy = sb("ssy", [P, 4, NT, 2])
        rstdy = sb("rstdy", [P, 4, NT])
        half_neg = sb("half_neg", [P, 16])
        posi = sb("posi", [P, NT], I32)
        posf = sb("posf", [P, NT])
        ba_w = sb("ba_w", [P, KD, 16])
        router = sb("router", [P, KD, NE])
        alog = sb("alog", [P, HEADS])
        dtb = sb("dtb", [P, HEADS])
        normg = sb("normg", [P, DH])
        scratch = sb("scratch", [P, SCRATCH])

        def view(at, *shape):
            n = 1
            for s in shape:
                n *= s
            assert at + n <= SCRATCH
            ap = scratch[:, at:at + n]
            if len(shape) == 2:
                return ap.rearrange("p (a b) -> p a b", a=shape[0])
            if len(shape) == 3:
                return ap.rearrange("p (a b c) -> p a b c", a=shape[0], b=shape[1])
            return ap

        def const(name, a=0, n=None):
            at, size = CONST[name]
            return consts[:, at + a:at + a + (size if n is None else n)]

        ident, ones = const("ident"), const("ones")

        proj = view(0, NT, 4 * N)
        qkT = view(4096, 8, TOK)
        sL = view(6144, 2, 384)
        pooled = view(9408, 2, TOK)
        prob = view(6912, 2, 384)
        poolc = A[:, 1:3, :].rearrange("p a b -> p (a b)")[:, 0:POOLG * 3 * P].rearrange("p (g n) -> p g n", g=POOLG)
        poolw = A[:, 1:3, :].rearrange("p a b -> p (a b)")[:, POOLG * 3 * P:POOLG * 4 * P].rearrange("p (g n) -> p g n", g=POOLG)
        pT = view(7680, 4, 384)
        rope_in = view(9216, 3, 32)
        rope_n = view(9312, 32)
        rope_r = view(9344, 32)
        cs = view(9376, 32)
        rope_t = view(9408, 4, 16, ROT)
        nmax = view(9920, HEADS, 2)
        den = view(9936, HEADS, 2)
        rden = view(9952, HEADS, 2)
        oT = hT
        sil = view(0, NT, N)
        act_n = view(1024, NT, N)
        qkvT = view(0, 3, 4, TOK)
        nat = view(3072, NT, N)
        raw = [view(at, 4, TOK + 4) for at in (4096, 7184)]
        conv = [view(at, 4, TOK) for at in (5136, 8224)]
        sq = view(6160, 4, TOK)
        X = view(3072, 2, 4, P)
        U = view(4096, 2, 4, P)
        Y = view(5120, 2, 4, P)
        CT = view(6144, 2, 4, P)
        LT = view(7168, 2, 4, P)
        attnT = view(8192, 2, 4, P)
        ET = view(9216, 2, 4, P)
        vb = qkvT[:, 2].rearrange("p h (c n) -> p c h n", c=2)
        kg0 = ET[:, 0]
        o2 = ET[:, 1].rearrange("p h n -> p (h n)")
        sgate = hT[:, :, :].rearrange("p c t -> p (c t)").rearrange("p (t d) -> p t d", t=NT)
        u0, S1 = X[:, 0], X[:, 1]
        r1, v1 = Y[:, 0], Y[:, 1]
        qs = CT[:, 0]
        small = sb("small", [P, 24, 16])
        ba, beta, gdec = small[:, 0:2, :], small[:, 2, :], small[:, 3, :]
        bt = [small[:, 4 + i, :] for i in range(4)]
        eg = small[:, 8:10, :].rearrange("p a b -> p (a b)")[:, 0:24]
        ssqk = small[:, 10, :].rearrange("p (r b) -> p r b", r=2)
        rqk = small[:, 11, :].rearrange("p (r b) -> p r b", r=2)
        bk = small[:, 12, 0:8]
        kge = small[:, 12, 8:12]
        nbe = small[:, 12, 12:16]
        rsq = small[:, 13, :].rearrange("p (c h) -> p c h", c=2)
        sso = small[:, 14, :].rearrange("p (c h) -> p c h", c=2)
        fo = small[:, 15, :].rearrange("p (c h) -> p c h", c=2)
        f1 = small[:, 16, :].rearrange("p (c h) -> p c h", c=2)
        logit = small[:, 17, :].rearrange("p (t e) -> p t e", t=NT)
        best = small[:, 18, :].rearrange("p (t e) -> p t e", t=NT)
        besti = sb("besti", [P, NT, 8], U32)
        bestf = small[:, 19, :].rearrange("p (t e) -> p t e", t=NT)
        pexp = small[:, 20, :].rearrange("p (k t) -> p k t", k=8)
        sel = small[:, 21, :].rearrange("p (t e) -> p t e", t=NT)
        comb = small[:, 22, :].rearrange("p (t e) -> p t e", t=NT)
        rt = small[:, 23, :].rearrange("p (t e) -> p t e", t=NT)
        pos = sb("pos", [P, 3, NE])
        table = sb("table", [P, 4, NE])
        match = sb("match", [P, EXTRA_MAX, NE])
        tabf = sb("tabf", [P, 5])
        tabi = sb("tabi", [P, 5], I32)
        heT = view(0, KD, P)
        place = view(1024, NT, P)
        placew = view(1280, NT, P)
        placeT = view(1536, NT, P)
        msil = view(1792, 1, N)
        mact = view(2304, 1, N)
        ye = view(3328, D)
        yout = view(4352, NT, D)

        slot_loaded = [sem(f"slot_loaded{s}") for s in range(RING)]
        hi_ready = sem("hi_ready")
        lo_ready = sem("lo_ready")
        half_used = sem("half_used")
        lhs_hi = sem("lhs_hi")
        lhs_lo = sem("lhs_lo")
        act_hi = sem("act_hi")
        gate_row_ready = sem("gate_row_ready")
        ada_step = sem("ada_step")
        filled = [sem(f"bank_filled{b}") for b in range(8)]
        emptied = [sem(f"bank_emptied{b}") for b in range(8)]
        const_in = sem("const_in")
        late_const_in = sem("late_const_in")
        rows_in = sem("rows_in")
        x_in = sem("x_in")
        pos_in = sem("pos_in")
        grow_in = sem("grow_in")
        abias_in = sem("abias_in")
        poolw_in = sem("poolw_in")
        odd_in = sem("odd_in")
        out_done = sem("out_done")
        csil_ready = sem("csil_ready")
        ss_ready = sem("ss_ready")
        rstd_ready = sem("rstd_ready")
        xn_ready = sem("xn_ready")
        ssy_ready = sem("ssy_ready")
        rstdy_ready = sem("rstdy_ready")
        x_ready = sem("x_ready")
        trig_arg = sem("trig_arg")
        trig_ready = sem("trig_ready")
        roped = sem("roped")
        maxed = sem("maxed")
        exped = sem("exped")
        normed = sem("normed")
        ba_dve = sem("ba_dve")
        ba_act = sem("ba_act")
        pad_ready = sem("pad_ready")
        tap_ready = sem("tap_ready")
        conv_ready = sem("conv_ready")
        silu_ready = sem("silu_ready")
        sq_ready = sem("sq_ready")
        rqk_ready = sem("rqk_ready")
        rhs_ready = sem("rhs_ready")
        et_act = sem("et_act")
        ct_ready = sem("ct_ready")
        u_ready = sem("u_ready")
        gate_scaled = sem("gate_scaled")
        fo_arg = sem("fo_arg")
        fo_ready = sem("fo_ready")
        r_ready = sem("r_ready")
        o_ready = sem("o_ready")
        route_arg = sem("route_arg")
        route_exp = sem("route_exp")
        sel_ready = sem("sel_ready")
        table_ready = sem("table_ready")
        dve_step = sem("dve_step")
        act_step = sem("act_step")
        pool_step = sem("pool_step")
        place_ready = sem("place_ready")
        mo_ready = sem("mo_ready")

        def use(name, it):
            if it is None:
                return BANK[name]
            bank, before = MOE_BANK[name]
            return bank, it * MOE_BANK_USES[bank] + (BANK_USES[bank] + before)

        def bank(name, it=None):
            return ps[use(name, it)[0]]

        def wait_free(pe, name, it=None):
            b, before = use(name, it)
            if it is not None or before:
                pe.wait_ge(emptied[b], before)

        def signal_filled(ins, name, it=None):
            ins.then_inc(filled[use(name, it)[0]], 1)

        def wait_filled(eng, name, it=None):
            b, before = use(name, it)
            eng.wait_ge(filled[b], before + 1)

        def signal_emptied(ins, name, it=None):
            ins.then_inc(emptied[use(name, it)[0]], 1)

        def wait_emptied(eng, name, it=None):
            b, before = use(name, it)
            eng.wait_ge(emptied[b], before + 1)

        def slot(n):
            return n % RING

        def wait_tile(eng, n, it=None):
            if it is None:
                eng.wait_ge(slot_loaded[n % RING], 16 * (n // RING + 1))
            else:
                m = NSTREAM + n
                eng.wait_ge(slot_loaded[m % RING], it * (16 * NMOE // RING) + 16 * (m // RING + 1))

        def wide(s):
            return ring[:, s, :].rearrange("p (k n) -> p k n", n=N)

        def long(s):
            return ring[:, s, :].rearrange("p (k n) -> p k n", n=D)

        def wait_parts(eng, g, it=None):
            if it is None:
                eng.wait_ge(lo_ready, g + 1)
            else:
                eng.wait_ge(lo_ready, it * NMOE_HALF + (NHALF + g + 1))

        def half_of_tile(g, it=None):
            tiles, at = (DENSE, AT) if it is None else (MOE, MOE_AT)
            n = at[tiles[g // 2]]
            s = slot(n if it is None else NSTREAM + n)
            return ring[:, s, (g % 2) * HALF:(g % 2 + 1) * HALF], n

        def wait_gathered(eng, it):
            eng.wait_ge(lhs_lo, it * 2 + (lhs_count(("o", 2), 4) + 2))

        def wait_parts_free(eng, g, it=None):
            if it is None:
                if g < PARTS:
                    return
                how, value = HALF_END[g - PARTS]
                if how == "count":
                    eng.wait_ge(half_used, value)
                else:
                    wait_filled(eng, value)
            elif g == PARTS - 1:
                wait_gathered(eng, it)
            elif g < PARTS:
                eng.wait_ge(half_used, it * MOE_HALVES_COUNTED + (HALVES_COUNTED - (PARTS - 1) + g + 1))
            else:
                how, value = MOE_HALF_END[g - PARTS]
                if how == "count":
                    eng.wait_ge(half_used, it * MOE_HALVES_COUNTED + (HALVES_COUNTED + value))
                else:
                    wait_filled(eng, value, it)

        def last_half(kind, b, it=None):
            return (HALF_AT if it is None else MOE_HALF_AT)[(kind, b, 1)] + 1

        def ahead(kind, b, it=None):
            return min(last_half(kind, b, it) + PARTS, NHALF if it is None else NMOE_HALF)

        def midway_ahead(kind, b):
            return last_half(kind, b) + 2 + PARTS

        LHS_USES = {("h", 0): 0, ("o", 0): 1, ("h", 1): 2, ("h", 2): 3, ("o", 2): 4}

        def lhs_count(use, pairs):
            return 4 * LHS_USES[use] + pairs

        def row3(ap, n):
            return ap.unsqueeze(1).to_broadcast([P, n, ap.shape[1]])

        def col3(ap, n):
            return ap.unsqueeze(2).to_broadcast([P, ap.shape[1], n])

        block = ctx.enter_context(nc.Block())

        @block.sync
        def _(sp):
            def wide_source(w, n, h):
                return w.rearrange("(k p) n -> p k n", p=P)[:, 4 * h:4 * h + 4, n * N:(n + 1) * N]

            def long_source(w, n):
                return w.rearrange("(k p) n -> p k n", p=P)[:, 2 * n:2 * n + 2, :]

            def source(kind, n, h):
                if kind == "ada":
                    layer, block_n = ADA[n]
                    return wide_source(I["ada_w"][layer], block_n, h)
                if kind == "fd":
                    return long_source(I["even_ffn_w_down"][0], 2 * n + h)
                w = {"ein": "even_w_in", "eout": "even_w_out", "fg": "even_ffn_w_gate", "fu": "even_ffn_w_up",
                     "oin": "odd_w_in", "oout": "odd_w_out"}[kind]
                return wide_source(I[w][0], n, h)

            def target(n, kind):
                return long(slot(n)) if kind[1:] == "d" else wide(slot(n))

            def wait_slot(n):
                kind, b, h = STREAM[n]
                if kind == "ada":
                    sp.wait_ge(ada_step, 8 * b + 4 * h + 4)
                else:
                    wait_parts(sp, HALF_AT[STREAM[n]] + 1)

            def flat(ap):
                return ap.rearrange("a (r p) -> (a r) p", p=P)

            sp.dma_start(rowsB[0:8, :], flat(I["c"])).then_inc(rows_in, 16)
            sp.dma_start(rowsB[8:104, :], flat(I["odd_conv_w"][0])).then_inc(rows_in, 16)
            sp.dma_start(rowsB[104:108, :], flat(I["even_pool_scale"])).then_inc(rows_in, 16)
            sp.dma_start(consts[:, 0:FIRST_CONSTS], const_dram[:, 0:FIRST_CONSTS]).then_inc(const_in, 16)
            sp.dma_start(rowsA[0:96, :], flat(I["ada_b"])).then_inc(rows_in, 16)
            sp.dma_start(rowsA[96:112, :], flat(I["mix_pre_g"])).then_inc(rows_in, 16)
            sp.dma_start(rowsA[112:128, :], flat(I["ffn_pre_g"])).then_inc(rows_in, 16)
            for n, (kind, b, h) in enumerate(STREAM):
                if n == 7:
                    sp.dma_start(x[:, :, :], I["x"][0].rearrange("(t p) d -> p t d", p=P)).then_inc(x_in, 16)
                if n >= RING:
                    wait_slot(n - RING)
                sp.dma_start(target(n, kind), source(kind, b, h)).then_inc(slot_loaded[slot(n)], 16)

            def expert_tiles(e, it, before):
                for n, (kind, b, h) in enumerate(MOE):
                    m = NSTREAM + n
                    if n >= RING:
                        wait_parts(sp, 2 * (n - RING) + 1, it)
                    elif before is None:
                        wait_slot(m - RING)
                    else:
                        wait_parts(sp, 2 * (NMOE + n - RING) + 1, before)
                    w = I[{"mg": "odd_moe_w_gate", "mu": "odd_moe_w_up", "md": "odd_moe_w_down"}[kind]]
                    w = w[0][bass.ds(e, 1), :, :].rearrange("a r c -> (a r) c")
                    src = long_source(w, 2 * b + h) if kind == "md" else wide_source(w, b, h)
                    sp.dma_start(target(m, kind), src).then_inc(slot_loaded[slot(m)], 16)

            expert_tiles(0, 0, None)
            with sp.Fori(1, NE) as i:
                expert_tiles(i, i, i - 1)
            sp.wait_ge(table_ready, 1)
            n_extra = sp.value_load(tabi[0:1, 0:1], min_val=0, max_val=EXTRA_MAX)
            with sp.If(n_extra > 0):
                with sp.Fori(0, n_extra) as i:
                    e = sp.value_load(tabi[0:1, bass.ds(i + 1, 1)], min_val=0, max_val=NE - 1)
                    expert_tiles(e, i + NE, i + (NE - 1))
            for t in range(NT):
                sp.wait_ge(x_ready, NT * 3 + t + 1)
                sp.dma_start(out_dram[0, t * P:(t + 1) * P, :], x[:, t, :]).then_inc(out_done, 16)
            sp.wait_ge(out_done, 16 * NT)

        @block.tensor
        def _(pe):
            def three_passes(out, hi, lo, w, cols, start, stop):
                pe.matmul(out, hi, wh[:, w, cols], start=start, stop=False)
                pe.matmul(out, hi, wl[:, w, cols], start=False, stop=False)
                return pe.matmul(out, lo, wh[:, w, cols], start=False, stop=stop)

            def dense(names, tile, lhs, it=None, use=None, midway=None):
                first_half = (HALF_AT if it is None else MOE_HALF_AT)[tile]
                for part in range(4):
                    g = first_half + part
                    wait_parts(pe, g, it)
                    if use is not None:
                        pe.wait_ge(lhs_lo, lhs_count(use, part + 1))
                    for kk in range(2):
                        k = 2 * part + kk
                        for t, name in enumerate(names):
                            if k == 0:
                                wait_free(pe, name, it)
                            hi, lo = lhs(k, t)
                            mm = three_passes(bank(name, it)[:, :], hi, lo, g % PARTS, slice(kk * N, (kk + 1) * N), k == 0, k == KD - 1)
                            if k == KD - 1:
                                signal_filled(mm, name, it)
                    if part < 3:
                        mm.then_inc(half_used, 1)
                    if part == 1 and midway is not None:
                        midway()

            def down(name_of, b, tile, nt, it=None):
                first_half = (HALF_AT if it is None else MOE_HALF_AT)[tile]
                for f in range(4):
                    g = first_half + f
                    wait_parts(pe, g, it)
                    for t in range(nt):
                        for half in range(2):
                            first, last = b == 0 and f == 0, b == NB - 1 and f == 3
                            name = name_of(t, half)
                            if first:
                                wait_free(pe, name, it)
                            mm = three_passes(bank(name, it)[:, :], actTh[:, t, f, :], actTl[:, t, f, :], g % PARTS,
                                              slice(half * N, (half + 1) * N), first, last)
                            if last:
                                signal_filled(mm, name, it)
                    if not last:
                        mm.then_inc(half_used, 1)

            def transposes(name, sources, it=None):
                wait_free(pe, name, it)
                for i, src in enumerate(sources):
                    mm = pe.transpose(bank(name, it)[:, i * P:(i + 1) * P], src, ident)
                signal_filled(mm, name, it)

            def ada_reduce(j):
                layer, n = ADA[j]
                pe.wait_ge(ada_step, 8 * (j + 1))
                name = ("ada", j)
                wait_free(pe, name)
                a = acc[:, j % ACC_RING, :]
                if n // 2 in (2, 5):
                    mm = pe.matmul(bank(name)[:, :], ones, a, start=True, stop=True)
                else:
                    for c in range(4):
                        mm = pe.matmul(bank(name)[:, c:c + 1], a[:, c * P:(c + 1) * P], ones[:, 0:1], start=True, stop=True)
                signal_filled(mm, name)

            def transpose_h(w):
                for j in range(4):
                    pe.wait_ge(xn_ready, NT * (w + 1))
                    transposes(("ht", w, j), [xn[:, t, c * P:(c + 1) * P] for c in (2 * j, 2 * j + 1) for t in range(NT)])

            def h_tile(k, t):
                return hT[:, k, t * P:(t + 1) * P]

            def lhs_tile(k, t):
                return LH[:, k, t * P:(t + 1) * P], LL[:, k, t * P:(t + 1) * P]


            pe.wait_ge(const_in, 16)
            pe.wait_ge(rows_in, 96)
            transposes(("cols", 0), [rowsA[:, :]])
            signal_filled(pe.transpose(bank(("cols", 1))[:, 0:ROWSB], rowsB[0:ROWSB, :], ident[0:ROWSB, 0:ROWSB]), ("cols", 1))
            for j in range(4):
                ada_reduce(j)
            transpose_h(0)

            for n in range(4):
                dense([("ein", n, t) for t in range(NT)], ("ein", n, 0), lhs_tile, use=("h", 0) if n == 0 else None)
                if n:
                    ada_reduce(3 + n)
            pe.wait_ge(roped, NT)
            for j in range(4):
                transposes(("qkt", j), [proj[:, t, c * P:(c + 1) * P] for c in (2 * j, 2 * j + 1) for t in range(NT)])
            for j in range(4):
                wait_emptied(pe, ("qkt", j))
            pe.wait_ge(late_const_in, 16)
            pe.wait_ge(poolw_in, 32)
            for t in range(NT):
                wait_emptied(pe, ("ein", 3, t))

            def pool_windows(g):
                u = [proj[:, t, 3 * N + g * P:3 * N + (g + 1) * P] for t in range(NT)]
                name = ("pool", g)
                wait_free(pe, name)
                pe.matmul(bank(name)[:, 0:TOK], u[0], poolc[:, g, 0:TOK], start=True, stop=False)
                mm = pe.matmul(bank(name)[:, P:TOK], u[1], poolc[:, g, TOK:3 * P], start=False, stop=True)
                signal_filled(mm, name)

            def mix_pooled(g):
                wait_emptied(pe, ("pool", g))
                name = ("mix", g)
                wait_free(pe, name)
                signal_filled(pe.matmul(bank(name)[:, 0:TOK], poolw[:, g, :], pooled[:, g % 2, :], start=True, stop=True), name)

            def scores(h):
                lo = HD * (h % 2)
                q, k = qkT[lo:lo + HD, h // 2, :], qkT[lo:lo + HD, 4 + h // 2, :]
                name = ("score", h)
                wait_free(pe, name)
                pe.matmul(bank(name)[:, 0:P], q[:, 0:P], k[:, 0:P], start=True, stop=True)
                signal_filled(pe.matmul(bank(name)[:, P:3 * P], q[:, P:TOK], k[:, 0:TOK], start=True, stop=True), name)

            def weigh_values(pair):
                name = ("pv", pair)
                wait_free(pe, name)
                for h in (2 * pair, 2 * pair + 1):
                    wait_emptied(pe, ("pt", h))
                    lo = HD * (h % 2)
                    v = [proj[:, t, 2 * N + h * HD:2 * N + (h + 1) * HD] for t in range(NT)]
                    pe.matmul(bank(name)[lo:lo + HD, 0:TOK], v[0], pT[:, h % 4, 0:TOK], start=True, stop=False)
                    mm = pe.matmul(bank(name)[lo:lo + HD, P:TOK], v[1], pT[:, h % 4, TOK:3 * P], start=False, stop=True)
                signal_filled(mm, name)

            scores(0)
            for h in range(HEADS + 2):
                if h + 1 < HEADS:
                    scores(h + 1)
                if h % 2 == 0 and h // 2 < POOLG:
                    pool_windows(h // 2)
                if h % 2 == 1 and h // 2 < POOLG:
                    mix_pooled(h // 2)
                if 1 <= h <= HEADS:
                    pe.wait_ge(normed, h)
                    transposes(("pt", h - 1), [prob[:, (h - 1) % 2, i * P:(i + 1) * P] for i in range(3)])
                if h >= 2 and h % 2 == 1:
                    weigh_values((h - 2) // 2)
            for g in range(POOLG):
                wait_emptied(pe, ("mix", g))
            for n in range(2):
                dense([("y", 0, t, n) for t in range(NT)], ("eout", n, 0), lhs_tile, use=("o", 0) if n == 0 else None)
                if n == 0:
                    ada_reduce(7)
            for j in (8, 9):
                ada_reduce(j)

            transpose_h(1)
            def turn_inner(b, t):
                wait_emptied(pe, ("fu", b, t))
                transposes(("ft", b, t), [act_n[:, t, f * P:(f + 1) * P] for f in range(4)])

            for b in range(NB + 1):
                if b:
                    ada_reduce(8 + 2 * b)
                if b < NB:
                    dense([("fg", b, t) for t in range(NT)], ("fg", b, 0), lhs_tile, use=("h", 1) if b == 0 else None)
                if b:
                    turn_inner(b - 1, 0)
                    ada_reduce(9 + 2 * b)
                if b < NB:
                    dense([("fu", b, t) for t in range(NT)], ("fu", b, 0), lhs_tile, midway=(lambda: turn_inner(b - 1, 1)) if b else None)
                if b:
                    if b == NB:
                        turn_inner(b - 1, 1)
                    for t in range(NT):
                        wait_emptied(pe, ("ft", b - 1, t))
                    down(lambda t, half: ("y", 1, t, half), b - 1, ("fd", b - 1, 0), NT)

            transpose_h(2)

            def gate_logits():
                for j in range(4):
                    wait_emptied(pe, ("ht", 2, j))
                pe.wait_ge(odd_in, 80)
                wait_free(pe, ("ba",))
                for t in range(NT):
                    for k in range(KD):
                        mm = pe.matmul(bank(("ba",))[:, 16 * t:16 * t + 16], h_tile(k, t), ba_w[:, k, :], start=(k == 0), stop=(k == KD - 1))
                signal_filled(mm, ("ba",))

            def decay_sums():
                pe.wait_ge(ba_dve, 9)
                wait_free(pe, ("gc",))
                for c in range(2):
                    pe.matmul(bank(("gc",))[:, 8 * c:8 * c + 8], const("upto"), gdec[:, 8 * c:8 * c + 8], start=True, stop=True)
                signal_filled(pe.matmul(bank(("gc",))[:, 16:24], const("after"), gdec[:, 0:8], start=True, stop=True), ("gc",))

            def project(g, r, midway=None):
                n = 2 * r + g
                names = [("oin", g, r, t) if r < 3 else ("gate", g, t) for t in range(NT)]
                dense(names, ("oin", n, 0), lhs_tile, use=("h", 2) if n == 0 else None, midway=midway)

            def turn(g, r):
                for t in range(NT):
                    wait_emptied(pe, ("oin", g, r, t))
                for j in range(2):
                    transposes(("rt", g, r, j), [nat[:, t, c * P:(c + 1) * P] for c in (2 * j, 2 * j + 1) for t in range(NT)])

            def per_head(name, lhsT, rhs):
                wait_free(pe, name)
                for h in range(4):
                    mm = pe.matmul(bank(name)[:, h * P:(h + 1) * P], lhsT(h), rhs(h), start=True, stop=True)
                signal_filled(mm, name)

            def turn_output(group):
                pe.wait_ge(o_ready, NT * (group + 1))
                for j in (2 * group, 2 * group + 1):
                    transposes(("ot", j), [xn[:, t, c * P:(c + 1) * P] for c in (2 * j, 2 * j + 1) for t in range(NT)])

            for g in range(ODD_GROUPS):
                project(g, 0, gate_logits if g == 0 else None)
                for r in range(1, 4):
                    project(g, r, lambda: turn(g, r - 1))
                    if g == 0 and r == 2:
                        decay_sums()
                q, k, v = (qkvT[:, r] for r in range(3))
                for r in range(2):
                    pe.wait_ge(sq_ready, 2 * g + r + 1)
                    name = ("ss", g, r)
                    wait_free(pe, name)
                    for i in range(8):
                        mm = pe.matmul(bank(name)[:, i:i + 1], sq[:, i % 4, (i // 4) * P:(i // 4 + 1) * P], ones[:, 0:1], start=True, stop=True)
                    signal_filled(mm, name)
                for c in range(2):
                    pe.wait_ge(rhs_ready, 4 * g + c + 1)
                    name = ("decay", g, c)
                    wait_free(pe, name)
                    signal_filled(pe.matmul(bank(name)[:, :], const("after"), Y[:, c].rearrange("p h n -> p (h n)"), start=True, stop=True), name)
                for c in range(2):
                    pe.wait_ge(rhs_ready, 4 * g + 2 + c + 1)
                    name = ("brow", g, c)
                    wait_free(pe, name)
                    signal_filled(pe.matmul(bank(name)[:, :], ones, CT[:, c].rearrange("p h n -> p (h n)"), start=True, stop=True), name)
                pe.wait_ge(silu_ready, 3 * g + 3)
                for c in range(2):
                    cc = slice(c * P, (c + 1) * P)
                    per_head(("kk", g, c), lambda h: k[:, h, cc], lambda h: k[:, h, cc])
                for c in range(2):
                    cc = slice(c * P, (c + 1) * P)
                    per_head(("kq", g, c), lambda h: k[:, h, cc], lambda h: q[:, h, cc])
                for c in range(2):
                    transposes(("vn", g, c), [v[:, h, c * P:(c + 1) * P] for h in range(4)])
                transposes(("kn", g), [k[:, h, 0:P] for h in range(4)])
                for c in range(2):
                    pe.wait_ge(u_ready, 2 * g + c + 1)
                    transposes(("x0", g, c), [U[:, c, h, :] for h in range(4)])
                for s in range(1, 7):
                    for c in range(2):
                        pe.wait_ge(ct_ready, 12 * g + 2 * (s - 1) + c + 1)
                        if s == 1:
                            wait_emptied(pe, ("x0", g, c))
                        else:
                            wait_emptied(pe, ("dX", g, s - 1, c))
                        per_head(("Y", g, s, c), lambda h: CT[:, c, h, :], lambda h: X[:, c, h, :])
                    if g == 1 and s == 5:
                        turn_output(0)
                    for c in range(2):
                        wait_emptied(pe, ("Y", g, s, c))
                        if s > 1:
                            wait_emptied(pe, ("dU", g, s - 1, c))
                        if s < 6:
                            per_head(("dX", g, s, c), lambda h: U[:, c, h, :], lambda h: Y[:, c, h, :])
                        per_head(("dU", g, s, c), lambda h: Y[:, c, h, :], lambda h: U[:, c, h, :])
                for c in range(2):
                    wait_emptied(pe, ("dU", g, 6, c))
                    wait_emptied(pe, ("vn", g, c))
                wait_emptied(pe, ("kn", g))
                per_head(("u0", g), lambda h: U[:, 0, h, :], lambda h: vb[:, 0, h, :])
                wait_emptied(pe, ("u0", g))
                per_head(("S1", g), lambda h: kg0[:, h, :], lambda h: u0[:, h, :])
                wait_emptied(pe, ("S1", g))
                per_head(("kS", g), lambda h: k[:, h, P:TOK], lambda h: S1[:, h, :])
                pe.wait_ge(r_ready, g + 1)
                per_head(("v1", g), lambda h: U[:, 1, h, :], lambda h: r1[:, h, :])
                per_head(("o0", g), lambda h: attnT[:, 0, h, :], lambda h: u0[:, h, :])
                per_head(("qS", g), lambda h: q[:, h, P:TOK], lambda h: S1[:, h, :])
                wait_emptied(pe, ("v1", g))
                per_head(("o1", g), lambda h: attnT[:, 1, h, :], lambda h: v1[:, h, :])
            turn_output(1)
            for n in range(2):
                dense([("y", 2, t, n) for t in range(NT)], ("oout", n, 0), lhs_tile, use=("o", 2) if n == 0 else None)

            transpose_h(3)
            for j in range(4):
                wait_emptied(pe, ("ht", 3, j))
            wait_free(pe, ("route",))
            for t in range(NT):
                for k in range(KD):
                    mm = pe.matmul(bank(("route",))[:, 8 * t:8 * t + 8], h_tile(k, t), router[:, k, :], start=(k == 0), stop=(k == KD - 1))
            signal_filled(mm, ("route",))
            pe.wait_ge(sel_ready, NT)
            wait_free(pe, ("slot",))
            b = bank(("slot",))
            pe.matmul(b[:, 0:8], const("before"), sel[:, 0, :], start=True, stop=True)
            pe.matmul(b[:, 8:16], const("before"), sel[:, 1, :], start=True, stop=False)
            pe.matmul(b[:, 8:16], ones, sel[:, 0, :], start=False, stop=True)
            pe.matmul(b[:, 16:24], ones, sel[:, 0, :], start=True, stop=False)
            signal_filled(pe.matmul(b[:, 16:24], ones, sel[:, 1, :], start=False, stop=True), ("slot",))

            def gather(j, it=None):
                name = ("mh", j)
                wait_free(pe, name, it)
                for cc in range(4):
                    c = 4 * j + cc
                    for t in range(NT):
                        mm = pe.matmul(bank(name, it)[:, cc * P:(cc + 1) * P], xn[:, t, c * P:(c + 1) * P], place[:, t, :],
                                       start=(t == 0), stop=(t == NT - 1))
                signal_filled(mm, name, it)

            def expert(it):
                wait_gathered(pe, it)
                for b in range(NB + 1):
                    if b < NB:
                        dense([("mg", b, 0)], ("mg", b, 0), lhs_tile, it)
                    if b:
                        wait_emptied(pe, ("mu", b - 1, 0), it)
                        transposes(("mt", b - 1, 0), [mact[:, 0, f * P:(f + 1) * P] for f in range(4)], it)
                    if b == 1:
                        transposes(("mp",), [placew[:, t, :] for t in range(NT)], it)
                    if b == NB:
                        pe.wait_ge(place_ready, it * 4 + 8)
                        gather(0, it)
                    if b < NB:
                        dense([("mu", b, 0)], ("mu", b, 0), lhs_tile, it)
                    if b:
                        wait_emptied(pe, ("mt", b - 1, 0), it)
                        down(lambda t, half: ("my", half), b - 1, ("md", b - 1, 0), 1, it)
                gather(1, it)
                wait_emptied(pe, ("mp",), it)
                for n in range(2):
                    wait_emptied(pe, ("my", n), it)
                for t in range(NT):
                    for n in range(2):
                        name = ("mo", t, n)
                        wait_free(pe, name, it)
                        signal_filled(pe.matmul(bank(name, it)[:, :], placeT[:, t, :], ye[:, n * N:(n + 1) * N], start=True, stop=True), name, it)

            pe.wait_ge(place_ready, 4)
            gather(0)
            gather(1)
            pe.wait_ge(table_ready, 1)
            n_extra = pe.value_load(tabi[0:1, 0:1], min_val=0, max_val=EXTRA_MAX)
            with pe.Fori(0, NE - 1) as i:
                expert(i)
            expert(NE - 1)
            with pe.If(n_extra > 0):
                with pe.Fori(0, n_extra) as i:
                    expert(i + NE)

        @block.scalar
        def _(act):
            steps = [0]
            told = {}

            def tell(ins, signal):
                told[id(signal)] = told.get(id(signal), 0) + 1
                ins.then_inc(signal, 1)
                act.wait_ge(signal, told[id(signal)])

            def hand_over(ins, name, it=None):
                signal_emptied(ins, name, it)
                wait_emptied(act, name, it)

            def link(ins):
                steps[0] += 1
                ins.then_inc(act_step, 1)
                act.wait_ge(act_step, steps[0])

            def later_loads():
                wait_tile(act, AT[("ada", 3, 0)])
                act.dma_start(consts[:, FIRST_CONSTS:], const_dram[:, FIRST_CONSTS:]).then_inc(late_const_in, 16)
                with nc.allow_non_contiguous_dma(reason="256 positions"):
                    act.dma_start(posi[:, :], I["positions"][0].rearrange("(t p) -> p t", p=P)).then_inc(pos_in, 16)
                act.dma_start(poolw[:, :, :], I["even_pool_w"][0].rearrange("g c d -> c g d")).then_inc(poolw_in, 16)
                act.dma_start(poolc[:, :, :], pool_dram.rearrange("g p n -> p g n")).then_inc(poolw_in, 16)
                act.dma_start(ba_w[:, :, :], I["odd_w_in"][0].rearrange("(k p) n -> p k n", p=P)[:, :, 4 * D:4 * D + 16]).then_inc(odd_in, 16)
                act.dma_start(router[:, :, :], I["odd_router_w"][0].rearrange("(k p) n -> p k n", p=P)).then_inc(odd_in, 16)
                act.dma_start(alog[:, :], I["odd_a_log"][0].partition_broadcast(P)).then_inc(odd_in, 16)
                act.dma_start(dtb[:, :], I["odd_dt_bias"][0].partition_broadcast(P)).then_inc(odd_in, 16)
                act.dma_start(normg[:, :], I["odd_norm_g"][0].partition_broadcast(P)).then_inc(odd_in, 16)

            split_at = [0]

            def split_until(end, it=None):
                for g in range(split_at[0], end):
                    w, n = half_of_tile(g, it)
                    wait_tile(act, n, it)
                    wait_parts_free(act, g, it)
                    act.activation(wh[:, g % PARTS, :], w, ACT.Copy).then_inc(hi_ready, 1)
                split_at[0] = end

            def split_pair(src, j, name):
                wait_emptied(act, name)
                act.activation(LH[:, 2 * j:2 * j + 2, :].rearrange("p c t -> p (c t)"), src[:, 2 * j:2 * j + 2, :].rearrange("p c t -> p (c t)"),
                               ACT.Copy).then_inc(lhs_hi, 1)

            def square_sums(w):
                if w == 0:
                    act.wait_ge(x_in, 16)
                for t in range(NT):
                    if w:
                        act.wait_ge(x_ready, NT * (w - 1) + t + 1)
                    tell(act.activation(xn[:, t, :], x[:, t, :], ACT.Square, accum_out=ss[:, w, t:t + 1]), ss_ready)

            def modulate(w):
                for j in range(4):
                    name = ("ht", w, j)
                    if j % 2 == 0:
                        wait_filled(act, name)
                        for cc in range(2):
                            c = 2 * j + cc
                            ins = act.activation(hT[:, c, :], bank(name)[:, cc * TOK:(cc + 1) * TOK], ACT.Identity,
                                                 bias=shift[:, w, c:c + 1], scale=gain[:, w, c:c + 1])
                        signal_emptied(ins, name)
                    if w < 3:
                        split_pair(hT, j, name)

            def y_square_sums(w):
                for t in range(NT):
                    for n in range(2):
                        wait_filled(act, ("y", w, t, n))
                        tell(act.activation(hT[:, 4 * t + 2 * n:4 * t + 2 * n + 2, :].rearrange("p c t -> p (c t)"), bank(("y", w, t, n))[:, :], ACT.Square,
                             accum_out=ssy[:, w, t, n:n + 1]), ssy_ready)

            def copy_out(name, out, it=None, width=N, func=ACT.Copy):
                wait_filled(act, name, it)
                hand_over(act.activation(out, bank(name, it)[:, 0:width], func), name, it)

            copy_out(("cols", 1), colB[:, 0:ROWSB], width=ROWSB)
            wait_emptied(act, ("cols", 1))
            tell(act.activation(csil[:, :], colB[:, 0:KD], ACT.Silu), csil_ready)
            later_loads()
            square_sums(0)
            modulate(0)

            for n in range(4):
                split_until(ahead("ein", n))
                for t in range(NT):
                    copy_out(("ein", n, t), proj[:, t, n * N:(n + 1) * N])
                if n == 1:
                    act.wait_ge(trig_arg, 1)
                    tell(act.activation(cs, rope_r, ACT.Sin), trig_ready)
            for j in range(4):
                copy_out(("qkt", j), qkT[:, 2 * j:2 * j + 2, :].rearrange("p c t -> p (c t)"))
            for h in range(HEADS + 2):
                if h < HEADS:
                    act.wait_ge(maxed, h + 1)
                    for i, (a, b) in enumerate(((0, P), (P, 3 * P))):
                        tell(act.activation(prob[:, h % 2, a:b], sL[:, h % 2, a:b], ACT.Exp, bias=nmax[:, h, i:i + 1],
                             accum_out=den[:, h, i:i + 1]), exped)
                if h % 2 == 0 and h // 2 < POOLG:
                    copy_out(("pool", h // 2), pooled[:, h // 2 % 2, :], width=TOK)
                if h % 2 == 1 and h // 2 < POOLG:
                    g = h // 2
                    name = ("mix", g)
                    wait_filled(act, name)
                    hand_over(act.activation(oT[:, 4 + g, :], bank(name)[:, 0:TOK], ACT.Copy, scale=colB[:, 104 + g:105 + g]), name)
                if 1 <= h <= HEADS:
                    copy_out(("pt", h - 1), pT[:, (h - 1) % 4, :], width=3 * P)
                if h >= 2 and h % 2 == 1:
                    pair = (h - 2) // 2
                    copy_out(("pv", pair), oT[:, pair, :], width=TOK)
            for j in range(4):
                split_pair(oT, j, ("pv", 2 * j + 1) if j < 2 else ("mix", 2 * j - 3))
            split_until(ahead("eout", 1))
            y_square_sums(0)

            square_sums(1)
            modulate(1)
            for b in range(NB + 1):
                if b < NB:
                    split_until(ahead("fg", b))
                    for t in range(NT):
                        wait_filled(act, ("fg", b, t))
                        ins = act.activation(sil[:, t, :], bank(("fg", b, t))[:, :], ACT.Silu)
                        hand_over(ins, ("fg", b, t))
                else:
                    split_until(ahead("fd", NB - 2))
                if b:
                    for t in range(NT):
                        name = ("ft", b - 1, t)
                        if b < NB and t == 1:
                            split_until(midway_ahead("fg", b))
                        wait_filled(act, name)
                        if b > 1 and t == 0:
                            act.wait_ge(half_used, HALF_END[HALF_AT[("fd", b - 2, 1)] + 1][1])
                        act.activation(actTh[:, t, :, :].rearrange("p f n -> p (f n)"), bank(name)[:, :], ACT.Copy).then_inc(act_hi, 1)
            split_until(ahead("fd", NB - 1))
            y_square_sums(1)

            square_sums(2)
            modulate(2)
            def split_output(group):
                for j in (2 * group, 2 * group + 1):
                    wait_filled(act, ("ot", j))
                    act.activation(LH[:, 2 * j:2 * j + 2, :].rearrange("p c t -> p (c t)"), bank(("ot", j))[:, :], ACT.Copy).then_inc(lhs_hi, 1)

            def gate_functions():
                act.wait_ge(ba_dve, 4)
                tell(act.activation(bt[0], bt[0], ACT.Exp), ba_act)
                act.wait_ge(odd_in, 80)
                tell(act.activation(bt[3][:, 0:8], alog[:, :], ACT.Exp), ba_act)
                tell(act.activation(bt[1], bt[1], ACT.Exp), ba_act)
                tell(act.activation(bt[1], bt[1], ACT.Ln, bias=1.0), ba_act)

            for g in range(ODD_GROUPS):
                def natural(r):
                    split_until(ahead("oin", 2 * r + g))
                    for t in range(NT):
                        name = ("oin", g, r, t)
                        wait_filled(act, name)
                        if r:
                            wait_filled(act, ("rt", g, r - 1, 1))
                        hand_over(act.activation(nat[:, t, :], bank(name)[:, :], ACT.Copy), name)

                def take_turned(r):
                    split_until(min(midway_ahead("oin", 2 * r + g), NHALF))
                    for j in range(2):
                        name = ("rt", g, r, j)
                        wait_filled(act, name)
                        if r == 2 and j == 0:
                            act.wait_ge(conv_ready, 3 * g + 1)
                        hand_over(act.activation(raw[r % 2][:, 2 * j:2 * j + 2, 3:3 + TOK], bank(name)[:, :].rearrange("p (h t) -> p h t", h=2), ACT.Copy), name)

                def activate(r):
                    act.wait_ge(conv_ready, 3 * g + r + 1)
                    tell(act.activation(qkvT[:, r].rearrange("p h t -> p (h t)"), conv[r % 2][:, :, :].rearrange("p h t -> p (h t)"), ACT.Silu), silu_ready)

                for r in range(3):
                    natural(r)
                    if g == 0 and r == 0:
                        gate_functions()
                    if g == 0 and r == 2:
                        name = ("gc",)
                        wait_filled(act, name)
                        hand_over(act.activation(eg, bank(name)[:, 0:24], ACT.Exp), name)
                    take_turned(r)
                    if r:
                        activate(r - 1)
                split_until(ahead("oin", 6 + g))
                for r in range(2):
                    copy_out(("ss", g, r), ssqk[:, r, :], width=8)
                activate(2)
                for t in range(NT):
                    copy_out(("gate", g, t), sgate[:, t, g * N:(g + 1) * N], func=ACT.Silu)
                for c in range(2):
                    wait_emptied(act, ("decay", g, c))
                    e = ET[:, c].rearrange("p h n -> p (h n)")
                    tell(act.activation(e, e, ACT.Exp), et_act)
                for c in range(2):
                    copy_out(("x0", g, c), X[:, c].rearrange("p h n -> p (h n)"))
                for s in range(1, 7):
                    for c in range(2):
                        copy_out(("Y", g, s, c), Y[:, c].rearrange("p h n -> p (h n)"))
                    if g == 1 and s == 5:
                        split_output(0)
                copy_out(("u0", g), u0.rearrange("p h n -> p (h n)"))
                copy_out(("S1", g), S1.rearrange("p h n -> p (h n)"))
                copy_out(("v1", g), v1.rearrange("p h n -> p (h n)"))
                copy_out(("o0", g), xn[:, 0, g * N:(g + 1) * N])
            split_output(1)
            split_until(NHALF)
            y_square_sums(2)

            square_sums(3)
            modulate(3)

            def begin(it):
                split_at[0] = 0
                split_until(PARTS - 1, it)

            begin(0)
            act.wait_ge(route_arg, 1)
            tell(act.activation(pexp[:, 1, :], pexp[:, 0, :], ACT.Exp), route_exp)

            def take_gathered(j, it=None):
                name = ("mh", j)
                if j == 0:
                    wait_filled(act, name, it)
                    for cc in range(4):
                        ins = act.activation(heT[:, cc, :], bank(name, it)[:, cc * P:(cc + 1) * P], ACT.Identity,
                                             bias=shift[:, 3, cc:cc + 1], scale=gain[:, 3, cc:cc + 1])
                    signal_emptied(ins, name, it)
                wait_emptied(act, name, it)
                act.activation(LH[:, 4 * j:4 * j + 4, 0:P], heT[:, 4 * j:4 * j + 4, :], ACT.Copy).then_inc(lhs_hi, 1)

            def expert(it, begun, following):
                if not begun:
                    begin(it)
                split_at[0] = PARTS - 1
                for b in range(NB + 1):
                    if b < NB:
                        split_until(ahead("mg", b, it), it)
                        wait_filled(act, ("mg", b, 0), it)
                        if b:
                            wait_emptied(act, ("mu", b - 1, 0), it)
                        hand_over(act.activation(msil[:, 0, :], bank(("mg", b, 0), it)[:, :], ACT.Silu), ("mg", b, 0), it)
                    else:
                        split_until(ahead("md", NB - 2, it), it)
                    if b:
                        name = ("mt", b - 1, 0)
                        wait_filled(act, name, it)
                        if b > 1:
                            act.wait_ge(half_used, it * MOE_HALVES_COUNTED + (HALVES_COUNTED + MOE_HALF_END[MOE_HALF_AT[("md", b - 2, 1)] + 1][1]))
                        act.activation(actTh[:, 0, :, :].rearrange("p f n -> p (f n)"), bank(name, it)[:, :], ACT.Copy).then_inc(act_hi, 1)
                    if b == 1:
                        copy_out(("mp",), placeT[:, :, :].rearrange("p t n -> p (t n)"), it, width=TOK)
                split_until(NMOE_HALF, it)
                take_gathered(0, it)
                if following:
                    begin(it + 1)
                copy_out(("my", 0), ye[:, 0:N], it)
                take_gathered(1, it)

            for j in range(2):
                take_gathered(j)
            act.wait_ge(table_ready, 1)
            n_extra = act.value_load(tabi[0:1, 0:1], min_val=0, max_val=EXTRA_MAX)
            with act.Fori(0, NE - 1) as i:
                expert(i, True, True)
            expert(NE - 1, True, False)
            with act.If(n_extra > 0):
                with act.Fori(0, n_extra) as i:
                    expert(i + NE, False, False)
            for t in range(NT):
                act.wait_ge(mo_ready, t + 1)
                tell(act.activation(hT[:, 4 * t:4 * t + 4, :].rearrange("p c t -> p (c t)"), yout[:, t, :], ACT.Square, accum_out=ssy[:, 3, t, 0:1]), ssy_ready)

        @block.gpsimd
        def _(pool):
            steps = [0]
            told = {}

            def tell(ins, signal):
                told[id(signal)] = told.get(id(signal), 0) + 1
                ins.then_inc(signal, 1)
                pool.wait_ge(signal, told[id(signal)])

            def hand_over(ins, name, it=None):
                signal_emptied(ins, name, it)
                wait_emptied(pool, name, it)

            def link(ins):
                steps[0] += 1
                ins.then_inc(pool_step, 1)
                pool.wait_ge(pool_step, steps[0])

            link(pool.memset(half_neg[:, :], -0.5))

            def x_rstd(w):
                pool.wait_ge(ss_ready, NT * (w + 1))
                link(pool.tensor_scalar(rstd[:, w, :], ss[:, w, :], 1.0 / D, EPS, ALU.mult, ALU.add))
                tell(pool.tensor_tensor(rstd[:, w, :], rstd[:, w, :], half_neg[:, 0:NT], ALU.pow), rstd_ready)

            def y_rstd(w):
                pool.wait_ge(ssy_ready, 4 * w + (2 if w == 3 else 4))
                if w < 3:
                    link(pool.tensor_tensor(rstdy[:, w, :], ssy[:, w, :, 0], ssy[:, w, :, 1], ALU.add))
                    link(pool.tensor_scalar(rstdy[:, w, :], rstdy[:, w, :], 1.0 / D, EPS, ALU.mult, ALU.add))
                else:
                    link(pool.tensor_scalar(rstdy[:, w, :], ssy[:, w, :, 0], 1.0 / D, EPS, ALU.mult, ALU.add))
                tell(pool.tensor_tensor(rstdy[:, w, :], rstdy[:, w, :], half_neg[:, 0:NT], ALU.pow), rstdy_ready)

            def head_rstd(g, t):
                pool.wait_ge(fo_arg, NT * g + t + 1)
                f = fo[:, t, 4 * g:4 * g + 4]
                tell(pool.tensor_tensor(f, f, half_neg[:, 0:4], ALU.pow), fo_ready)

            def scale_gates(g):
                for t in range(NT):
                    wait_emptied(pool, ("gate", g, t))
                    s3 = sgate[:, t, g * N:(g + 1) * N].rearrange("p (h n) -> p h n", n=DH)
                    tell(pool.tensor_tensor(s3, s3, row3(normg[:, :], 4), ALU.mult), gate_scaled)

            def load_gate_rows(w):
                if w:
                    pool.wait_ge(gate_row_ready, 2 * w)
                pool.dma_start(grow[:, :], I["mix_post_g" if w % 2 == 0 else "ffn_post_g"][w // 2].partition_broadcast(P)).then_inc(grow_in, 16)
                if w == 1:
                    wait_filled(pool, ("mix", POOLG - 1))
                if w >= A_RING:
                    pool.wait_ge(x_ready, NT * (w - A_RING + 1))
                part = 2 if w % 2 == 0 else 5
                pool.dma_start(A[:, w % A_RING, :], I["ada_b"][w // 2, part * D:(part + 1) * D].partition_broadcast(P)).then_inc(abias_in, 16)

            load_gate_rows(0)
            x_rstd(0)
            load_gate_rows(1)
            y_rstd(0)
            x_rstd(1)
            load_gate_rows(2)
            load_gate_rows(3)
            y_rstd(1)
            x_rstd(2)
            pool.wait_ge(late_const_in, 16)
            for g in range(ODD_GROUPS):
                def first_tap(r):
                    for j in range(2):
                        wait_emptied(pool, ("rt", g, r, j))
                    if r == 2:
                        pool.wait_ge(silu_ready, 3 * g + 1)
                    for h in range(4):
                        col = 8 + 8 * r + 4 * g + h
                        ins = pool.tensor_scalar(conv[r % 2][:, h, :], raw[r % 2][:, h, 0:TOK], colB[:, col:col + 1], None, ALU.mult)
                    tell(ins, tap_ready)

                def squares(r):
                    pool.wait_ge(silu_ready, 3 * g + r + 1)
                    if r:
                        wait_filled(pool, ("ss", g, r - 1))
                    tell(pool.tensor_tensor(sq[:, :, :], qkvT[:, r], qkvT[:, r], ALU.mult), sq_ready)

                pool.wait_ge(pad_ready, g + 1)
                first_tap(0)
                first_tap(1)
                squares(0)
                first_tap(2)
                squares(1)
                for r in range(2):
                    wait_emptied(pool, ("ss", g, r))
                    link(pool.tensor_scalar(ssqk[:, r, :], ssqk[:, r, :], EPS, None, ALU.add))
                    tell(pool.tensor_tensor(rqk[:, r, :], ssqk[:, r, :], half_neg[:, 0:8], ALU.pow), rqk_ready)
                for s in range(1, 7):
                    for c in range(2):
                        if s == 1:
                            wait_emptied(pool, ("kk", g, c))
                        else:
                            wait_filled(pool, ("Y", g, s - 1, c))
                        tell(pool.tensor_tensor(CT[:, c], LT[:, c], row3(const("level", s * P, P), 4), ALU.mult), ct_ready)
                    if s == 1:
                        scale_gates(g)
                    if g == 1 and s in (2, 3):
                        head_rstd(0, s - 2)
            for t in range(NT):
                head_rstd(1, t)
            y_rstd(2)
            x_rstd(3)
            y_rstd(3)

        @block.vector
        def _(dve):
            steps = [0]
            told = {}

            def tell(ins, signal):
                told[id(signal)] = told.get(id(signal), 0) + 1
                ins.then_inc(signal, 1)
                dve.wait_ge(signal, told[id(signal)])

            def hand_over(ins, name, it=None):
                signal_emptied(ins, name, it)
                wait_emptied(dve, name, it)

            def link(ins):
                steps[0] += 1
                ins.then_inc(dve_step, 1)
                dve.wait_ge(dve_step, steps[0])

            tt, ts, stt = dve.tensor_tensor, dve.tensor_scalar, dve.scalar_tensor_tensor

            def copy_out(name, out, it=None, width=N):
                wait_filled(dve, name, it)
                hand_over(dve.tensor_copy(out, bank(name, it)[:, 0:width]), name, it)

            def ada_sum(j):
                if j >= ACC_RING:
                    wait_filled(dve, ("ada", j - ACC_RING))
                a = acc[:, j % ACC_RING, :]
                for k in range(KD):
                    n = AT[("ada", j, k // 4)]
                    if k % 4 == 0:
                        wait_tile(dve, n)
                    w = wide(slot(n))[:, k % 4, :]
                    if k == 0:
                        ins = ts(a, w, csil[:, 0:1], None, ALU.mult)
                    else:
                        dve.wait_ge(ada_step, 8 * j + k)
                        ins = stt(out=a, in0=w, scalar=csil[:, k:k + 1], in1=a, op0=ALU.mult, op1=ALU.add)
                    ins.then_inc(ada_step, 1)

            def ada_take(j):
                layer, n = ADA[j]
                part, name = n // 2, ("ada", j)
                w = 2 * layer + (part >= 3)
                wait_filled(dve, name)
                if part in (2, 5):
                    dve.wait_ge(abias_in, 16 * (w + 1))
                    dve.wait_ge(grow_in, 16 * (w + 1))
                    a = A[:, w % A_RING, (n % 2) * N:(n % 2 + 1) * N]
                    hand_over(tt(a, a, bank(name)[:, :], ALU.add), name)
                    tell(tt(a, a, grow[:, (n % 2) * N:(n % 2 + 1) * N], ALU.mult), gate_row_ready)
                    return
                bias = colA[:, 48 * layer + 4 * n:48 * layer + 4 * n + 4]
                lo = 4 * (n % 2)
                if part in (0, 3):
                    hand_over(tt(shift[:, w, lo:lo + 4], bank(name)[:, 0:4], bias, ALU.add), name)
                else:
                    hand_over(tt(mod_tmp[:, :], bank(name)[:, 0:4], bias, ALU.add), name)
                    g = (96 if part == 1 else 112) + 8 * layer + lo
                    link(stt(out=gain[:, w, lo:lo + 4], in0=mod_tmp[:, :], scalar=1.0, in1=colA[:, g:g + 4], op0=ALU.add, op1=ALU.mult))

            stream_at, split_at, taken = [0], [0], [0]

            def take_until(j):
                for i in range(taken[0], j):
                    ada_take(i)
                taken[0] = max(taken[0], j)

            def split_half(g, it=None):
                w, n = half_of_tile(g, it)
                s = g % PARTS
                dve.wait_ge(hi_ready, g + 1 if it is None else it * NMOE_HALF + (NHALF + g + 1))
                wait_tile(dve, n, it)
                tt(wl[:, s, :], w, wh[:, s, :].bitcast(F32), ALU.subtract).then_inc(lo_ready, 1)

            def advance(end):
                while split_at[0] < end or (end == NHALF and stream_at[0] < NSTREAM):
                    kind, b, h = STREAM[stream_at[0]]
                    if kind == "ada":
                        take_until(b - 1)
                        ada_sum(b)
                        stream_at[0] += 2
                    else:
                        g = split_at[0]
                        split_half(g)
                        split_at[0] += 1
                        stream_at[0] += g % 2

            def split_pair(src, j, use):
                dve.wait_ge(lhs_hi, lhs_count(use, j + 1))
                out, value, hi = (a[:, 2 * j:2 * j + 2, :] for a in (LL, src, LH))
                tt(out, value, hi.bitcast(F32), ALU.subtract).then_inc(lhs_lo, 1)

            def norm_x(w):
                dve.wait_ge(rstd_ready, w + 1)
                for t in range(NT):
                    tell(ts(xn[:, t, :], x[:, t, :], rstd[:, w, t:t + 1], None, ALU.mult), xn_ready)

            def modulate(w):
                for j in range(4):
                    name = ("ht", w, j)
                    if j % 2:
                        wait_filled(dve, name)
                        for cc in range(2):
                            c = 2 * j + cc
                            ins = ts(hT[:, c, :], bank(name)[:, cc * TOK:(cc + 1) * TOK], gain[:, w, c:c + 1], shift[:, w, c:c + 1], ALU.mult, ALU.add)
                        hand_over(ins, name)
                        if w < 3:
                            split_pair(hT, j - 1, ("h", w))
                            split_pair(hT, j, ("h", w))

            def add_y(w):
                for t in range(NT):
                    for n in range(2):
                        cols = slice(n * N, (n + 1) * N)
                        if w < 3:
                            name = ("y", w, t, n)
                            wait_filled(dve, name)
                            dve.wait_ge(ssy_ready, 4 * w + 2 * t + n + 1)
                            hand_over(tt(xn[:, t, cols], bank(name)[:, :], A[:, w % A_RING, cols], ALU.mult), name)
                        else:
                            link(tt(xn[:, t, cols], yout[:, t, cols], A[:, w % A_RING, cols], ALU.mult))
                dve.wait_ge(rstdy_ready, w + 1)
                for t in range(NT):
                    tell(stt(out=x[:, t, :], in0=xn[:, t, :], scalar=rstdy[:, w, t:t + 1], in1=x[:, t, :], op0=ALU.mult, op1=ALU.add), x_ready)

            copy_out(("cols", 0), colA[:, :], width=P)
            dve.wait_ge(csil_ready, 1)
            wait_emptied(dve, ("cols", 0))
            for j in range(4):
                take_until(j - 1)
                ada_sum(j)
            stream_at[0] = 8
            take_until(3)
            norm_x(0)
            take_until(4)
            modulate(0)

            advance(ahead("ein", 0))
            dve.wait_ge(pos_in, 16)
            dve.wait_ge(late_const_in, 16)
            link(dve.tensor_copy(posf[:, :], posi[:, :]))
            ang, ang2 = rope_in[:, 0, :], rope_in[:, 1, :]
            for t in range(NT):
                for half in range(2):
                    at = half * NT * ROT + t * ROT
                    link(ts(ang[:, at:at + ROT], const("freq"), posf[:, t:t + 1], None, ALU.mult))
            link(stt(out=rope_n, in0=ang, scalar=0.15915494309189535, in1=const("phase"), op0=ALU.mult, op1=ALU.add))
            link(ts(rope_n, rope_n, MAGIC, None, ALU.add))
            link(ts(rope_n, rope_n, -MAGIC, None, ALU.add))
            link(stt(out=ang2, in0=rope_n, scalar=-TWO_PI_HI, in1=ang, op0=ALU.mult, op1=ALU.add))
            link(stt(out=ang2, in0=rope_n, scalar=-TWO_PI_LO, in1=ang2, op0=ALU.mult, op1=ALU.add))
            link(stt(out=ang2, in0=const("phase"), scalar=6.283185307179586, in1=ang2, op0=ALU.mult, op1=ALU.add))
            tell(ts(rope_r, ang2, 3.1415925, -3.1415925, ALU.min, ALU.max), trig_arg)
            advance(ahead("ein", 1))
            for n in range(2):
                for t in range(NT):
                    wait_emptied(dve, ("ein", n, t))
            dve.wait_ge(trig_ready, 1)

            def rope(t):
                qk = proj[:, t, 0:2 * N].rearrange("p (h d) -> p h d", d=HD)
                x1, x2 = qk[:, :, 0:ROT], qk[:, :, ROT:2 * ROT]
                sin = row3(cs[:, t * ROT:(t + 1) * ROT], 16)
                cos = row3(cs[:, (NT + t) * ROT:(NT + t + 1) * ROT], 16)
                tt(rope_t[:, 0], x1, cos, ALU.mult)
                tt(rope_t[:, 1], x2, sin, ALU.mult)
                tt(rope_t[:, 2], x2, cos, ALU.mult)
                link(tt(rope_t[:, 3], x1, sin, ALU.mult))
                link(tt(x1, rope_t[:, 0], rope_t[:, 1], ALU.subtract))
                tell(tt(x2, rope_t[:, 2], rope_t[:, 3], ALU.add), roped)

            for t in range(NT):
                rope(t)
            advance(ahead("ein", 3))
            take_until(7)
            for h in range(HEADS + 1):
                if h < HEADS:
                    name = ("score", h)
                    wait_filled(dve, name)
                    s = sL[:, h % 2, :]
                    ins = stt(out=s, in0=bank(name)[:, 0:3 * P], scalar=HD ** -0.5, in1=const("mask"), op0=ALU.mult, op1=ALU.add)
                    hand_over(ins, name)
                    link(dve.tensor_reduce(nmax[:, h, 0:1], s[:, 0:P], AX.X, ALU.max, negate=True))
                    tell(dve.tensor_reduce(nmax[:, h, 1:2], s[:, P:3 * P], AX.X, ALU.max, negate=True), maxed)
                if h:
                    g = h - 1
                    dve.wait_ge(exped, 2 * h)
                    link(dve.reciprocal(rden[:, g, :], den[:, g, :]))
                    link(ts(prob[:, g % 2, 0:P], prob[:, g % 2, 0:P], rden[:, g, 0:1], None, ALU.mult))
                    tell(ts(prob[:, g % 2, P:3 * P], prob[:, g % 2, P:3 * P], rden[:, g, 1:2], None, ALU.mult), normed)
            for j in range(4):
                split_pair(oT, j, ("o", 0))
            advance(ahead("eout", 1))
            take_until(9)
            add_y(0)
            take_until(10)

            norm_x(1)
            modulate(1)

            def split_inner(b, t):
                name = ("ft", b, t)
                dve.wait_ge(act_hi, NT * b + t + 1)
                wait_filled(dve, name)
                ins = tt(actTl[:, t, :, :].rearrange("p f n -> p (f n)"), bank(name)[:, :], actTh[:, t, :, :].rearrange("p f n -> p (f n)").bitcast(F32), ALU.subtract)
                signal_emptied(ins, name)

            for b in range(NB):
                advance(ahead("fg", b))
                if b:
                    split_inner(b - 1, 0)
                    advance(midway_ahead("fg", b))
                    split_inner(b - 1, 1)
                advance(ahead("fu", b))
                for t in range(NT):
                    name = ("fu", b, t)
                    wait_emptied(dve, ("fg", b, t))
                    wait_filled(dve, name)
                    ins = tt(act_n[:, t, :], sil[:, t, :], bank(name)[:, :], ALU.mult)
                    hand_over(ins, name)
            advance(ahead("fd", NB - 2))
            take_until(23)
            for t in range(NT):
                split_inner(NB - 1, t)
            take_until(24)
            advance(ahead("fd", NB - 1))
            add_y(1)

            norm_x(2)
            modulate(2)
            advance(ahead("oin", 0))
            dve.wait_ge(odd_in, 80)
            name = ("ba",)
            wait_filled(dve, name)
            hand_over(dve.tensor_copy(ba.rearrange("p t n -> p (t n)"), bank(name)[:, 0:32]), name)

            def gate_step(ins):
                gate_n[0] += 1
                ins.then_inc(ba_dve, 1)
                dve.wait_ge(ba_dve, gate_n[0])

            gate_n = [0]
            z = bt[2].rearrange("p (t h) -> p t h", t=NT)
            gate_step(ts(bt[0].rearrange("p (t h) -> p t h", t=NT), ba[:, :, 0:8], -1.0, None, ALU.mult))
            gate_step(tt(z, ba[:, :, 8:16], row3(dtb[:, :], NT), ALU.add))
            gate_step(stt(out=bt[1], in0=bt[2], scalar=-1.0, in1=bt[2], op0=ALU.mult, op1=ALU.min))
            gate_step(ts(bt[2], bt[2], 0.0, None, ALU.max))
            dve.wait_ge(ba_act, 1)
            gate_step(ts(bt[0], bt[0], 1.0, None, ALU.add))
            gate_step(dve.reciprocal(beta, bt[0]))
            dve.wait_ge(ba_act, 4)
            gate_step(tt(gdec, bt[1], bt[2], ALU.add))
            g3 = gdec.rearrange("p (t h) -> p t h", t=NT)
            gate_step(tt(g3, g3, row3(bt[3][:, 0:8], NT), ALU.mult))
            gate_step(ts(gdec, gdec, -1.0, None, ALU.mult))

            def head_squares(g, t):
                wait_emptied(dve, ("o0", g))
                cols, heads = slice(g * N, (g + 1) * N), slice(4 * g, 4 * g + 4)
                link(tt(o2, xn[:, t, cols], xn[:, t, cols], ALU.mult))
                link(dve.tensor_reduce(sso[:, t, heads], o2.rearrange("p (h n) -> p h n", n=DH), AX.X, ALU.add))
                link(tt(f1[:, t, heads], rsq[:, t, heads], rsq[:, t, heads], ALU.mult))
                link(tt(f1[:, t, heads], f1[:, t, heads], sso[:, t, heads], ALU.mult))
                tell(ts(fo[:, t, heads], f1[:, t, heads], 1.0 / DH, EPS, ALU.mult, ALU.add), fo_arg)

            def head_norm(g, t):
                cols, heads = slice(g * N, (g + 1) * N), slice(4 * g, 4 * g + 4)
                dve.wait_ge(fo_ready, NT * g + t + 1)
                link(tt(fo[:, t, heads], fo[:, t, heads], rsq[:, t, heads], ALU.mult))
                o3 = xn[:, t, cols].rearrange("p (h n) -> p h n", n=DH)
                link(tt(o3, o3, col3(fo[:, t, heads], DH), ALU.mult))
                dve.wait_ge(gate_scaled, NT * g + t + 1)
                tell(tt(xn[:, t, cols], xn[:, t, cols], sgate[:, t, cols], ALU.mult), o_ready)

            def finish_output(g):
                for t in range(NT):
                    head_squares(g, t)
                for t in range(NT):
                    head_norm(g, t)

            def split_output(group):
                for j in (2 * group, 2 * group + 1):
                    name = ("ot", j)
                    dve.wait_ge(lhs_hi, lhs_count(("o", 2), j + 1))
                    wait_filled(dve, name)
                    out, hi = (a[:, 2 * j:2 * j + 2, :].rearrange("p c t -> p (c t)") for a in (LL, LH))
                    tt(out, bank(name)[:, :], hi.bitcast(F32), ALU.subtract).then_inc(lhs_lo, 1)
                    dve.wait_ge(lhs_lo, lhs_count(("o", 2), j + 1))
                    signal_emptied(dve.nop(), name)

            for g in range(ODD_GROUPS):
                heads = slice(4 * g, 4 * g + 4)
                if g:
                    wait_filled(dve, ("o1", g - 1))
                link(dve.memset(raw[0][:, :, 0:3], 0.0))
                tell(dve.memset(raw[1][:, :, 0:3], 0.0), pad_ready)
                for r in range(3):
                    advance(ahead("oin", 2 * (r + 1) + g))
                    dve.wait_ge(tap_ready, 3 * g + r + 1)
                    for w in range(1, CONVW):
                        for h in range(4):
                            col = colB[:, 8 + 24 * w + 8 * r + 4 * g + h:9 + 24 * w + 8 * r + 4 * g + h]
                            src, out = raw[r % 2][:, h, w:w + TOK], conv[r % 2][:, h, :]
                            ins = stt(out=out, in0=src, scalar=col, in1=out, op0=ALU.mult, op1=ALU.add)
                        if w == CONVW - 1:
                            tell(ins, conv_ready)
                        else:
                            link(ins)
                if g == 0:
                    wait_emptied(dve, ("gc",))
                dve.wait_ge(silu_ready, 3 * g + 3)
                for c in range(2):
                    gd = gdec[:, 8 * c + 4 * g:8 * c + 4 * g + 4]
                    tell(tt(Y[:, c], row3(const("upto"), 4), col3(gd, P), ALU.mult), rhs_ready)
                dve.wait_ge(rqk_ready, 2 * g + 2)
                rk = rqk[:, 1, :]
                for c in range(2):
                    link(tt(bk[:, 4 * c:4 * c + 4], rk[:, 4 * c:4 * c + 4], beta[:, 8 * c + 4 * g:8 * c + 4 * g + 4], ALU.mult))
                    link(ts(rsq[:, c, heads], rqk[:, 0, 4 * c:4 * c + 4], DH ** -0.5, None, ALU.mult))
                for c in range(2):
                    tell(tt(CT[:, c], row3(ident, 4), col3(bk[:, 4 * c:4 * c + 4], P), ALU.mult), rhs_ready)
                link(tt(kge, rk[:, 0:4], eg[:, 16 + 4 * g:20 + 4 * g], ALU.mult))
                link(tt(nbe, bk[:, 4:8], eg[:, 8 + 4 * g:12 + 4 * g], ALU.mult))
                for c in range(2):
                    name = ("decay", g, c)
                    wait_filled(dve, name)
                    ins = tt(ET[:, c], bank(name)[:, :].rearrange("p (h n) -> p h n", h=4), row3(const("neg"), 4), ALU.add)
                    hand_over(ins, name)
                for c in range(2):
                    name = ("brow", g, c)
                    wait_filled(dve, name)
                    dve.wait_ge(et_act, 2 * g + c + 1)
                    ins = tt(LT[:, c], ET[:, c], bank(name)[:, :].rearrange("p (h n) -> p h n", h=4), ALU.mult)
                    hand_over(ins, name)
                for c in range(2):
                    name = ("kk", g, c)
                    wait_filled(dve, name)
                    for h in range(4):
                        ins = stt(out=LT[:, c, h, :], in0=bank(name)[:, h * P:(h + 1) * P], scalar=rk[:, 4 * c + h:4 * c + h + 1], in1=LT[:, c, h, :],
                                  op0=ALU.mult, op1=ALU.mult)
                    hand_over(ins, name)
                    link(tt(U[:, c], LT[:, c], row3(const("level", 0, P), 4), ALU.mult))
                    tell(tt(U[:, c], row3(ident, 4), U[:, c], ALU.subtract), u_ready)
                for c in range(2):
                    name = ("kq", g, c)
                    wait_filled(dve, name)
                    for h in range(4):
                        ins = stt(out=attnT[:, c, h, :], in0=bank(name)[:, h * P:(h + 1) * P], scalar=rk[:, 4 * c + h:4 * c + h + 1], in1=ET[:, c, h, :],
                                  op0=ALU.mult, op1=ALU.mult)
                    hand_over(ins, name)
                for c in range(2):
                    name = ("vn", g, c)
                    wait_filled(dve, name)
                    ins = tt(vb[:, c], bank(name)[:, :].rearrange("p (h n) -> p h n", h=4), col3(beta[:, 8 * c + 4 * g:8 * c + 4 * g + 4], P), ALU.mult)
                    hand_over(ins, name)
                name = ("kn", g)
                wait_filled(dve, name)
                hand_over(tt(kg0, bank(name)[:, :].rearrange("p (h n) -> p h n", h=4), col3(kge, P), ALU.mult), name)
                for s in range(1, 7):
                    for c in range(2):
                        for what, M in (("dX", X), ("dU", U)):
                            if what == "dX" and s == 6:
                                continue
                            name = (what, g, s, c)
                            wait_filled(dve, name)
                            if s > 1:
                                wait_emptied(dve, (what, g, s - 1, c))
                            elif what == "dX":
                                wait_emptied(dve, ("x0", g, c))
                            else:
                                dve.wait_ge(u_ready, 2 * g + c + 1)
                            m = M[:, c].rearrange("p h n -> p (h n)")
                            hand_over(tt(m, m, bank(name)[:, :], ALU.subtract), name)
                    if g == 1 and s in (1, 2):
                        head_squares(0, s - 1)
                    if g == 1 and s in (3, 4):
                        head_norm(0, s - 3)
                    if g == 1 and s == 5:
                        split_output(0)
                name = ("kS", g)
                wait_filled(dve, name)
                hand_over(tt(r1, bank(name)[:, :].rearrange("p (h n) -> p h n", h=4), col3(nbe, P), ALU.mult), name)
                wait_emptied(dve, ("vn", g, 1))
                tell(tt(r1, vb[:, 1], r1, ALU.subtract), r_ready)
                name = ("qS", g)
                wait_filled(dve, name)
                hand_over(tt(qs, bank(name)[:, :].rearrange("p (h n) -> p h n", h=4), col3(eg[:, 8 + 4 * g:12 + 4 * g], P), ALU.mult), name)
                name = ("o1", g)
                wait_filled(dve, name)
                hand_over(tt(xn[:, 1, g * N:(g + 1) * N], qs.rearrange("p h n -> p (h n)"), bank(name)[:, :], ALU.add), name)
            finish_output(1)
            split_output(1)
            advance(NHALF)
            link(dve.memset(yout[:, :, :].rearrange("p t d -> p (t d)"), 0.0))
            add_y(2)

            norm_x(3)
            modulate(3)

            def split_until(end, it):
                for g in range(split_at[0], end):
                    split_half(g, it)
                split_at[0] = end

            def begin(it):
                split_at[0] = 0
                split_until(PARTS - 1, it)

            begin(0)
            name = ("route",)
            wait_filled(dve, name)
            hand_over(dve.tensor_copy(logit.rearrange("p t e -> p (t e)"), bank(name)[:, 0:16]), name)
            for t in range(NT):
                link(dve.max(best[:, t, :], logit[:, t, :]))
                link(dve.max_index(besti[:, t, :], best[:, t, :], logit[:, t, :]))
            link(dve.tensor_copy(bestf, besti[:, :, :]))
            tell(tt(pexp[:, 0, :], best[:, :, 1], best[:, :, 0], ALU.subtract), route_arg)
            dve.wait_ge(route_exp, 1)
            link(ts(pexp[:, 2, :], pexp[:, 1, :], 1.0, None, ALU.add))
            link(dve.reciprocal(pexp[:, 3, :], pexp[:, 2, :]))
            link(tt(pexp[:, 4, :], pexp[:, 3, :], pexp[:, 1, :], ALU.mult))
            for t in range(NT):
                first, second = bestf[:, t, 0:1], bestf[:, t, 1:2]
                link(ts(sel[:, t, :], const("iota8"), first, None, ALU.is_equal))
                link(ts(comb[:, t, :], sel[:, t, :], pexp[:, 3, t:t + 1], None, ALU.mult))
                link(ts(rt[:, t, :], const("iota8"), second, None, ALU.is_equal))
                link(stt(out=comb[:, t, :], in0=rt[:, t, :], scalar=pexp[:, 4, t:t + 1], in1=comb[:, t, :], op0=ALU.mult, op1=ALU.add))
                tell(tt(sel[:, t, :], sel[:, t, :], rt[:, t, :], ALU.add), sel_ready)
            name = ("slot",)
            wait_filled(dve, name)
            hand_over(dve.tensor_copy(pos[:, :, :].rearrange("p t e -> p (t e)"), bank(name)[:, 0:24]), name)
            def place_tokens(e, first_slot):
                for t in range(NT):
                    at, on, weight = (a[:, t, bass.ds(e, 1)] for a in (pos, sel, comb))
                    slots = const("iota", first_slot, P)
                    ts(place[:, t, :], slots, at, on, ALU.is_equal, ALU.mult).then_inc(place_ready, 1)
                    ts(placew[:, t, :], slots, at, weight, ALU.is_equal, ALU.mult).then_inc(place_ready, 1)

            def take_gathered(j, it=None):
                name = ("mh", j)
                if j == 1:
                    wait_filled(dve, name, it)
                    for cc in range(4):
                        c = 4 + cc
                        ins = ts(heT[:, c, :], bank(name, it)[:, cc * P:(cc + 1) * P], gain[:, 3, c:c + 1], shift[:, 3, c:c + 1], ALU.mult, ALU.add)
                    hand_over(ins, name, it)
                if it is None:
                    dve.wait_ge(lhs_hi, lhs_count(("o", 2), 4) + j + 1)
                else:
                    dve.wait_ge(lhs_hi, it * 2 + (lhs_count(("o", 2), 4) + 2 + j + 1))
                out, value, hi = LL[:, 4 * j:4 * j + 4, 0:P], heT[:, 4 * j:4 * j + 4, :], LH[:, 4 * j:4 * j + 4, 0:P]
                tt(out, value, hi.bitcast(F32), ALU.subtract).then_inc(lhs_lo, 1)

            def expert(it, begun, following, next_e, next_slot):
                if not begun:
                    begin(it)
                split_at[0] = PARTS - 1

                def split_inner(b):
                    name = ("mt", b, 0)
                    dve.wait_ge(act_hi, it * NB + (NT * NB + b + 1))
                    wait_filled(dve, name, it)
                    ins = tt(actTl[:, 0, :, :].rearrange("p f n -> p (f n)"), bank(name, it)[:, :], actTh[:, 0, :, :].rearrange("p f n -> p (f n)").bitcast(F32), ALU.subtract)
                    signal_emptied(ins, name, it)

                for b in range(NB):
                    if b:
                        split_until(ahead("mg", b, it), it)
                        split_inner(b - 1)
                    split_until(ahead("mu", b, it), it)
                    wait_emptied(dve, ("mg", b, 0), it)
                    wait_filled(dve, ("mu", b, 0), it)
                    ins = tt(mact[:, 0, :], msil[:, 0, :], bank(("mu", b, 0), it)[:, :], ALU.mult)
                    hand_over(ins, ("mu", b, 0), it)
                    if b == 3:
                        wait_filled(dve, ("mp",), it)
                        place_tokens(next_e, next_slot)
                split_until(ahead("md", NB - 2, it), it)
                split_inner(NB - 1)
                split_until(NMOE_HALF, it)
                take_gathered(0, it)
                if following:
                    begin(it + 1)
                copy_out(("my", 1), ye[:, N:D], it)
                take_gathered(1, it)
                for t in range(NT):
                    for n in range(2):
                        name = ("mo", t, n)
                        wait_filled(dve, name, it)
                        y = yout[:, t, n * N:(n + 1) * N]
                        hand_over(tt(y, y, bank(name, it)[:, :], ALU.add), name, it)

            place_tokens(0, 0)
            over, upto = table[:, 0, :], table[:, 1, :]
            link(ts(over, pos[:, 2, :], float(P), None, ALU.is_gt))
            link(dve.tensor_tensor_scan(upto, over, over, 0.0, ALU.add, ALU.max))
            link(dve.tensor_copy(tabf[:, 0:1], upto[:, NE - 1:NE]))
            for j in range(EXTRA_MAX):
                link(ts(match[:, j, :], upto, float(j + 1), None, ALU.is_equal))
                link(tt(match[:, j, :], match[:, j, :], over, ALU.mult))
                link(tt(match[:, j, :], match[:, j, :], const("iota8"), ALU.mult))
                link(dve.tensor_reduce(tabf[:, 1 + j:2 + j], match[:, j, :], AX.X, ALU.add))
            link(dve.memset(tabf[:, 1 + EXTRA_MAX:2 + EXTRA_MAX], 0.0))
            tell(dve.tensor_copy(tabi[:, :], tabf[:, :]), table_ready)
            for j in range(2):
                take_gathered(j)
            n_extra = dve.value_load(tabi[0:1, 0:1], min_val=0, max_val=EXTRA_MAX)
            with dve.Fori(0, NE - 1) as i:
                expert(i, True, True, i + 1, 0)
            first_extra = dve.value_load(tabi[0:1, 1:2], min_val=0, max_val=NE - 1)
            expert(NE - 1, True, False, first_extra, P)
            with dve.If(n_extra > 0):
                with dve.Fori(0, n_extra) as i:
                    after_it = dve.value_load(tabi[0:1, bass.ds(i + 2, 1)], min_val=0, max_val=NE - 1)
                    expert(i + NE, False, False, after_it, P)
            dve.nop().then_inc(mo_ready, 1)
            dve.nop().then_inc(mo_ready, 1)
            add_y(3)


def kernel(**inputs):
    import numpy as np
    import concourse.bacc as bacc
    from concourse.bass_utils import run_bass_kernel_spmd

    nc = bacc.Bacc("TRN2", target_bir_lowering=False, num_devices=1)
    arrays, aps = {}, {}

    def give(name, a):
        arrays[name] = a
        return nc.dram_tensor(name, a.shape, mybir.dt.from_np(a.dtype), kind="ExternalInput").ap()

    for name in IN_NAMES:
        aps[name] = give(f"in_{name}", np.ascontiguousarray(inputs[name]))
    table, pool = constants(np)
    const_dram, pool_dram = give("in_constants", table), give("in_pool_windows", pool)
    out = nc.dram_tensor("out_x", (1, TOK, D), F32, kind="ExternalOutput").ap()
    build_trunk(nc, aps, const_dram, pool_dram, out)
    result = run_bass_kernel_spmd(nc, [arrays], core_ids=[0])
    return result.results[0]["out_x"]
```
